# Optimizing a Trainium2 kernel written in Bass

```python
import math
import jax, jax.numpy as jnp
from jax import lax
import numpy as np

D_MODEL = 1024
BATCH = 1
SEQ = 512
DEPTH = 2
DEC_BATCH = 8
DEC_SEQ = 4
PAST_LEN = 1024
PAGE_SIZE = 128

N_A_LAYERS = DEPTH // 2
N_B_LAYERS = DEPTH - N_A_LAYERS
CONV_WIDTH = 31
N_HEADS = 8
HEAD_DIM = 64
V_DIM = 2 * HEAD_DIM
QK_WIDTH = N_HEADS * 2 * HEAD_DIM
V_WIDTH = N_HEADS * V_DIM
N_GROUPS = 4
EXPERTS_PER_GROUP = 4
N_EXPERTS = N_GROUPS * EXPERTS_PER_GROUP
TOP_K = 2
D_EXPERT = 256
Q_BLOCK = 128
EPS = 1e-6
NEG = -1e30

kernel_name = "yoco_conformer_diffattn_hmoe_step"

def rmsnorm(x, g):
    xf = x.astype(jnp.float32)
    y = xf * lax.rsqrt(jnp.mean(xf * xf, axis=-1, keepdims=True) + EPS)
    return (y * g.astype(jnp.float32)).astype(x.dtype)

def layernorm(x, g, b):
    xf = x.astype(jnp.float32)
    mu = jnp.mean(xf, axis=-1, keepdims=True)
    xc = xf - mu
    y = xc * lax.rsqrt(jnp.mean(xc * xc, axis=-1, keepdims=True) + EPS)
    return (y * g.astype(jnp.float32) + b.astype(jnp.float32)).astype(x.dtype)

def conv_module(xn, past, w_pw1, b_pw1, w_dw, b_dw, ln_g, ln_b, w_pw2, b_pw2):
    u = xn @ w_pw1 + b_pw1
    glu = u[..., :D_MODEL] * jax.nn.sigmoid(u[..., D_MODEL:])
    full = jnp.concatenate([past.astype(glu.dtype), glu], axis=1)
    conv = lax.conv_general_dilated(
        full, w_dw[:, None, :], window_strides=(1,), padding='VALID',
        dimension_numbers=('NWC', 'WIO', 'NWC'), feature_group_count=D_MODEL) + b_dw
    h = jax.nn.silu(layernorm(conv, ln_g, ln_b))
    return h @ w_pw2 + b_pw2, full[:, -(CONV_WIDTH - 1):]

def hier_moe(xn, w_grp, b_grp, w_er, b_er, w_gate, w_up, w_down):
    g_logits = (xn @ w_grp + b_grp).astype(jnp.float32)
    p_grp = jax.nn.softmax(g_logits, axis=-1)
    g_idx = jnp.argmax(g_logits, axis=-1)
    p_g = jnp.take_along_axis(p_grp, g_idx[..., None], axis=-1)
    e_logits = (jnp.einsum('btd,dge->btge', xn, w_er) + b_er).astype(jnp.float32)
    e_logits = jnp.take_along_axis(e_logits, g_idx[..., None, None], axis=-2)[..., 0, :]
    p_e = jax.nn.softmax(e_logits, axis=-1)
    top_p, top_i = lax.top_k(p_e, TOP_K)
    gates = p_g * top_p / jnp.sum(top_p, axis=-1, keepdims=True)
    expert_id = g_idx[..., None] * EXPERTS_PER_GROUP + top_i
    dense_gate = jnp.sum(jax.nn.one_hot(expert_id, N_EXPERTS, dtype=jnp.float32) * gates[..., None], axis=-2)
    h = jax.nn.silu(jnp.einsum('btd,edf->btef', xn, w_gate)) * jnp.einsum('btd,edf->btef', xn, w_up)
    h = h * dense_gate.astype(h.dtype)[..., None]
    return jnp.einsum('btef,efd->btd', h, w_down)

def diff_scores_values(q, qpos, k, v, kpos, slopes, lam):
    s = jnp.einsum('bqhcd,bkhcd->bhcqk', q, k).astype(jnp.float32) * (HEAD_DIM ** -0.5)
    dist = (qpos[:, None] - kpos[None, :]).astype(jnp.float32)
    bias = -slopes[:, None, None] * dist
    s = jnp.where(dist >= 0, s + bias[None, :, None], NEG)
    p = jax.nn.softmax(s, axis=-1)
    a = p[:, :, 0] - lam * p[:, :, 1]
    return jnp.einsum('bhqk,bkhe->bqhe', a.astype(v.dtype), v)

def diff_attention(xn, k, v, qpos, kpos, w_q, lq1, lk1, lq2, lk2, subln_g, w_o, lam_init, slopes):
    b, t, _ = xn.shape
    q = (xn @ w_q).reshape(b, t, N_HEADS, 2, HEAD_DIM)
    lam = (jnp.exp(jnp.sum(lq1.astype(jnp.float32) * lk1.astype(jnp.float32)))
           - jnp.exp(jnp.sum(lq2.astype(jnp.float32) * lk2.astype(jnp.float32))) + lam_init)
    if t % Q_BLOCK == 0:
        nb = t // Q_BLOCK
        qb = jnp.moveaxis(q.reshape(b, nb, Q_BLOCK, N_HEADS, 2, HEAD_DIM), 1, 0)
        pb = qpos.reshape(nb, Q_BLOCK)
        ob = lax.map(lambda a: diff_scores_values(a[0], a[1], k, v, kpos, slopes, lam), (qb, pb))
        o = jnp.moveaxis(ob, 0, 1).reshape(b, t, N_HEADS, V_DIM)
    else:
        o = diff_scores_values(q, qpos, k, v, kpos, slopes, lam)
    o = rmsnorm(o, subln_g) * (1.0 - lam_init)
    return o.reshape(b, t, V_WIDTH) @ w_o

def run_trunk(x, conv_past, k_past, v_past, pos0, p):
    b, t, _ = x.shape
    qpos = pos0 + jnp.arange(t, dtype=jnp.int32)
    slopes = jnp.exp2(-8.0 * jnp.arange(1, N_HEADS + 1, dtype=jnp.float32) / N_HEADS)
    h = x
    new_conv = []
    k_new = v_new = k_all = v_all = kpos = None
    for l in range(DEPTH):
        xn = rmsnorm(h, p['norm_mix'][l])
        if l < N_A_LAYERS:
            out, st = conv_module(xn, conv_past[l], p['conv_w_pw1'][l], p['conv_b_pw1'][l], p['conv_w_dw'][l],
                                  p['conv_b_dw'][l], p['conv_ln_g'][l], p['conv_ln_b'][l],
                                  p['conv_w_pw2'][l], p['conv_b_pw2'][l])
            new_conv.append(st)
        else:
            j = l - N_A_LAYERS
            lam_init = 0.8 - 0.6 * math.exp(-0.3 * l)
            out = diff_attention(xn, k_all, v_all, qpos, kpos, p['attn_w_q'][j], p['attn_lambda_q1'][j],
                                 p['attn_lambda_k1'][j], p['attn_lambda_q2'][j], p['attn_lambda_k2'][j],
                                 p['attn_subln_g'][j], p['attn_w_o'][j], lam_init, slopes)
        h = h + out
        h = h + hier_moe(rmsnorm(h, p['norm_ffn'][l]), p['moe_w_grp'][l], p['moe_b_grp'][l],
                         p['moe_w_exp_router'][l], p['moe_b_exp_router'][l], p['moe_w_gate'][l],
                         p['moe_w_up'][l], p['moe_w_down'][l])
        if l == N_A_LAYERS - 1:
            kv = rmsnorm(h, p['norm_kv']) @ p['w_kv']
            k_new = kv[..., :QK_WIDTH].reshape(b, t, N_HEADS, 2, HEAD_DIM)
            v_new = kv[..., QK_WIDTH:].reshape(b, t, N_HEADS, V_DIM)
            if k_past is None:
                k_all, v_all = k_new, v_new
            else:
                k_all = jnp.concatenate([k_past.astype(k_new.dtype), k_new], axis=1)
                v_all = jnp.concatenate([v_past.astype(v_new.dtype), v_new], axis=1)
            kpos = jnp.arange(k_all.shape[1], dtype=jnp.int32)
    return rmsnorm(h, p['norm_final']), jnp.stack(new_conv), k_new, v_new

def setup_inputs(seed: int = 0) -> dict:
    key = jax.random.key(seed)
    ks = iter(jax.random.split(key, 48))

    def nrm(shape, scale):
        return jax.random.normal(next(ks), shape, jnp.float32) * scale

    n_pages = PAST_LEN // PAGE_SIZE
    n_used = DEC_BATCH * n_pages
    n_pool = n_used + max(1, n_used // 4)
    d = D_MODEL
    inp = {}
    inp['x_prompt'] = nrm((BATCH, SEQ, d), 1.0)
    inp['x_sample'] = nrm((DEC_BATCH, DEC_SEQ, d), 1.0)
    inp['cache_k'] = nrm((n_pool, PAGE_SIZE, N_HEADS, 2, HEAD_DIM), 1.0)
    inp['cache_v'] = nrm((n_pool, PAGE_SIZE, N_HEADS, V_DIM), 1.0)
    inp['state_conv'] = nrm((N_A_LAYERS, DEC_BATCH, CONV_WIDTH - 1, d), 0.5)
    inp['page_table'] = jax.random.permutation(next(ks), n_pool)[:n_used].reshape(DEC_BATCH, n_pages).astype(jnp.int32)
    inp['norm_mix'] = 1.0 + nrm((DEPTH, d), 0.05)
    inp['norm_ffn'] = 1.0 + nrm((DEPTH, d), 0.05)
    inp['norm_kv'] = 1.0 + nrm((d,), 0.05)
    inp['norm_final'] = 1.0 + nrm((d,), 0.05)
    inp['conv_w_pw1'] = nrm((N_A_LAYERS, d, 2 * d), d ** -0.5)
    inp['conv_b_pw1'] = nrm((N_A_LAYERS, 2 * d), 0.02)
    inp['conv_w_dw'] = nrm((N_A_LAYERS, CONV_WIDTH, d), CONV_WIDTH ** -0.5)
    inp['conv_b_dw'] = nrm((N_A_LAYERS, d), 0.02)
    inp['conv_ln_g'] = 1.0 + nrm((N_A_LAYERS, d), 0.05)
    inp['conv_ln_b'] = nrm((N_A_LAYERS, d), 0.02)
    inp['conv_w_pw2'] = nrm((N_A_LAYERS, d, d), d ** -0.5)
    inp['conv_b_pw2'] = nrm((N_A_LAYERS, d), 0.02)
    inp['w_kv'] = nrm((d, QK_WIDTH + V_WIDTH), d ** -0.5)
    inp['attn_w_q'] = nrm((N_B_LAYERS, d, QK_WIDTH), d ** -0.5)
    inp['attn_lambda_q1'] = nrm((N_B_LAYERS, HEAD_DIM), 0.1)
    inp['attn_lambda_k1'] = nrm((N_B_LAYERS, HEAD_DIM), 0.1)
    inp['attn_lambda_q2'] = nrm((N_B_LAYERS, HEAD_DIM), 0.1)
    inp['attn_lambda_k2'] = nrm((N_B_LAYERS, HEAD_DIM), 0.1)
    inp['attn_subln_g'] = 1.0 + nrm((N_B_LAYERS, V_DIM), 0.05)
    inp['attn_w_o'] = nrm((N_B_LAYERS, V_WIDTH, d), V_WIDTH ** -0.5)
    inp['moe_w_grp'] = nrm((DEPTH, d, N_GROUPS), d ** -0.5)
    inp['moe_b_grp'] = nrm((DEPTH, N_GROUPS), 0.01)
    inp['moe_w_exp_router'] = nrm((DEPTH, d, N_GROUPS, EXPERTS_PER_GROUP), d ** -0.5)
    inp['moe_b_exp_router'] = nrm((DEPTH, N_GROUPS, EXPERTS_PER_GROUP), 0.01)
    inp['moe_w_gate'] = nrm((DEPTH, N_EXPERTS, d, D_EXPERT), d ** -0.5)
    inp['moe_w_up'] = nrm((DEPTH, N_EXPERTS, d, D_EXPERT), d ** -0.5)
    inp['moe_w_down'] = nrm((DEPTH, N_EXPERTS, D_EXPERT, d), D_EXPERT ** -0.5)
    return inp

def reference(x_prompt, x_sample, cache_k, cache_v, state_conv, page_table,
              norm_mix, norm_ffn, norm_kv, norm_final,
              conv_w_pw1, conv_b_pw1, conv_w_dw, conv_b_dw, conv_ln_g, conv_ln_b, conv_w_pw2, conv_b_pw2,
              w_kv, attn_w_q, attn_lambda_q1, attn_lambda_k1, attn_lambda_q2, attn_lambda_k2,
              attn_subln_g, attn_w_o,
              moe_w_grp, moe_b_grp, moe_w_exp_router, moe_b_exp_router, moe_w_gate, moe_w_up, moe_w_down):
    p = dict(norm_mix=norm_mix, norm_ffn=norm_ffn, norm_kv=norm_kv, norm_final=norm_final,
             conv_w_pw1=conv_w_pw1, conv_b_pw1=conv_b_pw1, conv_w_dw=conv_w_dw, conv_b_dw=conv_b_dw,
             conv_ln_g=conv_ln_g, conv_ln_b=conv_ln_b, conv_w_pw2=conv_w_pw2, conv_b_pw2=conv_b_pw2,
             w_kv=w_kv, attn_w_q=attn_w_q, attn_lambda_q1=attn_lambda_q1, attn_lambda_k1=attn_lambda_k1,
             attn_lambda_q2=attn_lambda_q2, attn_lambda_k2=attn_lambda_k2, attn_subln_g=attn_subln_g,
             attn_w_o=attn_w_o, moe_w_grp=moe_w_grp, moe_b_grp=moe_b_grp,
             moe_w_exp_router=moe_w_exp_router, moe_b_exp_router=moe_b_exp_router,
             moe_w_gate=moe_w_gate, moe_w_up=moe_w_up, moe_w_down=moe_w_down)
    conv_zero = jnp.zeros((N_A_LAYERS, x_prompt.shape[0], CONV_WIDTH - 1, D_MODEL), x_prompt.dtype)
    y_prompt, conv_prompt, k_prompt, v_prompt = run_trunk(x_prompt, conv_zero, None, None, 0, p)
    db = x_sample.shape[0]
    n_past = page_table.shape[1] * PAGE_SIZE
    k_past = cache_k[page_table].reshape(db, n_past, N_HEADS, 2, HEAD_DIM)
    v_past = cache_v[page_table].reshape(db, n_past, N_HEADS, V_DIM)
    y_sample, conv_sample, k_sample, v_sample = run_trunk(x_sample, state_conv, k_past, v_past, n_past, p)
    return (y_prompt, y_sample, conv_prompt, conv_sample, k_prompt, v_prompt, k_sample, v_sample)


_drawn_inputs = setup_inputs


def setup_inputs(seed=0):
    import zlib

    import numpy as np

    out = dict(_drawn_inputs(seed))
    spreads = {}
    factors = {}
    for name, (base, spread) in spreads.items():
        noise = np.random.default_rng([zlib.crc32(name.encode()), seed]).standard_normal(out[name].shape)
        drawn = base * np.exp(spread * noise) if base else spread * noise
        out[name] = __import__('jax').numpy.asarray(drawn.astype(out[name].dtype))
    for name, factor in factors.items():
        out[name] = (out[name] * factor).astype(out[name].dtype)
    return out
```

```python
import math
from contextlib import ExitStack

import numpy as np

import concourse.bass as bass
from concourse import mybir

F32, I32 = mybir.dt.float32, mybir.dt.int32
ALU, ACT, AX = mybir.AluOpType, mybir.ActivationFunctionType, mybir.AxisListType

D = 1024
KD = D // 128
SEQ = 512
NSEQ, DSEQ = 8, 4
NDEC = NSEQ * DSEQ
NTOK = SEQ + NDEC
NT = 5
ROWS = [128, 128, 128, 128, NDEC]
CONVW = 31
PASTC = CONVW - 1
NH, HD = 8, 64
NG, EPG = 4, 4
NE = NG * EPG
DE = 256
PAGE, NPAGE = 128, 8
PAST = PAGE * NPAGE
EPS = 1e-6
LAM_INIT = 0.8 - 0.6 * math.exp(-0.3)
NEG = -1e30
MAIN = 128 * NE
EXTRA = 2 * NTOK // 128
SLOTS = MAIN + 128 * EXTRA
NKEY = PAST + NDEC

PCOL = {}
_at = 0
for _n, _w in (("g_mix0", 8), ("g_mix1", 8), ("g_ffn0", 8), ("g_ffn1", 8), ("g_kv", 8), ("b_pw1", 16),
               ("b_dw", 8), ("ln_g", 8), ("ln_b", 8), ("subln", 1), ("w_dw", 8 * CONVW),
               ("wr0", 160), ("wr1", 160), ("br0", 20), ("br1", 20), ("lams", 256)):
    PCOL[_n] = (_at, _w)
    _at += _w
NPCOL = _at
CCOL = {}
_at = 0
for _n, _w in (("ident", 128), ("before", 128), ("ones", 128), ("mean", 128), ("rev4", 4), ("expert", 16),
               ("upto", 256), ("tile", 8), ("comb", 64), ("isc0", 1), ("isc1", 1), ("headmask", 8), ("newbias", 4 * NDEC)):
    CCOL[_n] = (_at, _w)
    _at += _w
NCCOL = _at


def constants():
    p = np.arange(128)
    t = {}
    t["ident"] = np.eye(128)
    t["before"] = p[:, None] < p[None, :]
    t["ones"] = np.ones((128, 128))
    t["mean"] = np.full((128, 128), 1.0 / D)
    t["rev4"] = np.tile(np.array([4, 3, 2, 1]), (128, 1))
    t["expert"] = np.tile(np.arange(16), (128, 1))
    e = np.arange(NE)
    t["upto"] = np.tile((e[None, :] <= e[:, None]).reshape(1, -1), (128, 1))
    t["tile"] = np.tile(np.arange(EXTRA), (128, 1))
    row_s, row_c, row_ht = p // 64, p // 32 % 2, p % 32
    col = np.arange(64)
    t["comb"] = (row_s[:, None] == col[None, :] // 32) & (row_ht[:, None] == col[None, :] % 32)
    t["isc0"] = (row_c == 0)[:, None]
    t["isc1"] = (row_c == 1)[:, None]
    t["headmask"] = (p // 4 % 8)[:, None] == np.arange(8)[None, :]
    slope = 2.0 ** -(p // 4 % 8 + 1.0)
    tok = p % 4
    nb = np.empty((128, 4, NDEC))
    k = np.arange(NDEC)
    for pair in range(4):
        own = (2 * pair + row_s)[:, None] == k[None, :] // DSEQ
        ahead = tok[:, None] - (k % DSEQ)[None, :]
        nb[:, pair] = np.where(own & (ahead >= 0), -slope[:, None] * ahead, NEG)
    t["newbias"] = nb.reshape(128, -1)
    table = np.concatenate([np.asarray(t[n], np.float32).reshape(128, -1) for n in CCOL], axis=1)
    past = (-slope[:, None] * (PAST + tok[:, None] - np.arange(PAST)[None, :])).astype(np.float32)
    j = np.arange(896)[None, :] - 384
    dist = np.where(j <= p[:, None], j - p[:, None], NEG).astype(np.float32)
    ids = (np.arange(NT)[None, :] * 128 + p[:, None]).astype(np.int32)
    zero = np.zeros((128, SLOTS // 128), np.int32)
    return {"c_table": table, "c_past": past, "c_dist": dist, "c_ids": ids, "c_zero": zero}


def program(nc, a, o, scratch):
    with ExitStack() as ctx:
        def sb(name, shape, dt=F32):
            return ctx.enter_context(nc.sbuf_tensor(name, shape, dt))

        sems = {}

        TAGS = ("mix0", "ffn0", "kv", "o", "ffn1", "final")
        PER_TAG = {"ss": NT, "ms": 1, "sd": 1, "xh": NT, "t": KD + 1, "ev0": KD // 2 + 1, "ev1": KD // 2}
        PER_O = {"ss": 0, "ms": 0, "sd": 0, "xh": 4, "t": KD, "ev0": KD // 2, "ev1": KD // 2}
        PER_LAYER = {"gd": 1, "ed": 1, "gex": 1, "eex": 1, "logits": 1, "chosen": 1, "ranks": 1, "slots": 1, "extra_tab": 1, "extra_tok": 16, "turned": NE,
                     "xgT": 2 * NE, "gu": NE, "silu": NE, "hidden": NE, "ht": NE, "hT": NE, "down": NE, "y_v": NE, "y_a": NE,
                     "y_out_0": 8 * NE, "y_out_1": 8 * NE, "xg_0": 8 * NE, "xg_1": 8 * NE, "tokrow": 16,
                     "owner_out": 32 * NT, "rows_out": 32, "collected": NT, "ygat_0": 96, "ygat_1": 64,
                     "w_moe_0": 12 * NE, "w_moe_1": 12 * NE, "w_moe_2": 12 * NE, "w_moe_3": 12 * NE}

        IN_ORDER = {
            "pe_conv": (("state_t", 2 * KD), ("pw1_mm", KD), ("last_t", 2), ("mean", 1), ("var", 1)),
            "dve_ln": (("centred", KD), ("var_eps", 1), ("scaled", KD)),
            "act_conv": (("sig", 2 * KD), ("last_rows", 4), ("sq", KD), ("ln_sd", 1), ("conv_h", KD)),
            "pe_qkv": (("k_mm", NH), ("v_mm", 2 * NT), ("k_back", 2 * NT), ("q_mm", NH)),
            "dve_qkv": (("lam_sum", 1), ("kTd", 1), ("v_done", 2 * NT), ("qz1", NH), ("qdec", 1)),
            "act_qkv": (("kT", NH), ("k_rows", 2 * NT), ("qz0", NH), ("lam_exp", 1)),
            "chunk0": (("w_pw1_0", 32), ("w_pw2_0", 16), ("w_att0", 16), ("w_o0", 16)),
            "chunk1": (("w_pw1_1", 32), ("w_pw2_1", 16), ("w_att1", 16), ("w_o1", 16)),
            "chunk2": (("w_pw1_2", 32), ("w_att2", 16)),
            "chunk3": (("w_pw1_3", 32), ("w_att3", 16)),
        }
        BASE = {n: (s, sum(c for _, c in names[:q])) for s, names in IN_ORDER.items() for q, (n, _) in enumerate(names)}

        def place(name):
            if name in BASE:
                return BASE[name]
            stem, _, tag = name.partition("_")
            if stem in PER_TAG and tag in TAGS:
                return stem, sum((PER_O if x == "o" else PER_TAG)[stem] for x in TAGS[:TAGS.index(tag)])
            stem, _, layer = name.partition("@")
            return stem, PER_LAYER[stem] * int(layer) if layer else 0

        def sem(name):
            real = place(name)[0]
            if real not in sems:
                sems[real] = ctx.enter_context(nc.semaphore(real))
            return sems[real]

        resid = sb("resid", [128, NT, D])
        xhat = sb("xhat", [128, NT, D])
        xT = sb("xT", [128, KD, NTOK])
        ring = sb("ring", [128, 24576])
        work = sb("work", [128, 8704])
        par = sb("par", [128, NPCOL])
        con = sb("con", [128, NCCOL])
        junk = sb("junk", [128, D])
        small = sb("small", [128, 2130])
        ids = sb("ids", [128, NT], I32)
        slot_i = sb("slot_i", [128, 2, NT], I32)
        extra_tok = sb("extra_tok", [128, EXTRA], I32)
        extra_tab = sb("extra_tab", [128, EXTRA + 1], I32)
        tokrow = sb("tokrow", [128, NE], I32)
        pages = sb("pages", [1, 2 * NSEQ * NPAGE], I32)
        ps = [ctx.enter_context(nc.psum_tensor(f"ps{i}", [128, 512], F32)) for i in range(8)]

        def P(name):
            s, w = PCOL[name]
            return par[:, s:s + w]

        def C(name):
            s, w = CCOL[name]
            return con[:, s:s + w]

        used = [0]

        def sm(n):
            used[0] += n
            assert used[0] <= 2130
            return small[:, used[0] - n:used[0]]

        def WK(s, n):
            return work[:, s:s + n]

        def RG(s, n):
            return ring[:, s:s + n]

        ident = C("ident")
        SLOT = 6144

        def xTd(k):
            return xT[:, k, SEQ:NTOK]

        gp = WK(0, 8 * 542).rearrange("p (m t) -> p m t", m=8)
        gw = WK(4336, 8 * 272).rearrange("p (m s t) -> p m s t", m=8, s=NSEQ)
        sig = WK(6512, 2 * NTOK).rearrange("p (b t) -> p b t", b=2)
        cv = xhat[:, :, :].rearrange("p a d -> p (a d)")[:, 0:KD * NTOK].rearrange("p (m t) -> p m t", m=8)
        sq = WK(0, KD * NTOK).rearrange("p (m t) -> p m t", m=8)
        lnr = WK(6512, NTOK)
        state = RG(4096, 2048).rearrange("p (a d) -> p a d", a=2)
        last_p = RG(SLOT + 4096, 1024)
        last_s = RG(SLOT + 5120, 1024)
        prod = RG(2 * SLOT + 4096, 2 * 992).rearrange("p (b s x) -> p b s x", b=2, s=NDEC)
        bpw2 = RG(3 * SLOT + 4096, 1024)
        xg = WK(0, 2048).rearrange("p (b d) -> p b d", b=2)
        xgT = WK(2048, 1024).rearrange("p (k s) -> p k s", k=KD)
        hm = WK(3072, 512).rearrange("p (b f) -> p b f", b=2)
        hT = WK(3584, 256).rearrange("p (f s) -> p f s", f=2)
        sil = WK(3840, 512).rearrange("p (b f) -> p b f", b=2)
        yrow = WK(4352, 2048).rearrange("p (b d) -> p b d", b=2)
        ygat = WK(0, 4096).rearrange("p (b c d) -> p b c d", b=2, c=2)
        logit = WK(6400, 100).rearrange("p (i n) -> p i n", i=NT)
        gfin = WK(6528, 1024)
        xqT = WK(0, KD * NTOK).rearrange("p (k t) -> p k t", k=KD)
        kT = WK(4352, KD * NTOK).rearrange("p (h t) -> p h t", h=NH)
        vtok = xhat
        qz = [RG(4096 * c, 4096).rearrange("p (h t) -> p h t", h=NH) for c in range(2)]
        qdec = RG(8192, 4096).rearrange("p (s h r) -> p s h r", s=NSEQ, h=NH)
        otok = RG(12288, 4096).rearrange("p (i d) -> p i d", i=4)
        tbuf = RG(16384, 2048).rearrange("p (b c n) -> p b c n", b=2, c=2)
        aT = RG(18432, 1024).rearrange("p (b n) -> p b n", b=2)
        biash = RG(19456, 1792).rearrange("p (b n) -> p b n", b=2)
        dist = RG(21248, 896)
        ktk = RG(14336, 2048).rearrange("p (b d) -> p b d", b=2)
        kp = [[RG(1024 * (2 * b + j), 1024).rearrange("p (h n) -> p h n", h=NH) for j in range(2)] for b in range(2)]
        kring = WK(0, 4096).rearrange("p (b d) -> p b d", b=4)
        vring = RG(16384, 8192).rearrange("p (b d) -> p b d", b=8)
        xTflat = xT[:, :, :].rearrange("p k t -> p (k t)")
        tdec = xTflat[:, 0:2 * NKEY].rearrange("p (b n) -> p b n", b=2)
        aTd0 = xTflat[:, 2112:2112 + 9 * 128].rearrange("p (g r) -> p g r", g=9)
        aTd1 = kT[:, 0:3, 0:384].rearrange("p h (g r) -> p h g r", g=3)

        def aTd(quad, g):
            return aTd1[:, g // 3, g % 3, :] if quad else aTd0[:, g, :]
        oT = WK(0, KD * SEQ).rearrange("p (k t) -> p k t", k=KD)
        pastb = xTflat[:, 3264:3264 + PAST]
        odec = WK(4096, 256).rearrange("p (h t) -> p h t", h=NH)
        gwc = WK(7600, 256).rearrange("p (m t) -> p m t", m=KD)
        orow = sm(128)

        stat = {n: sm(w) for n, w in dict(ss=5, ms=5, sd=5, rstd=5).items()}
        r = {n: sm(w) for n, w in dict(
            gmax=5, geq=20, gsel=20, gmx=5, goh=20, gd=20, gex=20, gsum=5, pg=5, etmp=80, es=20, em=5, ed=20,
            eex=20, esum=5, er=5, pe=20, p1=5, eq1=20, sel1=20, mx1=5, oh1=20, pe2=20, p2=5, eq2=20, sel2=20,
            mx2=5, oh2=20, s12=5, rs=5, rsg=5, gate1=5, gate2=5, OH1=80, OH2=80, M=80, slot=80, t1=80, s1=5,
            s2=5, cnt=16, nx=16, nx2=16, cx=16, px=16, xbase=16, cmp=128, xe=9, rank=80, ext=80, diff=80).items()}

        out_sem = sem("outputs")
        n_out = [0]


        def at(name, count):
            return count + place(name)[1]

        LAYERS = (0, 1)
        EXTRA_SLOTS = (2, 0)

        def wload(l, e, slot):
            base = slot * SLOT
            gu = RG(base, 4096).rearrange("p (k n) -> p k n", k=KD)
            dn = RG(base + 4096, 2048).rearrange("p (f n) -> p f n", f=2)
            one = bass.ds(e, 1)
            g = a["moe_w_gate"][l][one].rearrange("a (k p) f -> p (a k) f", p=128)
            u = a["moe_w_up"][l][one].rearrange("a (k p) f -> p (a k) f", p=128)
            d = a["moe_w_down"][l][one].rearrange("a (f p) n -> p (a f) n", p=128)
            return ((gu[:, :, 0:DE], g), (gu[:, :, DE:2 * DE], u), (dn, d))


        asm_ = {n: sm(w) for n, w in dict(mx=4, nm=4, sums=4, rec=4, rl=4, oss=32, oms=32, osd=32, orstd=32, osc=8, lam=4, nlam=1,
                                         isc=1, dmx=3, dm=1, dnm=1, dsum=1, drec=1, drsc=1, combs=64, rss=1, rms=1, rsd=1,
                                         rrs=1, orn=128).items()}
        UNITS = [(h, i) for h in range(NH) for i in range(4)]
        N_UNITS = NSEQ // 2 * NPAGE
        LAG = 2
        FIRST_VALUES = 2 * NPAGE + LAG + 1
        QUAD0_VALUED = FIRST_VALUES + NPAGE

        def attention_pool(pool):
            pool.wait_ge(sem("k_mm"), at("k_mm", NH))
            pool.memset(qz[0][64:128, :, :], 0.0).then_inc(sem("qzero"), 1)
            pool.memset(qz[1][0:64, :, :], 0.0).then_inc(sem("qzero"), 1)
            pool.wait_ge(sem("v_mm"), at("v_mm", 2 * NT))
            pool.wait_ge(sem("qzero"), at("qzero", 2))
            pool.memset(RG(8192, 4096), 0.0).then_inc(sem("qzero"), 1)
            prompt_bias(pool)

        def attention_pe(pe):
            turn_pe(pe, "kv", xhat, NT)
            wait_turned(pe, "kv")
            for h in range(NH):
                if h % 4 == 0:
                    pe.wait_ge(sem(f"w_att{h // 4}"), at(f"w_att{h // 4}", 16))
                if h - 1 > 0:
                    pe.wait_ge(sem("kT"), at("kT", h - 1))
                w = RG(4096 * (h // 4), 4096).rearrange("p (k n) -> p k n", k=KD)
                for k in range(KD):
                    lhs = w[:, k, 128 * (h % 4):128 * (h % 4) + 128]
                    pe.matmul(ps[3 + h % 2][:, :], lhs, xT[:, k, 0:SEQ], start=(k == 0), stop=(k == KD - 1))
                    mm = pe.matmul(ps[5][:, NDEC * h:NDEC * h + NDEC], lhs, xTd(k), start=(k == 0), stop=(k == KD - 1))
                mm.then_inc(sem("k_mm"), 1)
            for c in range(2):
                pe.wait_ge(sem(f"w_att{2 + c}"), at(f"w_att{2 + c}", 16))
            n = 0
            for i in range(NT):
                for c in range(2):
                    if n - 3 > 0:
                        pe.wait_ge(sem("v_done"), at("v_done", n - 3))
                    w = RG(4096 * (2 + c), 4096).rearrange("p (k n) -> p k n", k=KD)
                    for k in range(KD):
                        mm = pe.matmul(ps[(6, 7, 0, 1)[n % 4]][0:ROWS[i], :], xT[:, k, 128 * i:128 * i + ROWS[i]], w[:, k, :], start=(k == 0), stop=(k == KD - 1))
                    mm.then_inc(sem("v_mm"), 1)
                    n += 1
            pe.wait_ge(sem("kT"), at("kT", NH))
            pe.wait_ge(sem("kTd"), at("kTd", 1))
            n = 0
            for i in range(NT):
                for b in range(2):
                    if n - 3 > 0:
                        pe.wait_ge(sem("k_rows"), at("k_rows", n - 3))
                    for h in range(4 * b, 4 * b + 4):
                        mm = pe.transpose(ps[2 + n % 4][0:ROWS[i], 128 * (h % 4):128 * (h % 4) + 128], kT[:, h, 128 * i:128 * i + ROWS[i]], ident)
                    mm.then_inc(sem("k_back"), 1)
                    n += 1
            pe.wait_ge(sem("v_done"), at("v_done", 2 * NT))
            for h in range(NH):
                if h % 4 == 0:
                    pe.wait_ge(sem(f"w_att{4 + h // 4}"), at(f"w_att{4 + h // 4}", 16))
                if h - 1 > 0:
                    pe.wait_ge(sem("qz0"), at("qz0", h - 1))
                if h - 1 > 0:
                    pe.wait_ge(sem("qz1"), at("qz1", h - 1))
                w = RG(4096 * (4 + h // 4), 4096).rearrange("p (k n) -> p k n", k=KD)
                for k in range(KD):
                    lhs = w[:, k, 128 * (h % 4):128 * (h % 4) + 128]
                    pe.matmul(ps[6 + h % 2][:, :], lhs, xqT[:, k, 0:SEQ], start=(k == 0), stop=(k == KD - 1))
                    mm = pe.matmul(ps[1][:, NDEC * h:NDEC * h + NDEC], lhs, xqT[:, k, SEQ:NTOK], start=(k == 0), stop=(k == KD - 1))
                mm.then_inc(sem("q_mm"), 1)

            def scores(u):
                h, i = UNITS[u]
                if 2 * (u - 1) > 0:
                    pe.wait_ge(sem("scored"), at("scored", 2 * (u - 1)))
                for c in range(2):
                    mm = pe.matmul(ps[2 * (u % 2) + c][:, 0:128 * (i + 1)], qz[c][:, h, 128 * i:128 * i + 128], kT[:, h, 0:128 * (i + 1)], start=True, stop=True)
                mm.then_inc(sem("s_mm"), 1)
            pe.wait_ge(sem("qz0"), at("qz0", NH))
            pe.wait_ge(sem("qz1"), at("qz1", NH))
            pe.wait_ge(sem("qdec"), at("qdec", 1))
            pe.wait_ge(sem("k_rows"), at("k_rows", 2 * NT))
            scores(0)
            scores(1)
            for u, (h, i) in enumerate(UNITS):
                pe.wait_ge(sem("weights"), at("weights", u + 1))
                if u - 1 > 0:
                    pe.wait_ge(sem("aT"), at("aT", u - 1))
                for b in range(i + 1):
                    mm = pe.transpose(ps[4 + u % 2][:, 128 * b:128 * b + 128], tbuf[:, u % 2, 0, 128 * b:128 * b + 128], ident)
                mm.then_inc(sem("a_turned"), 1)
                if u + 2 < len(UNITS):
                    scores(u + 2)
                pe.wait_ge(sem("aT"), at("aT", u + 1))
                if u - 1 > 0:
                    pe.wait_ge(sem("o_rows"), at("o_rows", u - 1))
                for b in range(i + 1):
                    mm = pe.matmul(ps[6 + u % 2][:, 0:128], aT[:, u % 2, 128 * b:128 * b + 128], vtok[:, b, 128 * h:128 * h + 128], start=(b == 0), stop=(b == i))
                mm.then_inc(sem("o_mm"), 1)
            pe.wait_ge(sem("o_rows"), at("o_rows", len(UNITS)))

            def page_turned(g):
                pe.wait_ge(sem(f"kpage{g % 4}"), at(f"kpage{g % 4}", 16 * (g // 4 + 1)))
                for b in range(2):
                    if g > 0:
                        pe.wait_ge(sem(f"kp{b}"), at(f"kp{b}", g))
                    for h in range(4):
                        c0 = 128 * (4 * b + h)
                        mm = pe.transpose(ps[b][:, 128 * h:128 * h + 128], kring[:, g % 4, c0:c0 + 128], ident)
                    mm.then_inc(sem("kturned_half"), 1) if b == 0 else mm.then_inc(sem("kturned"), 1)

            def page_scores(n, heads):
                pair, p = divmod(n, NPAGE)
                c0 = 128 * (p % 4)
                for h in heads:
                    for j in range(2):
                        mm = pe.matmul(ps[4 + p // 4][64 * j:64 * j + 64, c0:c0 + 128], qdec[:, 2 * pair + j, h, :], kp[n % 2][j][:, h, :], start=(h == 0), stop=(h == NH - 1))
                return mm

            def unit(n):
                for j in range(2):
                    if n < N_UNITS:
                        page_turned(2 * n + j)
                    if n:
                        if j == 0:
                            for b in range(2):
                                if 2 * n > 0:
                                    pe.wait_ge(sem(f"kp{b}"), at(f"kp{b}", 2 * n))
                            pair, p = divmod(n - 1, NPAGE)
                            if 3 * (pair - 1) + (1 if p < 4 else 2) > 0:
                                pe.wait_ge(sem("dscored"), at("dscored", 3 * (pair - 1) + (1 if p < 4 else 2)))
                        mm = page_scores(n - 1, range(4 * j, 4 * j + 4))
                if n:
                    mm.then_inc(sem("dec_scores"), 1)

            def new_scores(pair):
                if 3 * pair > 0:
                    pe.wait_ge(sem("dscored"), at("dscored", 3 * pair))
                for h in range(NH):
                    for j in range(2):
                        mm = pe.matmul(ps[6][64 * j:64 * j + 64, 0:NDEC], qdec[:, 2 * pair + j, h, :], kT[:, h, SEQ:NTOK], start=(h == 0), stop=(h == NH - 1))
                mm.then_inc(sem("new_scores"), 1)

            def pair_turned(pair):
                pe.wait_ge(sem("combs"), at("combs", pair + 1))
                if pair > 0:
                    pe.wait_ge(sem("aTd"), at("aTd", pair))
                if pair == 3:
                    pe.wait_ge(sem("odec"), at("odec", 1))
                for kk in range(NPAGE):
                    mm = pe.matmul(ps[7][:, 64 * kk:64 * kk + 64], tdec[:, pair % 2, 128 * kk:128 * kk + 128], asm_["combs"], start=True, stop=True)
                mm = pe.matmul(ps[6][0:NDEC, 64:128], tdec[:, pair % 2, PAST:NKEY], asm_["combs"], start=True, stop=True)
                mm.then_inc(sem("dT"), 1)

            def values_step(quad, p):
                if p == 0:
                    pe.wait_ge(sem("aTd"), at("aTd", 2 * (quad + 1)))
                    if 2 * quad > 0:
                        pe.wait_ge(sem("headed"), at("headed", 2 * quad))
                if p < NPAGE:
                    pe.wait_ge(sem(f"vpage{p % 2}"), at(f"vpage{p % 2}", 64 * (4 * quad + p // 2 + 1)))
                for c in range(2):
                    for j in range(4):
                        if p < NPAGE:
                            mm = pe.matmul(ps[2 + c][32 * j:32 * j + 32, :], aTd(quad, p)[:, 32 * j:32 * j + 32], vring[:, 4 * (p % 2) + j, 512 * c:512 * c + 512], start=(p == 0), stop=False)
                        else:
                            mm = pe.matmul(ps[2 + c][32 * j:32 * j + 32, :], aTd(quad, p)[0:NDEC, 32 * j:32 * j + 32], vtok[0:NDEC, 4, 512 * c:512 * c + 512], start=False, stop=True, tile_position=(0, 32 * j))
                mm.then_inc(sem("pv_mm" if p < NPAGE else "pv_all"), 1)

            def quad_turned(quad):
                pe.wait_ge(sem("orn"), at("orn", quad + 1))
                if 3 + quad > 0:
                    pe.wait_ge(sem("aTd"), at("aTd", 3 + quad))
                pe.transpose(ps[7][:, 0:128], asm_["orn"], ident).then_inc(sem("orn_t"), 1)
            new_scores(0)
            for n in range(N_UNITS + 1):
                unit(n)
                pair, p = divmod(n - LAG - NPAGE, NPAGE)
                if p == 0 and 0 <= pair < 3:
                    new_scores(pair + 1)
                    pair_turned(pair)
                if 0 <= n - FIRST_VALUES <= NPAGE:
                    values_step(0, n - FIRST_VALUES)
                if n == QUAD0_VALUED + 2:
                    quad_turned(0)
            turn_pe(pe, "o", otok, 4, dec=False)
            pair_turned(3)
            for p in range(NPAGE + 1):
                values_step(1, p)
            quad_turned(1)
            pe.wait_ge(sem("odec"), at("odec", 2))
            wait_turned(pe, "o", dec=False)
            for c in range(2):
                pe.wait_ge(sem(f"w_o{c}"), at(f"w_o{c}", 16))
            rows_out(pe, "wo", oT, [RG(4096 * c, 4096).rearrange("p (k n) -> p k n", k=KD) for c in range(2)], dec=odec)

        def attention_act(act):
            for i in range(NT):
                act.wait_ge(sem("collected@0"), at("collected@0", i + 1))
                row_squares(act, "kv", i)
            row_roots(act, "kv")
            turned_act(act, "kv", [(xT, P("g_kv")), (xqT, P("g_mix1"))])
            for h in range(NH):
                act.wait_ge(sem("k_mm"), at("k_mm", h + 1))
                act.copy(kT[:, h, 0:SEQ], ps[3 + h % 2][:, :]).then_inc(sem("kT"), 1)
            for n in range(2 * NT):
                i, b = n // 2, n % 2
                act.wait_ge(sem("k_back"), at("k_back", n + 1))
                if b == 0 and i >= 2:
                    if 16 * (i // 2) > 0:
                        act.wait_ge(sem(f"k_out{i % 2}"), at(f"k_out{i % 2}", 16 * (i // 2)))
                act.copy(ktk[0:ROWS[i], i % 2, 512 * b:512 * b + 512], ps[2 + n % 4][0:ROWS[i], :]).then_inc(sem("k_rows"), 1)
            act.wait_ge(sem("qzero"), at("qzero", 3))
            for h in range(NH):
                act.wait_ge(sem("q_mm"), at("q_mm", h + 1))
                act.activation(qz[0][0:64, h, :], ps[6 + h % 2][0:64, :], ACT.Copy, scale=HD ** -0.5).then_inc(sem("qz0"), 1)
            act.wait_ge(sem("lam_sum"), at("lam_sum", 1))
            act.activation(asm_["lam"][:, 2:4], asm_["lam"][:, 0:2], ACT.Exp).then_inc(sem("lam_exp"), 1)

            def exps(u):
                h, i = UNITS[u]
                act.wait_ge(sem("negmax"), at("negmax", u + 1))
                for c in range(2):
                    x = 2 * (u % 2) + c
                    t = tbuf[:, u % 2, c, 0:128 * (i + 1)]
                    act.activation(t, t, ACT.Exp, bias=asm_["nm"][:, x:x + 1], accum_out=asm_["sums"][:, x:x + 1]).then_inc(sem("exps"), 1)

            def square(u):
                h, i = UNITS[u]
                act.wait_ge(sem("o_rows"), at("o_rows", u + 1))
                act.activation(junk[:, 128 * (u % 8):128 * (u % 8) + 128], otok[:, i, 128 * h:128 * h + 128], ACT.Square,
                               accum_out=asm_["oss"][:, 8 * i + h:8 * i + h + 1]).then_inc(sem("oss"), 1)
            exps(0)
            for u, (h, i) in enumerate(UNITS):
                if u + 1 < len(UNITS):
                    exps(u + 1)
                act.wait_ge(sem("a_turned"), at("a_turned", u + 1))
                if u - 1 > 0:
                    act.wait_ge(sem("o_mm"), at("o_mm", u - 1))
                act.copy(aT[:, u % 2, 0:128 * (i + 1)], ps[4 + u % 2][:, 0:128 * (i + 1)]).then_inc(sem("aT"), 1)
                if u:
                    if u > 8:
                        if u - 8 > 0:
                            act.wait_ge(sem("oss"), at("oss", u - 8))
                    square(u - 1)
            act.wait_ge(sem("oss"), at("oss", len(UNITS) - 8))
            square(len(UNITS) - 1)
            act.wait_ge(sem("oms"), at("oms", 1))
            act.activation(asm_["osd"], asm_["oms"], ACT.Sqrt).then_inc(sem("osd"), 1)
            def exp_pair(pair):
                act.wait_ge(sem("dnm"), at("dnm", pair + 1))
                t = tdec[:, pair % 2, :]
                act.activation(t, t, ACT.Exp, bias=asm_["dnm"], accum_out=asm_["dsum"]).then_inc(sem("dexp"), 1)

            def turned_weights(pair):
                act.wait_ge(sem("dT"), at("dT", pair + 1))
                cols = slice(64 * (pair % 2), 64 * (pair % 2) + 64)
                groups = ps[7][:, :].rearrange("p (g r) -> p g r", g=NPAGE)
                if pair < 2:
                    act.copy(aTd0[:, 0:NPAGE, cols], groups)
                else:
                    act.copy(aTd1[:, 0:2, :, cols], groups[:, 0:6, :].rearrange("p (h g) r -> p h g r", h=2))
                    act.copy(aTd1[:, 2, 0:2, cols], groups[:, 6:NPAGE, :])
                act.copy(aTd(pair // 2, NPAGE)[0:NDEC, cols], ps[6][0:NDEC, 64:128]).then_inc(sem("aTd"), 1)

            def root(quad):
                act.wait_ge(sem("rms_row"), at("rms_row", quad + 1))
                act.activation(asm_["rsd"], asm_["rms"], ACT.Sqrt).then_inc(sem("rsd"), 1)
            for n in range(N_UNITS):
                for j in range(2):
                    act.wait_ge(sem("kturned"), at("kturned", 2 * n + j + 1))
                    if n - 1 > 0:
                        act.wait_ge(sem("dec_scores"), at("dec_scores", n - 1))
                    act.copy(kp[n % 2][j][:, 4:8, :], ps[1][:, :].rearrange("p (h n) -> p h n", h=4)).then_inc(sem("kp1"), 1)
                pair, p = divmod(n - NPAGE, NPAGE)
                if pair >= 0 and p == 1:
                    exp_pair(pair)
                if pair >= 0 and p == LAG + 1:
                    turned_weights(pair)
                if n == QUAD0_VALUED + 1:
                    root(0)
            exp_pair(3)
            turned_act(act, "o", [(oT, asm_["osc"])])
            turned_weights(3)
            root(1)

        def attention_dve(v):
            norm_stats(v, "kv")
            v.wait_ge(sem("rows_out@0"), at("rows_out@0", 32))
            norm_rows(v, "kv")
            lv = P("lams").rearrange("p (b c d) -> p b c d", b=2, c=2)
            for b in range(2):
                link(v, v.tensor_tensor(junk[:, 64 * b:64 * b + 64], lv[:, b, 0, :], lv[:, b, 1, :], ALU.mult))
                i = v.tensor_reduce(asm_["lam"][:, b:b + 1], junk[:, 64 * b:64 * b + 64], AX.X, ALU.add)
                if b == 0:
                    link(v, i)
            i.then_inc(sem("lam_sum"), 1)
            for h in range(NH):
                i = v.tensor_scalar(asm_["osc"][:, h:h + 1], P("subln"), 1.0 - LAM_INIT, None, ALU.mult)
            link(v, i)
            turned_dve(v, "kv", [(xT, P("g_kv")), (xqT, P("g_mix1"))])
            v.wait_ge(sem("k_mm"), at("k_mm", NH))
            v.tensor_copy(kT[:, :, SEQ:NTOK], ps[5][:, 0:KD * NDEC].rearrange("p (h t) -> p h t", h=NH)).then_inc(sem("kTd"), 1)
            n = 0
            v.wait_ge(sem("t_kv"), at("t_kv", KD + 1))
            for i in range(NT):
                for c in range(2):
                    v.wait_ge(sem("v_mm"), at("v_mm", n + 1))
                    v.tensor_copy(vtok[0:ROWS[i], i, 512 * c:512 * c + 512], ps[(6, 7, 0, 1)[n % 4]][0:ROWS[i], :]).then_inc(sem("v_done"), 1)
                    n += 1
            v.wait_ge(sem("qzero"), at("qzero", 3))
            for h in range(NH):
                v.wait_ge(sem("q_mm"), at("q_mm", h + 1))
                v.tensor_scalar(qz[1][64:128, h, :], ps[6 + h % 2][64:128, :], HD ** -0.5, None, ALU.mult).then_inc(sem("qz1"), 1)
            for h in range(NH):
                for c in range(2):
                    rows = slice(64 * c, 64 * c + 64)
                    i = v.tensor_scalar(qdec[rows, :, h, 32 * c + 4 * h:32 * c + 4 * h + 4], ps[1][rows, NDEC * h:NDEC * h + NDEC].rearrange("p (s t) -> p s t", s=NSEQ), HD ** -0.5, None, ALU.mult)
            i.then_inc(sem("qdec"), 1)
            v.wait_ge(sem("lam_exp"), at("lam_exp", 1))
            link(v, v.tensor_tensor(asm_["lam"][:, 0:1], asm_["lam"][:, 3:4], asm_["lam"][:, 2:3], ALU.subtract))
            link(v, v.tensor_scalar(asm_["nlam"], asm_["lam"][:, 0:1], -LAM_INIT, None, ALU.add))
            link(v, v.scalar_tensor_tensor(asm_["isc"], C("isc1"), asm_["nlam"], C("isc0"), ALU.mult, ALU.add))
            for b in range(2):
                v.wait_ge(sem(f"k_out{b}"), at(f"k_out{b}", (48, 32)[b]))

            def score(u):
                h, i = UNITS[u]
                v.wait_ge(sem("s_mm"), at("s_mm", u + 1))
                v.wait_ge(sem("biash"), at("biash", h + 1))
                if u - 1 > 0:
                    v.wait_ge(sem("a_turned"), at("a_turned", u - 1))
                n = 128 * (i + 1)
                for c in range(2):
                    x = 2 * (u % 2) + c
                    v.tensor_tensor_reduce(tbuf[:, u % 2, c, 0:n], ps[x][:, 0:n], biash[:, h % 2, 384 - 128 * i:384 - 128 * i + n], 1.0, -3e38,
                                           ALU.add, ALU.max, asm_["mx"][:, x:x + 1]).then_inc(sem("scored"), 1)
                v.wait_ge(sem("scored"), at("scored", 2 * (u + 1)))
                x = 2 * (u % 2)
                v.tensor_scalar(asm_["nm"][:, x:x + 2], asm_["mx"][:, x:x + 2], -1.0, None, ALU.mult).then_inc(sem("negmax"), 1)

            def weights(u):
                h, i = UNITS[u]
                n = 128 * (i + 1)
                x = 2 * (u % 2)
                v.wait_ge(sem("exps"), at("exps", 2 * (u + 1)))
                link(v, v.reciprocal(asm_["rec"][:, x:x + 2], asm_["sums"][:, x:x + 2]))
                link(v, v.tensor_tensor(asm_["rl"][:, x:x + 1], asm_["rec"][:, x + 1:x + 2], asm_["nlam"], ALU.mult))
                t0, t1 = tbuf[:, u % 2, 0, 0:n], tbuf[:, u % 2, 1, 0:n]
                link(v, v.tensor_scalar(t1, t1, asm_["rl"][:, x:x + 1], None, ALU.mult))
                v.scalar_tensor_tensor(t0, t0, asm_["rec"][:, x:x + 1], t1, ALU.mult, ALU.add).then_inc(sem("weights"), 1)

            def o_rows(u):
                h, i = UNITS[u]
                v.wait_ge(sem("o_mm"), at("o_mm", u + 1))
                v.tensor_copy(otok[:, i, 128 * h:128 * h + 128], ps[6 + u % 2][:, 0:128]).then_inc(sem("o_rows"), 1)
            score(0)
            for u in range(len(UNITS)):
                if u + 1 < len(UNITS):
                    score(u + 1)
                weights(u)
                if u:
                    o_rows(u - 1)
            o_rows(len(UNITS) - 1)
            v.wait_ge(sem("o_rows"), at("o_rows", len(UNITS)))
            v.sem_inc(sem("prompt_done"), 1)
            v.wait_ge(sem("oss"), at("oss", len(UNITS)))
            v.tensor_scalar(asm_["oms"], asm_["oss"], 1.0 / 128, EPS, ALU.mult, ALU.add).then_inc(sem("oms"), 1)
            v.wait_ge(sem("osd"), at("osd", 1))
            link(v, v.reciprocal(asm_["orstd"], asm_["osd"]))
            for i in range(4):
                head_ = otok[:, i, :].rearrange("p (h e) -> p h e", h=NH)
                v.tensor_tensor(head_, head_, asm_["orstd"][:, 8 * i:8 * i + 8].unsqueeze(2).broadcast_to([128, NH, 128]), ALU.mult).then_inc(sem("xh_o"), 1)
            v.wait_ge(sem("past_in"), at("past_in", 16))

            def biased(pair, dst, bank, bias, x):
                v.tensor_tensor_reduce(dst, bank, bias, 1.0, -3e38, ALU.add, ALU.max, asm_["dmx"][:, x:x + 1]).then_inc(sem("dscored"), 1)

            def first_half(pair):
                v.wait_ge(sem("dec_scores"), at("dec_scores", NPAGE * pair + 4))
                if pair - 1 > 0:
                    v.wait_ge(sem("dT"), at("dT", pair - 1))
                biased(pair, tdec[:, pair % 2, 0:512], ps[4][:, :], pastb[:, 0:512], 0)

            def pair_weights(pair):
                v.wait_ge(sem("dec_scores"), at("dec_scores", NPAGE * (pair + 1)))
                biased(pair, tdec[:, pair % 2, 512:PAST], ps[5][:, :], pastb[:, 512:PAST], 1)
                v.wait_ge(sem("new_scores"), at("new_scores", pair + 1))
                biased(pair, tdec[:, pair % 2, PAST:NKEY], ps[6][:, 0:NDEC], C("newbias")[:, NDEC * pair:NDEC * pair + NDEC], 2)
                v.wait_ge(sem("dscored"), at("dscored", 3 * (pair + 1)))
                link(v, v.tensor_reduce(asm_["dm"], asm_["dmx"], AX.X, ALU.max))
                v.tensor_scalar(asm_["dnm"], asm_["dm"], -1.0, None, ALU.mult).then_inc(sem("dnm"), 1)
                v.wait_ge(sem("dexp"), at("dexp", pair + 1))
                link(v, v.reciprocal(asm_["drec"], asm_["dsum"]))
                link(v, v.tensor_tensor(asm_["drsc"], asm_["drec"], asm_["isc"], ALU.mult))
                if pair > 0:
                    v.wait_ge(sem("dT"), at("dT", pair))
                v.tensor_scalar(asm_["combs"], C("comb"), asm_["drsc"], None, ALU.mult).then_inc(sem("combs"), 1)

            def own_heads(quad):
                v.wait_ge(sem("pv_all"), at("pv_all", quad + 1))
                hmk = C("headmask")
                for c in range(2):
                    v.tensor_tensor(junk[:, 512 * c:512 * c + 512].rearrange("p (h e) -> p h e", h=4), ps[2 + c][:, :].rearrange("p (h e) -> p h e", h=4),
                                    hmk[:, 4 * c:4 * c + 4].unsqueeze(2).broadcast_to([128, 4, 128]), ALU.mult).then_inc(sem("headed"), 1)
                v.wait_ge(sem("headed"), at("headed", 2 * (quad + 1)))
                link(v, v.tensor_reduce(orow, junk[:, :].rearrange("p (h e) -> p e h", h=NH), AX.X, ALU.add))
                link(v, v.tensor_tensor(junk[:, 0:128], orow, orow, ALU.mult))
                link(v, v.tensor_reduce(asm_["rss"], junk[:, 0:128], AX.X, ALU.add))
                v.tensor_scalar(asm_["rms"], asm_["rss"], 1.0 / 128, EPS, ALU.mult, ALU.add).then_inc(sem("rms_row"), 1)

            def head_norm(quad):
                v.wait_ge(sem("rsd"), at("rsd", quad + 1))
                link(v, v.reciprocal(asm_["rrs"], asm_["rsd"]))
                v.tensor_scalar(asm_["orn"], orow, asm_["rrs"], None, ALU.mult).then_inc(sem("orn"), 1)

            def features(quad):
                v.wait_ge(sem("orn_t"), at("orn_t", quad + 1))
                dst = odec[:, :, 16 * quad:16 * quad + 16].rearrange("p h (s t) -> p s h t", s=4)
                for s in range(4):
                    i = v.tensor_scalar(dst[:, s, :, :], ps[7][:, 32 * s:32 * s + 32].rearrange("p (h t) -> p h t", h=NH), asm_["osc"][:, 0:1], None, ALU.mult)
                i.then_inc(sem("odec"), 1)
            for n in range(N_UNITS):
                for j in range(2):
                    v.wait_ge(sem("kturned_half"), at("kturned_half", 2 * n + j + 1))
                    if n - 1 > 0:
                        v.wait_ge(sem("dec_scores"), at("dec_scores", n - 1))
                    v.tensor_copy(kp[n % 2][j][:, 0:4, :], ps[0][:, :].rearrange("p (h n) -> p h n", h=4)).then_inc(sem("kp0"), 1)
                pair, p = divmod(n, NPAGE)
                if p == 5:
                    first_half(pair)
                if p == 1 and pair > 0:
                    pair_weights(pair - 1)
                if n == QUAD0_VALUED:
                    own_heads(0)
                if n == QUAD0_VALUED + 1:
                    head_norm(0)
                if n == QUAD0_VALUED + 3:
                    features(0)
            pair_weights(3)
            turned_dve(v, "o", [(oT, asm_["osc"])], dec=False)
            own_heads(1)
            head_norm(1)
            features(1)
            rows_added(v, "wo")
            v.wait_ge(sem("wo_add"), at("wo_add", 2 * NT))

        def att_chunk(sp, c):
            wkv = a["w_kv"].rearrange("(k p) n -> p k n", p=128)
            wq = a["attn_w_q"][0].rearrange("(k p) n -> p k n", p=128)
            src = wkv[:, :, 512 * c:512 * c + 512] if c < 4 else wq[:, :, 512 * (c - 4):512 * (c - 3)]
            sp.dma_start(RG(4096 * c, 4096).rearrange("p (k n) -> p k n", k=KD), src).then_inc(sem(f"w_att{c}"), 16)

        def attention_first_loads(sp):
            for c in range(3):
                if NE - 3 + (c > 0) > 0:
                    sp.wait_ge(sem("down@0"), at("down@0", NE - 3 + (c > 0)))
                att_chunk(sp, c)

        def attention_loads(sp):
            sp.wait_ge(sem("collected@0"), at("collected@0", NT))
            for c in range(3, 6):
                att_chunk(sp, c)
            for i in range(NT):
                sp.wait_ge(sem("v_done"), at("v_done", 2 * (i + 1)))
                if i < 4:
                    sp.dma_start(o["v_prompt"][0, 128 * i:128 * i + 128].rearrange("p h e -> p (h e)"), vtok[:, i, :]).then_inc(out_sem, 16)
                else:
                    sp.dma_start(o["v_sample"].rearrange("s t h e -> (s t) (h e)"), vtok[0:NDEC, 4, :]).then_inc(out_sem, 16)
            for i in range(NT):
                sp.wait_ge(sem("k_rows"), at("k_rows", 2 * (i + 1)))
                n = ROWS[i]
                src = ktk[:, i % 2, :]
                if i < 4:
                    sp.dma_start(o["k_prompt"][0, 128 * i:128 * i + 128].rearrange("p h c d -> p (h c d)"), src).then_inc(sem(f"k_out{i % 2}"), 16)
                else:
                    sp.dma_start(o["k_sample"].rearrange("s t h c d -> (s t) (h c d)"), src[0:n, :]).then_inc(sem(f"k_out{i % 2}"), 16)
            n_out[0] += 16 * NT
            sp.wait_ge(sem("q_mm"), at("q_mm", NH))
            sp.dma_start(dist, a["c_dist"]).then_inc(sem("dist_in"), 16)
            sp.wait_ge(sem("pages_in"), at("pages_in", 16))
            sp.dma_start(pastb, a["c_past"]).then_inc(sem("past_in"), 16)
            ck = a["cache_k"].rearrange("n p h c d -> n p (h c d)")
            cvv = a["cache_v"].rearrange("n p h e -> n p (h e)")
            n_pool = a["cache_k"].shape[0]

            def page_in(src, dst, entry, s):
                reg = sp.value_load(pages[0:1, entry], min_val=0, max_val=n_pool - 1)
                sp.dma_start(dst, src[bass.ds(reg, 1)].rearrange("a p d -> p (a d)")).then_inc(s, 16)

            for u in range(4):
                page_in(ck, kring[:, u, :], slice(u, u + 1), sem(f"kpage{u}"))

            def key_groups(first, end):
                with sp.Fori(first, end) as g:
                    for u in range(4):
                        sp.wait_ge(sem("kturned"), at("kturned", 4 * g + (u - 3)))
                        page_in(ck, kring[:, u, :], bass.ds(4 * g + u, 1), sem(f"kpage{u}"))

            def values_in(n):
                if n - 1 > 0:
                    sp.wait_ge(sem("pv_mm"), at("pv_mm", n - 1))
                for j in range(4):
                    entry = NSEQ * NPAGE + 4 * n + j
                    page_in(cvv, vring[:, 4 * (n % 2) + j, :], slice(entry, entry + 1), sem(f"vpage{n % 2}"))
            key_groups(1, 6)
            sp.wait_ge(sem("prompt_done"), at("prompt_done", 1))
            values_in(0)
            key_groups(6, 8)
            values_in(1)
            key_groups(8, 11)
            for g in range(11, 16):
                for q in (2 * (g - 11), 2 * (g - 11) + 1):
                    if q < NPAGE:
                        values_in(q + 2)
                key_groups(g, g + 1)
            wo = a["attn_w_o"][0].rearrange("(k p) n -> p k n", p=128)
            for c in (1, 0):
                if c == 0:
                    sp.wait_ge(sem("dec_scores"), at("dec_scores", N_UNITS))
                sp.dma_start(RG(4096 * c, 4096).rearrange("p (k n) -> p k n", k=KD), wo[:, :, 512 * c:512 * c + 512]).then_inc(sem(f"w_o{c}"), 16)
            for n in range(10, 16):
                values_in(n)

        def prompt_bias(pool):
            pool.wait_ge(sem("dist_in"), at("dist_in", 16))
            for h in range(NH):
                if 8 * (h - 1) > 0:
                    pool.wait_ge(sem("scored"), at("scored", 8 * (h - 1)))
                pool.tensor_scalar(biash[:, h % 2, :], dist, 2.0 ** -(h + 1), None, ALU.mult).then_inc(sem("biash"), 1)

        def row_squares(act, tag, i):
            n = ROWS[i]
            act.activation(junk[0:n, :], resid[0:n, i, :], ACT.Square, accum_out=stat["ss"][0:n, i:i + 1]).then_inc(sem(f"ss_{tag}"), 1)
            act.wait_ge(sem(f"ss_{tag}"), at(f"ss_{tag}", i + 1))

        def row_roots(act, tag):
            act.wait_ge(sem(f"ms_{tag}"), at(f"ms_{tag}", 1))
            act.activation(stat["sd"], stat["ms"], ACT.Sqrt).then_inc(sem(f"sd_{tag}"), 1)

        def norm_stats(v, tag):
            v.wait_ge(sem(f"ss_{tag}"), at(f"ss_{tag}", NT))
            v.tensor_scalar(stat["ms"], stat["ss"], 1.0 / D, EPS, ALU.mult, ALU.add).then_inc(sem(f"ms_{tag}"), 1)
            v.wait_ge(sem(f"sd_{tag}"), at(f"sd_{tag}", 1))
            link(v, v.reciprocal(stat["rstd"], stat["sd"]))

        def norm_rows(v, tag):
            for i in range(NT):
                n = ROWS[i]
                v.tensor_scalar(xhat[0:n, i, :], resid[0:n, i, :], stat["rstd"][0:n, i:i + 1], None, ALU.mult).then_inc(sem(f"xh_{tag}"), 1)

        def turn_pe(pe, tag, src, tiles, dec=True):
            pe.wait_ge(sem(f"xh_{tag}"), at(f"xh_{tag}", tiles))
            for k in range(KD):
                if k >= 2:
                    if k // 2 > 0:
                        pe.wait_ge(sem(f"ev{k % 2}_{tag}"), at(f"ev{k % 2}_{tag}", k // 2))
                for i in range(4):
                    mm = pe.transpose(ps[k % 2][:, 128 * i:128 * i + 128], src[:, i, 128 * k:128 * k + 128], ident)
                mm.then_inc(sem(f"t_{tag}"), 1)
            if dec:
                for k in range(KD):
                    mm = pe.transpose(ps[2][:, NDEC * k:NDEC * k + NDEC], src[0:NDEC, 4, 128 * k:128 * k + 128], ident[0:NDEC, 0:NDEC])
                mm.then_inc(sem(f"t_{tag}"), 1)

        def turned_act(act, tag, outs):
            for k in range(1, KD, 2):
                act.wait_ge(sem(f"t_{tag}"), at(f"t_{tag}", k + 1))
                for dst, g in outs:
                    i = act.activation(dst[:, k, 0:SEQ], ps[1][:, :], ACT.Copy, scale=g[:, k:k + 1])
                i.then_inc(sem(f"ev1_{tag}"), 1)

        def turned_dve(v, tag, outs, dec=True):
            for k in range(0, KD, 2):
                v.wait_ge(sem(f"t_{tag}"), at(f"t_{tag}", k + 1))
                for dst, g in outs:
                    i = v.tensor_scalar(dst[:, k, 0:SEQ], ps[0][:, :], g[:, k:k + 1], None, ALU.mult)
                i.then_inc(sem(f"ev0_{tag}"), 1)
            if dec:
                v.wait_ge(sem(f"t_{tag}"), at(f"t_{tag}", KD + 1))
                for dst, g in outs:
                    i = v.tensor_tensor(dst[:, :, SEQ:NTOK], ps[2][:, 0:KD * NDEC].rearrange("p (k t) -> p k t", k=KD),
                                        g[:, 0:KD].unsqueeze(2).broadcast_to([128, KD, NDEC]), ALU.mult)
                i.then_inc(sem(f"ev0_{tag}"), 1)

        def wait_turned(eng, tag, dec=True):
            eng.wait_ge(sem(f"ev0_{tag}"), at(f"ev0_{tag}", KD // 2 + dec))
            eng.wait_ge(sem(f"ev1_{tag}"), at(f"ev1_{tag}", KD // 2))

        chain = [0]

        def link(v, ins):
            chain[0] += 1
            ins.then_inc(sem("dve_chain"), 1)
            v.wait_ge(sem("dve_chain"), at("dve_chain", chain[0]))

        def rows_out(pe, tag, src, w, dec=None):
            n = 0
            for i in range(NT):
                for c in range(2):
                    if n >= 4:
                        if n - 3 > 0:
                            pe.wait_ge(sem(f"{tag}_add"), at(f"{tag}_add", n - 3))
                    for k in range(KD):
                        lhs = dec[:, k, :] if (dec is not None and i == 4) else src[:, k, 128 * i:128 * i + ROWS[i]]
                        mm = pe.matmul(ps[2 + n % 4][0:ROWS[i], :], lhs, w[c][:, k, :], start=(k == 0), stop=(k == KD - 1))
                    mm.then_inc(sem(f"{tag}_mm"), 1)
                    n += 1

        def rows_added(v, tag):
            n = 0
            for i in range(NT):
                for c in range(2):
                    v.wait_ge(sem(f"{tag}_mm"), at(f"{tag}_mm", n + 1))
                    res = resid[0:ROWS[i], i, 512 * c:512 * c + 512]
                    v.tensor_tensor(res, ps[2 + n % 4][0:ROWS[i], :], res, ALU.add).then_inc(sem(f"{tag}_add"), 1)
                    n += 1

        def moe_pe(pe, l):
            turn_pe(pe, f"ffn{l}", xhat, NT)
            wait_turned(pe, f"ffn{l}")
            wr = P(f"wr{l}").rearrange("p (k n) -> p k n", k=KD)
            for i in range(NT):
                for k in range(KD):
                    mm = pe.matmul(ps[3][0:ROWS[i], 20 * i:20 * i + 20], xT[:, k, 128 * i:128 * i + ROWS[i]], wr[:, k, :], start=(k == 0), stop=(k == KD - 1))
            mm.then_inc(sem(f"logits@{l}"), 1)
            pe.wait_ge(sem(f"chosen@{l}"), at(f"chosen@{l}", 1))
            M = r["M"].rearrange("p (i e) -> p i e", i=NT)
            for i in range(NT):
                for q in range(i + 1):
                    n = ROWS[q]
                    lhs = C("ones") if q < i else C("before")
                    mm = pe.matmul(ps[4][0:ROWS[i], NE * i:NE * i + NE], lhs[0:n, 0:ROWS[i]], M[0:n, q, :], start=(q == 0), stop=(q == i))
            for q in range(NT):
                mm = pe.matmul(ps[4][:, NE * NT:NE * NT + NE], C("ones")[0:ROWS[q], :], M[0:ROWS[q], q, :], start=(q == 0), stop=(q == NT - 1))
            mm.then_inc(sem(f"ranks@{l}"), 1)

            def turn(e, par_, half):
                pe.wait_ge(sem(f"xg_{par_}@{l}"), at(f"xg_{par_}@{l}", 16 * (half + 1)))
                for k in range(KD):
                    mm = pe.transpose(ps[k // 4][:, 128 * (k % 4):128 * (k % 4) + 128], xg[:, par_, 128 * k:128 * k + 128], ident)
                mm.then_inc(sem(f"turned@{l}"), 1)

            def gate_up(e, slot, par_, quarter):
                pe.wait_ge(sem(f"w_moe_{slot}@{l}"), at(f"w_moe_{slot}@{l}", 48 * (quarter + 1)))
                pe.wait_ge(sem(f"xgT@{l}"), at(f"xgT@{l}", 2 * (e + 1)))
                if e - 1 > 0:
                    pe.wait_ge(sem(f"hidden@{l}"), at(f"hidden@{l}", e - 1))
                gu = RG(slot * SLOT, 4096).rearrange("p (k n) -> p k n", k=KD)
                for k in range(KD):
                    mm = pe.matmul(ps[2 + par_][:, :], xgT[:, k, :], gu[:, k, :], start=(k == 0), stop=(k == KD - 1))
                mm.then_inc(sem(f"gu@{l}"), 1)

            def hidden_turn(e, par_):
                pe.wait_ge(sem(f"hidden@{l}"), at(f"hidden@{l}", e + 1))
                for f in range(2):
                    mm = pe.transpose(ps[4][:, 128 * f:128 * f + 128], hm[:, par_, 128 * f:128 * f + 128], ident)
                mm.then_inc(sem(f"ht@{l}"), 1)

            def down(e, slot):
                pe.wait_ge(sem(f"hT@{l}"), at(f"hT@{l}", e + 1))
                if e > 0:
                    pe.wait_ge(sem(f"y_a@{l}"), at(f"y_a@{l}", e))
                if e > 0:
                    pe.wait_ge(sem(f"y_v@{l}"), at(f"y_v@{l}", e))
                dn = RG(slot * SLOT + 4096, 2048).rearrange("p (f n) -> p f n", f=2)
                for c in range(2):
                    for f in range(2):
                        mm = pe.matmul(ps[5 + c][:, :], hT[:, f, :], dn[:, f, 512 * c:512 * c + 512], start=(f == 0), stop=(f == 1))
                mm.then_inc(sem(f"down@{l}"), 1)

            turn(0, 0, 0)
            gate_up(0, 0, 0, 0)
            turn(1, 1, 0)
            for e in range(1, NE):
                gate_up(e, e % 4, e % 2, e // 4)
                hidden_turn(e - 1, (e - 1) % 2)
                if e < NE - 1:
                    turn(e + 1, (e + 1) % 2, (e + 1) // 2)
                down(e - 1, (e - 1) % 4)
            hidden_turn(NE - 1, 1)
            down(NE - 1, 3)

            pe.wait_ge(sem(f"extra_tab@{l}"), at(f"extra_tab@{l}", 1))
            n_extra = pe.value_load(extra_tab[0:1, EXTRA:EXTRA + 1], min_val=0, max_val=EXTRA)
            for x in range(EXTRA):
                with pe.If(n_extra > x):
                    slot = EXTRA_SLOTS[l] + x % 2
                    gu = RG(slot * SLOT, 4096).rearrange("p (k n) -> p k n", k=KD)
                    dn = RG(slot * SLOT + 4096, 2048).rearrange("p (f n) -> p f n", f=2)
                    done = sem(f"x{l}_pe")
                    pe.wait_ge(sem(f"x{l}_rows"), at(f"x{l}_rows", 16 * (x + 1)))
                    for k in range(KD):
                        mm = pe.transpose(ps[k // 4][:, 128 * (k % 4):128 * (k % 4) + 128], xg[:, 0, 128 * k:128 * k + 128], ident)
                    mm.then_inc(done, 1)
                    pe.wait_ge(sem(f"x{l}_w{x % 2}"), at(f"x{l}_w{x % 2}", 48 * (x // 2 + 1)))
                    pe.wait_ge(sem(f"x{l}_dve"), at(f"x{l}_dve", 3 * x + 1))
                    if x == 0:
                        pe.wait_ge(sem(f"hidden@{l}"), at(f"hidden@{l}", NE))
                    for k in range(KD):
                        mm = pe.matmul(ps[2][:, :], xgT[:, k, :], gu[:, k, :], start=(k == 0), stop=(k == KD - 1))
                    mm.then_inc(done, 1)
                    pe.wait_ge(sem(f"x{l}_dve"), at(f"x{l}_dve", 3 * x + 2))
                    for f in range(2):
                        mm = pe.transpose(ps[4][:, 128 * f:128 * f + 128], hm[:, 0, 128 * f:128 * f + 128], ident)
                    mm.then_inc(done, 1)
                    pe.wait_ge(sem(f"x{l}_act"), at(f"x{l}_act", 3 * x + 2))
                    if x == 0:
                        pe.wait_ge(sem(f"y_a@{l}"), at(f"y_a@{l}", NE))
                        pe.wait_ge(sem(f"y_v@{l}"), at(f"y_v@{l}", NE))
                    else:
                        if 3 * x > 0:
                            pe.wait_ge(sem(f"x{l}_dve"), at(f"x{l}_dve", 3 * x))
                    for c in range(2):
                        for f in range(2):
                            mm = pe.matmul(ps[5 + c][:, :], hT[:, f, :], dn[:, f, 512 * c:512 * c + 512], start=(f == 0), stop=(f == 1))
                    mm.then_inc(done, 1)

        def moe_act(act, l):
            turned_act(act, f"ffn{l}", [(xT, P(f"g_ffn{l}"))])
            act.wait_ge(sem(f"gd@{l}"), at(f"gd@{l}", 1))
            act.activation(r["gex"], r["gd"], ACT.Exp).then_inc(sem(f"gex@{l}"), 1)
            act.wait_ge(sem(f"ed@{l}"), at(f"ed@{l}", 1))
            act.activation(r["eex"], r["ed"], ACT.Exp).then_inc(sem(f"eex@{l}"), 1)

            def silu(e, par_):
                act.wait_ge(sem(f"gu@{l}"), at(f"gu@{l}", e + 1))
                if e - 1 > 0:
                    act.wait_ge(sem(f"hidden@{l}"), at(f"hidden@{l}", e - 1))
                act.activation(sil[:, par_, :], ps[2 + par_][:, 0:DE], ACT.Silu).then_inc(sem(f"silu@{l}"), 1)

            def finish(e, par_):
                act.wait_ge(sem(f"ht@{l}"), at(f"ht@{l}", e + 1))
                if e > 0:
                    act.wait_ge(sem(f"down@{l}"), at(f"down@{l}", e))
                act.copy(hT[:, :, :].rearrange("p f s -> p (f s)"), ps[4][:, 0:256]).then_inc(sem(f"hT@{l}"), 1)
                act.wait_ge(sem(f"down@{l}"), at(f"down@{l}", e + 1))
                if e >= 2:
                    if 16 * (e // 2) > 0:
                        act.wait_ge(sem(f"y_out_{par_}@{l}"), at(f"y_out_{par_}@{l}", 16 * (e // 2)))
                act.copy(yrow[:, par_, 512:1024], ps[6][:, :]).then_inc(sem(f"y_a@{l}"), 1)
                act.wait_ge(sem(f"y_a@{l}"), at(f"y_a@{l}", e + 1))
                act.wait_ge(sem(f"y_v@{l}"), at(f"y_v@{l}", e + 1))
                yd = scratch["y"][0:MAIN].rearrange("(q e) d -> q e d", e=NE)
                act.dma_start(yd[0:128, e, :], yrow[:, par_, :]).then_inc(sem(f"y_out_{par_}@{l}"), 16)
            silu(0, 0)
            for e in range(1, NE):
                silu(e, e % 2)
                finish(e - 1, (e - 1) % 2)
            finish(NE - 1, 1)
            act.wait_ge(sem(f"extra_tab@{l}"), at(f"extra_tab@{l}", 1))
            n_extra = act.value_load(extra_tab[0:1, EXTRA:EXTRA + 1], min_val=0, max_val=EXTRA)
            for x in range(EXTRA):
                with act.If(n_extra > x):
                    done = sem(f"x{l}_act")
                    act.wait_ge(sem(f"x{l}_pe"), at(f"x{l}_pe", 4 * x + 2))
                    act.activation(sil[:, 0, :], ps[2][:, 0:DE], ACT.Silu).then_inc(done, 1)
                    act.wait_ge(sem(f"x{l}_pe"), at(f"x{l}_pe", 4 * x + 3))
                    act.copy(hT[:, :, :].rearrange("p f s -> p (f s)"), ps[4][:, 0:256]).then_inc(done, 1)
                    act.wait_ge(sem(f"x{l}_pe"), at(f"x{l}_pe", 4 * x + 4))
                    if x == 0:
                        act.wait_ge(sem(f"y_out_0@{l}"), at(f"y_out_0@{l}", 16 * NE // 2))
                    else:
                        if 16 * x > 0:
                            act.wait_ge(sem(f"x{l}_y"), at(f"x{l}_y", 16 * x))
                    act.copy(yrow[:, 0, 512:1024], ps[6][:, :]).then_inc(done, 1)
                    act.wait_ge(sem(f"x{l}_act"), at(f"x{l}_act", 3 * x + 3))
                    act.wait_ge(sem(f"x{l}_dve"), at(f"x{l}_dve", 3 * x + 3))
                    act.dma_start(scratch["y"][MAIN:SLOTS].rearrange("(p x) d -> p x d", p=128)[:, x, :], yrow[:, 0, :]).then_inc(sem(f"x{l}_y"), 16)

        def moe_dve(v, l):
            turned_dve(v, f"ffn{l}", [(xT, P(f"g_ffn{l}"))])
            link(v, v.memset(WK(6400, 100), 0.0))
            link(v, v.memset(r["rank"], 0.0))
            v.wait_ge(sem(f"logits@{l}"), at(f"logits@{l}", 1))
            br = P(f"br{l}")
            link(v, v.tensor_tensor(logit[:, 0:4, :], ps[3][:, 0:80].rearrange("p (i n) -> p i n", i=4),
                                    br.unsqueeze(1).broadcast_to([128, 4, 20]), ALU.add))
            link(v, v.tensor_tensor(logit[0:NDEC, 4, :], ps[3][0:NDEC, 80:100], br[0:NDEC, :], ALU.add))
            G = logit[:, :, 0:NG]
            E_ = logit[:, :, NG:].rearrange("p i (g e) -> p i e g", g=NG)
            v4 = {n: r[n].rearrange("p (i n) -> p i n", i=NT) for n in
                  ("geq", "gsel", "goh", "gd", "gex", "es", "ed", "eex", "pe", "eq1", "sel1", "oh1", "pe2", "eq2", "sel2", "oh2")}

            def b4(x):
                return x.unsqueeze(2).broadcast_to([128, NT, 4])
            rev = C("rev4").unsqueeze(1).broadcast_to([128, NT, 4])

            def first_max(vals, mx, eq, sel, smx, oh):
                link(v, v.tensor_reduce(r[mx], vals, AX.X, ALU.max))
                link(v, v.tensor_tensor(v4[eq], vals, b4(r[mx]), ALU.is_equal))
                link(v, v.tensor_tensor(v4[sel], v4[eq], rev, ALU.mult))
                link(v, v.tensor_reduce(r[smx], v4[sel], AX.X, ALU.max))
                link(v, v.tensor_tensor(v4[oh], v4[sel], b4(r[smx]), ALU.is_equal))
            first_max(G, "gmax", "geq", "gsel", "gmx", "goh")
            v.tensor_tensor(v4["gd"], G, b4(r["gmax"]), ALU.subtract).then_inc(sem(f"gd@{l}"), 1)
            et = r["etmp"].rearrange("p (i e g) -> p i e g", i=NT, e=EPG)
            link(v, v.tensor_tensor(et, E_, v4["goh"].unsqueeze(2).broadcast_to([128, NT, EPG, NG]), ALU.mult))
            link(v, v.tensor_reduce(v4["es"], et, AX.X, ALU.add))
            link(v, v.tensor_reduce(r["em"], v4["es"], AX.X, ALU.max))
            v.tensor_tensor(v4["ed"], v4["es"], b4(r["em"]), ALU.subtract).then_inc(sem(f"ed@{l}"), 1)
            v.wait_ge(sem(f"gex@{l}"), at(f"gex@{l}", 1))
            link(v, v.tensor_reduce(r["gsum"], v4["gex"], AX.X, ALU.add))
            link(v, v.reciprocal(r["pg"], r["gsum"]))
            v.wait_ge(sem(f"eex@{l}"), at(f"eex@{l}", 1))
            link(v, v.tensor_reduce(r["esum"], v4["eex"], AX.X, ALU.add))
            link(v, v.reciprocal(r["er"], r["esum"]))
            link(v, v.tensor_tensor(v4["pe"], v4["eex"], b4(r["er"]), ALU.mult))
            first_max(v4["pe"], "p1", "eq1", "sel1", "mx1", "oh1")
            link(v, v.scalar_tensor_tensor(r["pe2"], r["oh1"], -2.0, r["pe"], ALU.mult, ALU.add))
            first_max(v4["pe2"], "p2", "eq2", "sel2", "mx2", "oh2")
            for oh, full in (("oh1", "OH1"), ("oh2", "OH2")):
                link(v, v.tensor_tensor(r[full].rearrange("p (i g e) -> p i g e", i=NT, g=NG),
                                        v4["goh"].unsqueeze(3).broadcast_to([128, NT, NG, EPG]),
                                        v4[oh].unsqueeze(2).broadcast_to([128, NT, NG, EPG]), ALU.mult))
            v.tensor_tensor(r["M"], r["OH1"], r["OH2"], ALU.add).then_inc(sem(f"chosen@{l}"), 1)
            link(v, v.tensor_tensor(r["s12"], r["p1"], r["p2"], ALU.add))
            link(v, v.reciprocal(r["rs"], r["s12"]))
            link(v, v.tensor_tensor(r["rsg"], r["rs"], r["pg"], ALU.mult))
            v.tensor_tensor(r["gate1"], r["p1"], r["rsg"], ALU.mult)
            link(v, v.tensor_tensor(r["gate2"], r["p2"], r["rsg"], ALU.mult))
            v.wait_ge(sem(f"ranks@{l}"), at(f"ranks@{l}", 1))
            rk = r["rank"].rearrange("p (i e) -> p i e", i=NT)
            link(v, v.tensor_copy(rk[:, 0:4, :], ps[4][:, 0:64].rearrange("p (i e) -> p i e", i=4)))
            link(v, v.tensor_copy(rk[0:NDEC, 4, :], ps[4][0:NDEC, 64:80]))
            link(v, v.tensor_copy(r["cnt"], ps[4][:, 80:96]))
            a_, b_ = r["nx"], r["nx2"]
            link(v, v.tensor_scalar(a_, r["cnt"], 128.0, None, ALU.is_gt))
            for q in range(2, 5):
                link(v, v.scalar_tensor_tensor(b_, r["cnt"], 128.0 * q, a_, ALU.is_gt, ALU.add))
                a_, b_ = b_, a_
            up = WK(7600, 256).rearrange("p (e f) -> p e f", e=NE)
            link(v, v.tensor_tensor(up, a_.unsqueeze(1).broadcast_to([128, NE, NE]), C("upto").rearrange("p (e f) -> p e f", e=NE), ALU.mult))
            link(v, v.tensor_reduce(r["cx"], up, AX.X, ALU.add))
            link(v, v.tensor_tensor(r["px"], r["cx"], a_, ALU.subtract))
            cmp = r["cmp"].rearrange("p (x e) -> p x e", x=EXTRA)
            link(v, v.tensor_tensor(cmp, r["cx"].unsqueeze(1).broadcast_to([128, EXTRA, NE]), C("tile").unsqueeze(2).broadcast_to([128, EXTRA, NE]), ALU.is_le))
            link(v, v.tensor_reduce(r["xe"][:, 0:EXTRA], cmp, AX.X, ALU.add))
            link(v, v.tensor_scalar(r["xe"][:, 0:EXTRA], r["xe"][:, 0:EXTRA], float(NE - 1), None, ALU.min))
            link(v, v.tensor_copy(r["xe"][:, EXTRA:EXTRA + 1], r["cx"][:, NE - 1:NE]))
            v.tensor_copy(extra_tab[:, :], r["xe"]).then_inc(sem(f"extra_tab@{l}"), 1)
            link(v, v.tensor_scalar(r["xbase"], r["px"], float(MAIN - 1), None, ALU.add))

            def per_token(x):
                return x.unsqueeze(1).broadcast_to([128, NT, NE])
            main = r["slot"].rearrange("p (i e) -> p i e", i=NT)
            link(v, v.scalar_tensor_tensor(main, rk, float(NE), per_token(C("expert")), ALU.mult, ALU.add))
            a_, b_ = r["ext"], r["diff"]
            link(v, v.tensor_scalar(a_, r["rank"], 128.0, None, ALU.is_ge))
            for q in range(2, 5):
                link(v, v.scalar_tensor_tensor(b_, r["rank"], 128.0 * q, a_, ALU.is_ge, ALU.add))
                a_, b_ = b_, a_
            link(v, v.tensor_scalar(b_, a_, float(1 - 128 * EXTRA), None, ALU.mult))
            link(v, v.scalar_tensor_tensor(r["ext"], r["rank"], float(EXTRA), b_, ALU.mult, ALU.add))
            ext = r["ext"].rearrange("p (i e) -> p i e", i=NT)
            link(v, v.tensor_tensor(ext, ext, per_token(r["xbase"]), ALU.add))
            link(v, v.tensor_tensor(r["diff"], r["ext"], r["slot"], ALU.subtract))
            link(v, v.scalar_tensor_tensor(r["ext"], r["rank"], 128.0, r["diff"], ALU.is_ge, ALU.mult))
            link(v, v.tensor_tensor(r["slot"], r["slot"], r["ext"], ALU.add))
            for c, (oh, s) in enumerate((("OH1", "s1"), ("OH2", "s2"))):
                link(v, v.tensor_tensor(r["t1"], r[oh], r["slot"], ALU.mult))
                link(v, v.tensor_reduce(r[s], r["t1"].rearrange("p (i e) -> p i e", i=NT), AX.X, ALU.add))
                link(v, v.tensor_copy(slot_i[:, c, :], r[s]))
            v.sem_inc(sem(f"slots@{l}"), 1)

            gT = P(f"g_ffn{l}")

            def xgT_out(e):
                v.wait_ge(sem(f"turned@{l}"), at(f"turned@{l}", e + 1))
                if e > 0:
                    v.wait_ge(sem(f"gu@{l}"), at(f"gu@{l}", e))
                for b in range(2):
                    v.tensor_tensor(xgT[:, 4 * b:4 * b + 4, :], ps[b][:, :].rearrange("p (k s) -> p k s", k=4),
                                    gT[:, 4 * b:4 * b + 4].unsqueeze(2).broadcast_to([128, 4, 128]), ALU.mult).then_inc(sem(f"xgT@{l}"), 1)

            def hidden(e, par_):
                v.wait_ge(sem(f"silu@{l}"), at(f"silu@{l}", e + 1))
                if e - 1 > 0:
                    v.wait_ge(sem(f"ht@{l}"), at(f"ht@{l}", e - 1))
                v.tensor_tensor(hm[:, par_, :], ps[2 + par_][:, DE:2 * DE], sil[:, par_, :], ALU.mult).then_inc(sem(f"hidden@{l}"), 1)

            def y_half(e, par_):
                v.wait_ge(sem(f"down@{l}"), at(f"down@{l}", e + 1))
                if e >= 2:
                    if 16 * (e // 2) > 0:
                        v.wait_ge(sem(f"y_out_{par_}@{l}"), at(f"y_out_{par_}@{l}", 16 * (e // 2)))
                v.tensor_copy(yrow[:, par_, 0:512], ps[5][:, :]).then_inc(sem(f"y_v@{l}"), 1)
            xgT_out(0)
            xgT_out(1)
            hidden(0, 0)
            for e in range(1, NE):
                if e < NE - 1:
                    xgT_out(e + 1)
                y_half(e - 1, (e - 1) % 2)
                hidden(e, e % 2)
            y_half(NE - 1, 1)
            n_extra = v.value_load(extra_tab[0:1, EXTRA:EXTRA + 1], min_val=0, max_val=EXTRA)
            for x in range(EXTRA):
                with v.If(n_extra > x):
                    done = sem(f"x{l}_dve")
                    v.wait_ge(sem(f"x{l}_pe"), at(f"x{l}_pe", 4 * x + 1))
                    for b in range(2):
                        i = v.tensor_tensor(xgT[:, 4 * b:4 * b + 4, :], ps[b][:, :].rearrange("p (k s) -> p k s", k=4),
                                            gT[:, 4 * b:4 * b + 4].unsqueeze(2).broadcast_to([128, 4, 128]), ALU.mult)
                    i.then_inc(done, 1)
                    v.wait_ge(sem(f"x{l}_act"), at(f"x{l}_act", 3 * x + 1))
                    v.tensor_tensor(hm[:, 0, :], ps[2][:, DE:2 * DE], sil[:, 0, :], ALU.mult).then_inc(done, 1)
                    v.wait_ge(sem(f"x{l}_pe"), at(f"x{l}_pe", 4 * x + 4))
                    if x == 0:
                        v.wait_ge(sem(f"y_out_0@{l}"), at(f"y_out_0@{l}", 16 * NE // 2))
                    else:
                        if 16 * x > 0:
                            v.wait_ge(sem(f"x{l}_y"), at(f"x{l}_y", 16 * x))
                    v.tensor_copy(yrow[:, 0, 0:512], ps[5][:, :]).then_inc(done, 1)
            for i in range(NT):
                n = ROWS[i]
                v.wait_ge(sem(f"ygat_{i % 2}@{l}"), at(f"ygat_{i % 2}@{l}", 32 * (i // 2 + 1)))
                res = resid[0:n, i, :]
                link(v, v.scalar_tensor_tensor(res, ygat[0:n, i % 2, 0, :], r["gate1"][0:n, i:i + 1], res, ALU.mult, ALU.add))
                v.scalar_tensor_tensor(res, ygat[0:n, i % 2, 1, :], r["gate2"][0:n, i:i + 1], res, ALU.mult, ALU.add).then_inc(sem(f"collected@{l}"), 1)


        block = ctx.enter_context(nc.Block())

        @block.sync
        def _(sp):
            sp.dma_start(con[:, :], a["c_table"]).then_inc(sem("con_in"), 16)
            sp.dma_start(resid[:, 0:4, :], a["x_prompt"][0].rearrange("(i p) d -> p i d", p=128)).then_inc(sem("x_in"), 16)
            sp.dma_start(resid[0:NDEC, 4, :], a["x_sample"].rearrange("s t d -> (s t) d")).then_inc(sem("x_in"), 16)
            sp.dma_start(par[:, :], a["params"]).then_inc(sem("par_in"), 16)
            w1 = a["conv_w_pw1"][0].rearrange("(k p) (b n) -> p k b n", p=128, b=2)
            for c in range(4):
                dst = RG(c * SLOT, 4096).rearrange("p (k b n) -> p k b n", k=KD, b=2)
                for b in range(2):
                    sp.dma_start(dst[:, :, b, :], w1[:, :, b, 256 * c:256 * c + 256]).then_inc(sem(f"w_pw1_{c}"), 16)
                if c == 0:
                    sp.dma_start(state[0:120, :, :], a["state_conv"][0].rearrange("(a s) t d -> (s t) a d", a=2)).then_inc(sem("state_in"), 16)
            sp.wait_ge(sem("extra_zero"), at("extra_zero", 1))
            for x in range(EXTRA):
                sp.dma_start(scratch["y"][MAIN + 128 * x:MAIN + 128 * x + 128], last_p).then_inc(sem("y_zero"), 16)
            sp.dma_start(bpw2, a["b_pw2_rows"]).then_inc(sem("bpw2_in"), 16)
            sp.dma_start(ids[:, :], a["c_ids"]).then_inc(sem("ids_in"), 16)
            sp.dma_start(pages[:, :], a["page_order"]).then_inc(sem("pages_in"), 16)
            for l in LAYERS:
                sp.dma_start(scratch[f"owner{l}"].rearrange("(p n) x -> p (n x)", p=128), a["c_zero"]).then_inc(sem("owner_zero"), 16)
            cs = o["conv_sample"][0]
            sp.dma_start(cs[:, 0:PASTC - DSEQ, :], a["state_conv"][0][:, DSEQ:, :]).then_inc(out_sem, 16)
            w2 = a["conv_w_pw2"][0].rearrange("(k p) n -> p k n", p=128)
            for c in range(2):
                sp.wait_ge(sem("pw1_mm"), at("pw1_mm", 2 * (c + 1)))
                dst = RG(c * SLOT, 4096).rearrange("p (k n) -> p k n", k=KD)
                sp.dma_start(dst, w2[:, :, 512 * c:512 * c + 512]).then_inc(sem(f"w_pw2_{c}"), 16)
            sp.wait_ge(sem("last_rows"), at("last_rows", 4))
            sp.dma_start(o["conv_prompt"][0, 0], last_p[2:32, :]).then_inc(out_sem, 16)
            for s in range(NSEQ):
                sp.dma_start(cs[s, PASTC - DSEQ:, :], last_s[4 * s:4 * s + 4, :]).then_inc(out_sem, 16)
            n_out[0] = 16 * (1 + 1 + NSEQ)

            for l in LAYERS:
                if l == 1:
                    sp.wait_ge(sem("t_o"), at("t_o", KD))
                    sp.wait_ge(sem("pv_all"), at("pv_all", 2))
                    sp.dma_start(gfin, a["g_final_rows"]).then_inc(sem("gfinal_in"), 16)
                for u in (2, 3, 0, 1):
                    if l == 0:
                        if u == 2:
                            sp.wait_ge(sem("pw1_mm"), at("pw1_mm", KD))
                            sp.wait_ge(sem("prod_used"), at("prod_used", KD))
                        elif u == 3:
                            sp.wait_ge(sem("bpw2_used"), at("bpw2_used", 1))
                        elif u == 0:
                            sp.wait_ge(sem("pw2_mm"), at("pw2_mm", 2 * NT))
                        else:
                            sp.wait_ge(out_sem, n_out[0])
                    elif u == 0:
                        sp.wait_ge(sem("wo_mm"), at("wo_mm", 2 * NT))
                    for dst, src in wload(l, u, u):
                        sp.dma_start(dst, src).then_inc(sem(f"w_moe_{u}@{l}"), 16)
                sp.wait_ge(sem(f"xh_ffn{l}"), at(f"xh_ffn{l}", NT))
                sp.dma_start(scratch[f"rows{l}"][0:SEQ].rearrange("(i p) d -> p i d", p=128), xhat[:, 0:4, :]).then_inc(sem(f"rows_out@{l}"), 16)
                sp.dma_start(scratch[f"rows{l}"][SEQ:NTOK], xhat[0:NDEC, 4, :]).then_inc(sem(f"rows_out@{l}"), 16)
                with sp.Fori(0, 3) as j:
                    for u in range(4):
                        sp.wait_ge(sem(f"down@{l}"), at(f"down@{l}", 4 * j + (u + 1)))
                        for dst, src in wload(l, 4 * j + (4 + u), u):
                            sp.dma_start(dst, src).then_inc(sem(f"w_moe_{u}@{l}"), 16)
                if l == 0:
                    attention_first_loads(sp)
                sp.wait_ge(sem(f"extra_tab@{l}"), at(f"extra_tab@{l}", 1))
                n_extra = sp.value_load(extra_tab[0:1, EXTRA:EXTRA + 1], min_val=0, max_val=EXTRA)
                for x in range(EXTRA):
                    with sp.If(n_extra > x):
                        if x < 2:
                            if NE - 3 + EXTRA_SLOTS[l] + x > 0:
                                sp.wait_ge(sem(f"down@{l}"), at(f"down@{l}", NE - 3 + EXTRA_SLOTS[l] + x))
                        else:
                            if 4 * (x - 1) > 0:
                                sp.wait_ge(sem(f"x{l}_pe"), at(f"x{l}_pe", 4 * (x - 1)))
                        e = sp.value_load(extra_tab[0:1, x:x + 1], min_val=0, max_val=NE - 1)
                        for dst, src in wload(l, e, EXTRA_SLOTS[l] + x % 2):
                            sp.dma_start(dst, src).then_inc(sem(f"x{l}_w{x % 2}"), 16)
                if l == 0:
                    attention_loads(sp)
            sp.wait_ge(sem("y_done"), at("y_done", NT))
            sp.dma_start(o["y_prompt"][0].rearrange("(i p) d -> p i d", p=128), resid[:, 0:4, :]).then_inc(out_sem, 16)
            sp.dma_start(o["y_sample"].rearrange("s t d -> (s t) d"), resid[0:NDEC, 4, :]).then_inc(out_sem, 16)
            n_out[0] += 32
            sp.wait_ge(out_sem, n_out[0])

        @block.gpsimd
        def _(pool):
            pool.memset(gp[:, :, 0:PASTC], 0.0).then_inc(sem("pad"), 1)
            pool.memset(last_p, 0.0).then_inc(sem("extra_zero"), 1)
            pool.memset(stat["ss"], 1.0).then_inc(sem("pad"), 1)
            wdw = P("w_dw").rearrange("p (m x) -> p m x", m=8)
            pool.wait_ge(sem("par_in"), at("par_in", 16))
            for m in range(KD):
                pool.wait_ge(sem("past0"), at("past0", m + 1))
                pool.wait_ge(sem("past1"), at("past1", m + 1))
                pool.wait_ge(sem("windows"), at("windows", m + 1))
                if m - 1 > 0:
                    pool.wait_ge(sem("prod_used"), at("prod_used", m - 1))
                w = gw[:, m, :, 0:CONVW]
                win = bass.AP(tensor=w.tensor, offset=w.offset, ap=[w.ap[0], w.ap[1], [1, DSEQ], [1, CONVW]])
                i = pool.tensor_tensor(prod[:, m % 2, :, :].rearrange("p (s t) x -> p s t x", s=NSEQ), win,
                                       wdw[:, m, :].unsqueeze(1).unsqueeze(1).broadcast_to([128, NSEQ, DSEQ, CONVW]), ALU.mult)
                i.then_inc(sem("prod"), 1)
            pool.wait_ge(sem("xh_mix0"), at("xh_mix0", NT))
            pool.wait_ge(sem("bpw2_in"), at("bpw2_in", 16))
            for i in range(NT):
                n = ROWS[i]
                ins = pool.tensor_tensor(resid[0:n, i, :], resid[0:n, i, :], bpw2[0:n, :], ALU.add)
                ins.then_inc(sem("bias_added"), 1)
            pool.wait_ge(sem("bias_added"), at("bias_added", NT))
            pool.sem_inc(sem("bpw2_used"), 1)

            for l in LAYERS:
                if l == 1:
                    attention_pool(pool)
                pool.wait_ge(sem("ids_in"), at("ids_in", 16))
                pool.wait_ge(sem("owner_zero"), at("owner_zero", 32))
                pool.wait_ge(sem(f"slots@{l}"), at(f"slots@{l}", 1))
                for i in range(NT):
                    for c in range(2):
                        n = ROWS[i]
                        pool.indirect_dma_start(scratch[f"owner{l}"], bass.IndirectOffsetOnAxis(ap=slot_i[0:n, c, i:i + 1], axis=0),
                                                ids[0:n, i:i + 1], None).then_inc(sem(f"owner_out@{l}"), 16)
                pool.wait_ge(sem(f"owner_out@{l}"), at(f"owner_out@{l}", 16 * 2 * NT))
                pool.dma_start(tokrow[:, :], scratch[f"owner{l}"][0:128 * NE].rearrange("(p n) x -> p (n x)", p=128)).then_inc(sem(f"tokrow@{l}"), 16)
                pool.wait_ge(sem(f"tokrow@{l}"), at(f"tokrow@{l}", 16))
                pool.wait_ge(sem(f"rows_out@{l}"), at(f"rows_out@{l}", 32))
                for e in range(NE):
                    if e - 1 > 0:
                        pool.wait_ge(sem(f"turned@{l}"), at(f"turned@{l}", e - 1))
                    pool.indirect_dma_start(xg[:, e % 2, :], None, scratch[f"rows{l}"], bass.IndirectOffsetOnAxis(ap=tokrow[:, e:e + 1], axis=0)).then_inc(sem(f"xg_{e % 2}@{l}"), 16)
                pool.dma_start(extra_tok[:, :], scratch[f"owner{l}"][MAIN:SLOTS].rearrange("(p x) a -> p (x a)", p=128)).then_inc(sem(f"extra_tok@{l}"), 16)
                pool.wait_ge(sem(f"extra_tok@{l}"), at(f"extra_tok@{l}", 16))
                pool.wait_ge(sem(f"extra_tab@{l}"), at(f"extra_tab@{l}", 1))
                pool.wait_ge(sem(f"turned@{l}"), at(f"turned@{l}", NE))
                n_extra = pool.value_load(extra_tab[0:1, EXTRA:EXTRA + 1], min_val=0, max_val=EXTRA)
                for x in range(EXTRA):
                    with pool.If(n_extra > x):
                        if 4 * x - 3 > 0:
                            pool.wait_ge(sem(f"x{l}_pe"), at(f"x{l}_pe", 4 * x - 3))
                        pool.indirect_dma_start(xg[:, 0, :], None, scratch[f"rows{l}"], bass.IndirectOffsetOnAxis(ap=extra_tok[:, x:x + 1], axis=0)).then_inc(sem(f"x{l}_rows"), 16)
                for b in range(2):
                    pool.wait_ge(sem(f"y_out_{b}@{l}"), at(f"y_out_{b}@{l}", 16 * NE // 2))
                for x in range(EXTRA):
                    with pool.If(n_extra > x):
                        pool.wait_ge(sem(f"x{l}_y"), at(f"x{l}_y", 16 * (x + 1)))
                        pool.nop()
                for i in range(NT):
                    n = ROWS[i]
                    if i - 1 > 0:
                        pool.wait_ge(sem(f"collected@{l}"), at(f"collected@{l}", i - 1))
                    for c in range(2):
                        pool.indirect_dma_start(ygat[0:n, i % 2, c, :], None, scratch["y"], bass.IndirectOffsetOnAxis(ap=slot_i[0:n, c, i:i + 1], axis=0)).then_inc(sem(f"ygat_{i % 2}@{l}"), 16)

        @block.tensor
        def _(pe):
            pe.wait_ge(sem("con_in"), at("con_in", 16))
            turn_pe(pe, "mix0", xhat, NT)
            pe.wait_ge(sem("state_in"), at("state_in", 16))
            for k in range(KD):
                for b in range(2):
                    if k > 0:
                        pe.wait_ge(sem(f"past{b}"), at(f"past{b}", k))
                    pe.transpose(ps[6 + b][:, 0:120], state[0:120, b, 128 * k:128 * k + 128], ident[0:120, 0:120]).then_inc(sem("state_t"), 1)
            wait_turned(pe, "mix0")
            for m in range(KD):
                c = m // 2
                if m % 2 == 0:
                    pe.wait_ge(sem(f"w_pw1_{c}"), at(f"w_pw1_{c}", 32))
                if 2 * (m - 1) > 0:
                    pe.wait_ge(sem("glu"), at("glu", 2 * (m - 1)))
                w = RG(c * SLOT, 4096).rearrange("p (k b n) -> p k b n", k=KD, b=2)
                b0 = 3 * (m % 2)
                for b in range(2):
                    for k in range(KD):
                        lhs = w[:, k, b, 128 * (m % 2):128 * (m % 2) + 128]
                        pe.matmul(ps[b0 + b][:, :], lhs, xT[:, k, 0:SEQ], start=(k == 0), stop=(k == KD - 1))
                        mm = pe.matmul(ps[b0 + 2][:, NDEC * b:NDEC * b + NDEC], lhs, xTd(k), start=(k == 0), stop=(k == KD - 1))
                mm.then_inc(sem("pw1_mm"), 1)
            pe.wait_ge(sem("glu"), at("glu", 2 * KD))
            for half in range(2):
                for m in range(4 * half, 4 * half + 4):
                    c0 = 128 * (m % 4)
                    pe.transpose(ps[half][0:32, c0:c0 + 128], gp[:, m, 510:542], ident)
                    mm = pe.transpose(ps[2 + half][0:32, c0:c0 + 128], gwc[:, m, :], ident)
                mm.then_inc(sem("last_t"), 1)
            for m in range(KD):
                pe.wait_ge(sem("conv"), at("conv", m + 1))
                pe.matmul(ps[6][:, :], C("mean"), cv[:, m, 0:SEQ], start=(m == 0), stop=(m == KD - 1))
                mm = pe.matmul(ps[7][:, 0:NDEC], C("mean"), cv[:, m, SEQ:NTOK], start=(m == 0), stop=(m == KD - 1))
            mm.then_inc(sem("mean"), 1)
            pe.wait_ge(sem("last_rows"), at("last_rows", 4))
            for m in range(KD):
                pe.wait_ge(sem("sq"), at("sq", m + 1))
                pe.matmul(ps[0][:, :], C("mean"), sq[:, m, 0:SEQ], start=(m == 0), stop=(m == KD - 1))
                mm = pe.matmul(ps[1][:, 0:NDEC], C("mean"), sq[:, m, SEQ:NTOK], start=(m == 0), stop=(m == KD - 1))
            mm.then_inc(sem("var"), 1)
            for c in range(2):
                pe.wait_ge(sem(f"w_pw2_{c}"), at(f"w_pw2_{c}", 16))
            pe.wait_ge(sem("conv_h"), at("conv_h", KD))
            rows_out(pe, "pw2", xT, [RG(c * SLOT, 4096).rearrange("p (k n) -> p k n", k=KD) for c in range(2)])
            for l in LAYERS:
                moe_pe(pe, l)
                if l == 0:
                    attention_pe(pe)

        @block.scalar
        def _(act):
            act.wait_ge(sem("pad"), at("pad", 2))
            for i in range(NT):
                act.wait_ge(sem("x_in"), at("x_in", 32))
                row_squares(act, "mix0", i)
            row_roots(act, "mix0")
            act.wait_ge(sem("par_in"), at("par_in", 16))
            turned_act(act, "mix0", [(xT, P("g_mix0"))])
            for k in range(KD):
                act.wait_ge(sem("state_t"), at("state_t", 2 * k + 2))
                act.copy(gw[:, k, 4:8, 0:PASTC], ps[7][:, 0:120].rearrange("p (s t) -> p s t", s=4)).then_inc(sem("past1"), 1)
            bp = P("b_pw1")
            for m in range(KD):
                act.wait_ge(sem("pw1_mm"), at("pw1_mm", m + 1))
                if 2 * (m - 1) > 0:
                    act.wait_ge(sem("glu"), at("glu", 2 * (m - 1)))
                b0 = 3 * (m % 2)
                act.activation(sig[:, m % 2, 0:SEQ], ps[b0 + 1][:, :], ACT.Sigmoid, bias=bp[:, 8 + m:9 + m]).then_inc(sem("sig"), 1)
                act.activation(sig[:, m % 2, SEQ:NTOK], ps[b0 + 2][:, NDEC:2 * NDEC], ACT.Sigmoid, bias=bp[:, 8 + m:9 + m]).then_inc(sem("sig"), 1)
            for half in range(2):
                act.wait_ge(sem("last_t"), at("last_t", half + 1))
                act.wait_ge(sem("y_zero"), at("y_zero", 16 * EXTRA))
                act.copy(last_p[0:32, 512 * half:512 * half + 512], ps[half][0:32, :]).then_inc(sem("last_rows"), 1)
                act.copy(last_s[0:32, 512 * half:512 * half + 512], ps[2 + half][0:32, :]).then_inc(sem("last_rows"), 1)
            for m in range(KD):
                act.wait_ge(sem("centred"), at("centred", m + 1))
                act.activation(sq[:, m, :], cv[:, m, :], ACT.Square).then_inc(sem("sq"), 1)
            act.wait_ge(sem("var_eps"), at("var_eps", 1))
            act.activation(lnr, lnr, ACT.Sqrt).then_inc(sem("ln_sd"), 1)
            for m in range(KD):
                act.wait_ge(sem("scaled"), at("scaled", m + 1))
                act.activation(xT[:, m, :], cv[:, m, :], ACT.Silu, bias=P("ln_b")[:, m:m + 1], scale=P("ln_g")[:, m:m + 1]).then_inc(sem("conv_h"), 1)
            for i in range(NT):
                act.wait_ge(sem("pw2_add"), at("pw2_add", 2 * (i + 1)))
                row_squares(act, "ffn0", i)
            row_roots(act, "ffn0")
            for l in LAYERS:
                moe_act(act, l)
                if l == 0:
                    attention_act(act)
                    for i in range(NT):
                        act.wait_ge(sem("wo_add"), at("wo_add", 2 * (i + 1)))
                        row_squares(act, "ffn1", i)
                    row_roots(act, "ffn1")
            for i in range(NT):
                act.wait_ge(sem("collected@1"), at("collected@1", i + 1))
                row_squares(act, "final", i)
            row_roots(act, "final")

        @block.vector
        def _(v):
            norm_stats(v, "mix0")
            norm_rows(v, "mix0")
            v.wait_ge(sem("par_in"), at("par_in", 16))
            turned_dve(v, "mix0", [(xT, P("g_mix0"))])
            for k in range(KD):
                v.wait_ge(sem("state_t"), at("state_t", 2 * k + 1))
                v.tensor_copy(gw[:, k, 0:4, 0:PASTC], ps[6][:, 0:120].rearrange("p (s t) -> p s t", s=4)).then_inc(sem("past0"), 1)
            bp = P("b_pw1")
            wdw = P("w_dw").rearrange("p (m x) -> p m x", m=8)
            v.wait_ge(sem("pad"), at("pad", 1))

            def glu(m):
                v.wait_ge(sem("sig"), at("sig", 2 * (m + 1)))
                b0 = 3 * (m % 2)
                v.scalar_tensor_tensor(gp[:, m, PASTC:], ps[b0][:, :], bp[:, m:m + 1], sig[:, m % 2, 0:SEQ], ALU.add, ALU.mult).then_inc(sem("glu"), 1)
                link(v, v.scalar_tensor_tensor(gwc[:, m, :], ps[b0 + 2][:, 0:NDEC], bp[:, m:m + 1], sig[:, m % 2, SEQ:NTOK], ALU.add, ALU.mult))
                v.tensor_copy(gw[:, m, :, PASTC:], gwc[:, m, :].rearrange("p (s t) -> p s t", s=NSEQ)).then_inc(sem("windows"), 1)
                v.wait_ge(sem("windows"), at("windows", m + 1))
                v.sem_inc(sem("glu"), 1)

            def conv(m):
                link(v, v.tensor_scalar(cv[:, m, 0:SEQ], gp[:, m, 0:SEQ], wdw[:, m, 0:1], P("b_dw")[:, m:m + 1], ALU.mult, ALU.add))
                for x in range(1, CONVW):
                    link(v, v.scalar_tensor_tensor(cv[:, m, 0:SEQ], gp[:, m, x:x + SEQ], wdw[:, m, x:x + 1], cv[:, m, 0:SEQ], ALU.mult, ALU.add))
                    if x == 15 and m < KD - 1:
                        glu(m + 1)
                v.wait_ge(sem("prod"), at("prod", m + 1))
                link(v, v.tensor_reduce(cv[:, m, SEQ:NTOK], prod[:, m % 2, :, :], AX.X, ALU.add))
                v.sem_inc(sem("prod_used"), 1)
                v.tensor_scalar(cv[:, m, SEQ:NTOK], cv[:, m, SEQ:NTOK], P("b_dw")[:, m:m + 1], None, ALU.add).then_inc(sem("conv"), 1)

            v.wait_ge(sem("t_mix0"), at("t_mix0", KD + 1))
            glu(0)
            for m in range(KD):
                conv(m)
            v.wait_ge(sem("mean"), at("mean", 1))
            v.wait_ge(sem("conv"), at("conv", KD))
            for m in range(KD):
                v.tensor_tensor(cv[:, m, 0:SEQ], cv[:, m, 0:SEQ], ps[6][:, :], ALU.subtract)
                v.tensor_tensor(cv[:, m, SEQ:NTOK], cv[:, m, SEQ:NTOK], ps[7][:, 0:NDEC], ALU.subtract).then_inc(sem("centred"), 1)
            v.wait_ge(sem("var"), at("var", 1))
            v.tensor_scalar(lnr[:, 0:SEQ], ps[0][:, :], EPS, None, ALU.add)
            v.tensor_scalar(lnr[:, SEQ:NTOK], ps[1][:, 0:NDEC], EPS, None, ALU.add).then_inc(sem("var_eps"), 1)
            v.wait_ge(sem("ln_sd"), at("ln_sd", 1))
            link(v, v.reciprocal(lnr, lnr))
            v.wait_ge(sem("centred"), at("centred", KD))
            for m in range(KD):
                v.tensor_tensor(cv[:, m, :], cv[:, m, :], lnr, ALU.mult).then_inc(sem("scaled"), 1)
            v.wait_ge(sem("bias_added"), at("bias_added", NT))
            rows_added(v, "pw2")
            v.wait_ge(sem("pw2_add"), at("pw2_add", 10))
            norm_stats(v, "ffn0")
            v.wait_ge(sem("conv_h"), at("conv_h", KD))
            norm_rows(v, "ffn0")
            for l in LAYERS:
                moe_dve(v, l)
                if l == 0:
                    attention_dve(v)
                    norm_stats(v, "ffn1")
                    norm_rows(v, "ffn1")
            norm_stats(v, "final")
            norm_rows(v, "final")
            v.wait_ge(sem("xh_final"), at("xh_final", NT))
            v.wait_ge(sem("gfinal_in"), at("gfinal_in", 16))
            for i in range(NT):
                n = ROWS[i]
                v.tensor_tensor(resid[0:n, i, :], xhat[0:n, i, :], gfin[0:n, :], ALU.mult).then_inc(sem("y_done"), 1)



_INS = ["x_prompt", "x_sample", "cache_k", "cache_v", "state_conv", "conv_w_pw1", "conv_w_pw2", "w_kv", "attn_w_q", "attn_w_o",
        "moe_w_gate", "moe_w_up", "moe_w_down"]
_OUTS = [("y_prompt", (1, SEQ, D)), ("y_sample", (NSEQ, DSEQ, D)), ("conv_prompt", (1, 1, PASTC, D)), ("conv_sample", (1, NSEQ, PASTC, D)),
         ("k_prompt", (1, SEQ, NH, 2, HD)), ("v_prompt", (1, SEQ, NH, 2 * HD)), ("k_sample", (NSEQ, DSEQ, NH, 2, HD)),
         ("v_sample", (NSEQ, DSEQ, NH, 2 * HD))]


def laid_out(inp):
    def feat(x):
        x = np.asarray(x)
        return x.reshape(-1, 128).T

    def rows(x):
        return np.tile(np.asarray(x).reshape(1, -1), (128, 1))
    t = {}
    for l in range(2):
        t[f"g_mix{l}"] = feat(inp["norm_mix"][l])
        t[f"g_ffn{l}"] = feat(inp["norm_ffn"][l])
        wr = np.concatenate([np.asarray(inp["moe_w_grp"][l]), np.asarray(inp["moe_w_exp_router"][l]).reshape(D, NE)], axis=1)
        t[f"wr{l}"] = wr.reshape(KD, 128, 20).transpose(1, 0, 2).reshape(128, -1)
        t[f"br{l}"] = rows(np.concatenate([np.asarray(inp["moe_b_grp"][l]), np.asarray(inp["moe_b_exp_router"][l]).reshape(-1)]))
    t["g_kv"] = feat(inp["norm_kv"])
    t["b_pw1"] = feat(inp["conv_b_pw1"][0])
    t["b_dw"] = feat(inp["conv_b_dw"][0])
    t["ln_g"] = feat(inp["conv_ln_g"][0])
    t["ln_b"] = feat(inp["conv_ln_b"][0])
    t["subln"] = feat(inp["attn_subln_g"][0])
    t["w_dw"] = np.asarray(inp["conv_w_dw"][0]).reshape(CONVW, KD, 128).transpose(2, 1, 0).reshape(128, -1)
    t["lams"] = rows(np.concatenate([np.asarray(inp[f"attn_lambda_{n}"][0]) for n in ("q1", "k1", "q2", "k2")]))
    pt = np.asarray(inp["page_table"])
    order = np.concatenate([pt.reshape(4, 2, 8).transpose(0, 2, 1).reshape(-1), pt.reshape(2, 4, 8).transpose(0, 2, 1).reshape(-1)])
    return {"params": np.concatenate([t[n] for n in PCOL], axis=1), "page_order": order.reshape(1, -1),
            "b_pw2_rows": rows(inp["conv_b_pw2"][0]), "g_final_rows": rows(inp["norm_final"])}


def kernel(**inputs):
    import concourse.bacc as bacc
    from concourse.bass_utils import run_bass_kernel_spmd

    nc = bacc.Bacc("TRN2", target_bir_lowering=False, num_devices=1)
    arrays = {n: np.ascontiguousarray(inputs[n]) for n in _INS}
    arrays.update({n: np.ascontiguousarray(x) for n, x in {**laid_out(inputs), **constants()}.items()})
    a = {n: nc.dram_tensor(f"in_{n}", x.shape, mybir.dt.from_np(x.dtype), kind="ExternalInput").ap() for n, x in arrays.items()}
    o = {n: nc.dram_tensor(f"out_{n}", s, F32, kind="ExternalOutput").ap() for n, s in _OUTS}
    scratch = {"y": nc.dram_tensor("y_rows", (SLOTS, D), F32, kind="Internal").ap()}
    for l in range(2):
        scratch[f"owner{l}"] = nc.dram_tensor(f"owner{l}", (SLOTS, 1), I32, kind="Internal").ap()
        scratch[f"rows{l}"] = nc.dram_tensor(f"rows{l}", (NTOK, D), F32, kind="Internal").ap()
    program(nc, a, o, scratch)
    nc.compile()
    r = run_bass_kernel_spmd(nc, [{f"in_{n}": x for n, x in arrays.items()}], core_ids=[0])
    return tuple(r.results[0][f"out_{n}"] for n, _ in _OUTS)
```

```python
import math
from contextlib import ExitStack

import numpy as np

import concourse.bass as bass
from concourse import mybir

F32, I32, BF16 = mybir.dt.float32, mybir.dt.int32, mybir.dt.bfloat16
ALU, ACT, AX = mybir.AluOpType, mybir.ActivationFunctionType, mybir.AxisListType

D = 1024
KD = D // 128
SEQ = 512
NSEQ, DSEQ = 8, 4
NDEC = NSEQ * DSEQ
NTOK = SEQ + NDEC
HTOK = NTOK // 2
NT = 5
ROWS = [128, 128, 128, 128, NDEC]
CONVW = 31
PASTC = CONVW - 1
NH, HD = 8, 64
NG, EPG = 4, 4
NE = NG * EPG
DE = 256
PAGE, NPAGE = 128, 8
PAST = PAGE * NPAGE
EPS = 1e-6
LAM_INIT = 0.8 - 0.6 * math.exp(-0.3)
NEG = -1e30
MAIN = 128 * NE
EXTRA = 2 * NTOK // 128
SLOTS = MAIN + 128 * EXTRA
NKEY = PAST + NDEC

PCOL = {}
_at = 0
for _n, _w in (("g_mix0", 8), ("g_mix1", 8), ("g_ffn0", 8), ("g_ffn1", 8), ("g_kv", 8), ("b_pw1", 16),
               ("b_dw", 8), ("ln_g", 8), ("ln_b", 8), ("subln", 1), ("w_dw", 8 * CONVW),
               ("wr0", 160), ("wr1", 160), ("br0", 20), ("br1", 20), ("lams", 256)):
    PCOL[_n] = (_at, _w)
    _at += _w
NPCOL = _at
CCOL = {}
_at = 0
for _n, _w in (("ident", 128), ("before", 128), ("ones", 128), ("mean", 128), ("rev4", 4), ("expert", 16),
               ("upto", 256), ("tile", 8), ("comb", 64), ("isc0", 1), ("isc1", 1), ("headmask", 8), ("newbias", 4 * NDEC)):
    CCOL[_n] = (_at, _w)
    _at += _w
NCCOL = _at


def constants():
    p = np.arange(128)
    t = {}
    t["ident"] = np.eye(128)
    t["before"] = p[:, None] < p[None, :]
    t["ones"] = np.ones((128, 128))
    t["mean"] = np.full((128, 128), 1.0 / D)
    t["rev4"] = np.tile(np.array([4, 3, 2, 1]), (128, 1))
    t["expert"] = np.tile(np.arange(16), (128, 1))
    e = np.arange(NE)
    t["upto"] = np.tile((e[None, :] <= e[:, None]).reshape(1, -1), (128, 1))
    t["tile"] = np.tile(np.arange(EXTRA), (128, 1))
    row_s, row_c, row_ht = p // 64, p // 32 % 2, p % 32
    col = np.arange(64)
    t["comb"] = (row_s[:, None] == col[None, :] // 32) & (row_ht[:, None] == col[None, :] % 32)
    t["isc0"] = (row_c == 0)[:, None]
    t["isc1"] = (row_c == 1)[:, None]
    t["headmask"] = (p // 4 % 8)[:, None] == np.arange(8)[None, :]
    slope = 2.0 ** -(p // 4 % 8 + 1.0)
    tok = p % 4
    nb = np.empty((128, 4, NDEC))
    k = np.arange(NDEC)
    for pair in range(4):
        own = (2 * pair + row_s)[:, None] == k[None, :] // DSEQ
        ahead = tok[:, None] - (k % DSEQ)[None, :]
        nb[:, pair] = np.where(own & (ahead >= 0), -slope[:, None] * ahead, NEG)
    t["newbias"] = nb.reshape(128, -1)
    table = np.concatenate([np.asarray(t[n], np.float32).reshape(128, -1) for n in CCOL], axis=1)
    past = (-slope[:, None] * (PAST + tok[:, None] - np.arange(PAST)[None, :])).astype(np.float32)
    j = np.arange(896)[None, :] - 384
    dist = np.where(j <= p[:, None], j - p[:, None], NEG).astype(np.float32)
    ids = (np.arange(NT)[None, :] * 128 + p[:, None]).astype(np.int32)
    zero = np.zeros((128, SLOTS // 128), np.int32)
    return {"c_table": table, "c_past": past, "c_dist": dist, "c_ids": ids, "c_zero": zero}


def program(nc, a, o, scratch):
    with ExitStack() as ctx:
        def sb(name, shape, dt=F32):
            return ctx.enter_context(nc.sbuf_tensor(name, shape, dt))

        sems = {}

        TAGS = ("mix0", "ffn0", "kv", "o", "ffn1", "final")
        PER_TAG = {"ss": NT, "ms": 1, "sd": 1, "xh": NT, "t": KD + 1, "ev0": KD // 2 + 1, "ev1": KD // 2}
        PER_O = {"ss": 0, "ms": 0, "sd": 0, "xh": 4, "t": KD, "ev0": KD // 2, "ev1": KD // 2}
        PER_LAYER = {"gd": 1, "ed": 1, "gex": 1, "eex": 1, "logits": 1, "chosen": 1, "ranks": 1, "slots": 1, "extra_tab": 1, "extra_tok": 16, "turned": NE,
                     "xgT": 2 * NE, "gu": NE, "silu": NE, "hidden": NE, "ht": NE, "hT": NE, "down": NE, "y_v": NE, "y_a": NE,
                     "y_out_0": 8 * NE, "y_out_1": 8 * NE, "xg_0": 8 * NE, "xg_1": 8 * NE, "tokrow": 16,
                     "owner_out": 32 * NT, "rows_out": 32, "collected": NT, "ygat_0": 64, "ygat_1": 64, "ygat_2": 32,
                     "w_moe_0": 12 * NE, "w_moe_1": 12 * NE, "w_moe_2": 12 * NE, "w_moe_3": 12 * NE}

        IN_ORDER = {
            "pe_conv": (("state_t", 2 * KD), ("pw1_mm", KD), ("last_t", 2), ("mean", 1), ("var", 1)),
            "dve_ln": (("centred", KD), ("var_eps", 1), ("scaled", KD)),
            "act_conv": (("sig", KD), ("last_rows", 4), ("sq", KD), ("ln_sd", 1), ("conv_h", KD)),
            "pe_qkv": (("k_mm", NH), ("v_mm", 2 * NT), ("k_back", 2 * NT), ("q_mm", NH)),
            "dve_qkv": (("lam_sum", 1), ("v_done", 2 * NT), ("qz1", NH)),
            "act_qkv": (("kT", NH), ("k_rows", 2 * NT), ("qz0", NH), ("lam_exp", 1)),
            "chunk0": (("w_pw1_0", 32), ("w_pw2_0", 16), ("w_att0", 16), ("w_o0", 16)),
            "chunk1": (("w_pw1_1", 32), ("w_pw2_1", 16), ("w_att1", 16), ("w_o1", 16)),
            "chunk2": (("w_pw1_2", 32), ("w_att2", 16)),
            "chunk3": (("w_pw1_3", 32), ("w_att3", 16)),
        }
        BASE = {n: (s, sum(c for _, c in names[:q])) for s, names in IN_ORDER.items() for q, (n, _) in enumerate(names)}

        def place(name):
            if name in BASE:
                return BASE[name]
            stem, _, tag = name.partition("_")
            if stem in PER_TAG and tag in TAGS:
                return stem, sum((PER_O if x == "o" else PER_TAG)[stem] for x in TAGS[:TAGS.index(tag)])
            stem, _, layer = name.partition("@")
            return stem, PER_LAYER[stem] * int(layer) if layer else 0

        def sem(name):
            real = place(name)[0]
            if real not in sems:
                sems[real] = ctx.enter_context(nc.semaphore(real))
            return sems[real]

        resid = sb("resid", [128, NT, D])
        xhat = sb("xhat", [128, NT, D])
        xT = sb("xT", [128, KD, NTOK])
        ring = sb("ring", [128, 24576])
        work = sb("work", [128, 8704])
        par = sb("par", [128, NPCOL])
        con = sb("con", [128, NCCOL])
        junk = sb("junk", [128, D])
        small = sb("small", [128, 1970])
        ids = sb("ids", [128, NT], I32)
        slot_i = sb("slot_i", [128, 2, NT], I32)
        extra_tok = sb("extra_tok", [128, EXTRA], I32)
        extra_tab = sb("extra_tab", [128, EXTRA + 1], I32)
        chosen = sb("chosen", [128, NT, NE], BF16)
        count = sb("count", [128, 2, 128], BF16)
        tokrow = sb("tokrow", [128, NE], I32)
        pages = sb("pages", [1, 2 * NSEQ * NPAGE], I32)
        banks = ctx.enter_context(nc.psum_tensor("banks", [128, 8, 512], F32))
        ps = [banks[:, i, :] for i in range(8)]

        def two_banks(b):
            return banks[:, b:b + 2, 0:HTOK]

        def halves(x):
            return x.rearrange("p (c t) -> p c t", c=2)

        def P(name):
            s, w = PCOL[name]
            return par[:, s:s + w]

        def C(name):
            s, w = CCOL[name]
            return con[:, s:s + w]

        used = [0]

        def sm(n):
            used[0] += n
            assert used[0] <= 1970
            return small[:, used[0] - n:used[0]]

        def WK(s, n):
            return work[:, s:s + n]

        def RG(s, n):
            return ring[:, s:s + n]

        ident = C("ident")
        SLOT = 6144

        def xTd(k):
            return xT[:, k, SEQ:NTOK]

        gp = WK(0, KD * (PASTC + NTOK)).rearrange("p (m t) -> p m t", m=KD)
        gw = WK(4592, 8 * 272).rearrange("p (m s t) -> p m s t", m=8, s=NSEQ)
        sig = WK(6768, 2 * NTOK).rearrange("p (b t) -> p b t", b=2)
        cv = xhat[:, :, :].rearrange("p a d -> p (a d)")[:, 0:KD * NTOK].rearrange("p (m t) -> p m t", m=8)
        POOL_TILES = (2, 5)
        DVE_TILES = (0, 1, 3, 4, 6, 7)
        sq = WK(0, KD * NTOK).rearrange("p (m t) -> p m t", m=8)
        lnr = WK(6768, NTOK)
        state = RG(4096, 2048).rearrange("p (a d) -> p a d", a=2)
        last_p = RG(SLOT + 4096, 1024)
        last_s = RG(SLOT + 5120, 1024)
        prod = RG(2 * SLOT + 4096, 2 * 992).rearrange("p (b s x) -> p b s x", b=2, s=NDEC)
        bpw2 = RG(3 * SLOT + 4096, 1024)
        xg = WK(0, 2048).rearrange("p (b d) -> p b d", b=2)
        xgT = WK(2048, 1024).rearrange("p (k s) -> p k s", k=KD)
        hm = WK(3072, 512).rearrange("p (b f) -> p b f", b=2)
        hT = WK(3584, 256).rearrange("p (f s) -> p f s", f=2)
        sil = WK(3840, 512).rearrange("p (b f) -> p b f", b=2)
        yrow = WK(4352, 2048).rearrange("p (b d) -> p b d", b=2)
        ygat = WK(0, 6144).rearrange("p (b c d) -> p b c d", b=3, c=2)
        logit = WK(6400, 100).rearrange("p (i n) -> p i n", i=NT)
        gfin = WK(6528, 1024)
        xqT = WK(0, KD * NTOK).rearrange("p (k t) -> p k t", k=KD)
        kT = WK(4352, KD * NTOK).rearrange("p (h t) -> p h t", h=NH)
        vtok = xhat
        qz = [RG(4096 * c, 4096).rearrange("p (h t) -> p h t", h=NH) for c in range(2)]
        qdec = RG(8192, 4096).rearrange("p (s h r) -> p s h r", s=NSEQ, h=NH)
        otok = RG(12288, 4096).rearrange("p (i d) -> p i d", i=4)
        tbuf = RG(16384, 2048).rearrange("p (b c n) -> p b c n", b=2, c=2)
        aT = RG(18432, 1024).rearrange("p (b n) -> p b n", b=2)
        biash = RG(19456, 1792).rearrange("p (b n) -> p b n", b=2)
        dist = RG(21248, 896)
        ktk = RG(14336, 2048).rearrange("p (b d) -> p b d", b=2)
        kp = [[RG(1024 * (2 * b + j), 1024).rearrange("p (h n) -> p h n", h=NH) for j in range(2)] for b in range(2)]
        kring = WK(0, 4096).rearrange("p (b d) -> p b d", b=4)
        vring = RG(16384, 8192).rearrange("p (b d) -> p b d", b=8)
        xTflat = xT[:, :, :].rearrange("p k t -> p (k t)")
        tdec = xTflat[:, 0:2 * NKEY].rearrange("p (b n) -> p b n", b=2)
        aTd0 = xTflat[:, 2112:2112 + 9 * 128].rearrange("p (g r) -> p g r", g=9)
        aTd1 = kT[:, 0:3, 0:384].rearrange("p h (g r) -> p h g r", g=3)

        def aTd(quad, g):
            return aTd1[:, g // 3, g % 3, :] if quad else aTd0[:, g, :]
        oT = WK(0, KD * SEQ).rearrange("p (k t) -> p k t", k=KD)
        pastb = xTflat[:, 3264:3264 + PAST]
        odec = WK(4096, 256).rearrange("p (h t) -> p h t", h=NH)
        orow = sm(128)

        stat = {n: sm(w) for n, w in dict(ss=5, ms=5, sd=5, rstd=5).items()}
        r = {n: sm(w) for n, w in dict(
            gmax=5, geq=20, gsel=20, gmx=5, goh=20, gd=20, gex=20, gsum=5, pg=5, etmp=80, es=20, em=5, ed=20,
            eex=20, esum=5, er=5, pe=20, p1=5, eq1=20, sel1=20, mx1=5, oh1=20, pe2=20, p2=5, eq2=20, sel2=20,
            mx2=5, oh2=20, s12=5, rs=5, rsg=5, gate1=5, gate2=5, OH1=80, OH2=80, slot=80, s1=5,
            s2=5, cnt=16, nx=16, nx2=16, cx=16, px=16, xbase=16, cmp=128, xe=9, rank=80, ext=80, diff=80).items()}

        r["t1"] = r["etmp"]
        out_sem = sem("outputs")
        n_out = [0]


        def at(name, count):
            return count + place(name)[1]

        LAYERS = (0, 1)
        EXTRA_SLOTS = (2, 0)

        def wload(l, e, slot):
            base = slot * SLOT
            gu = RG(base, 4096).rearrange("p (k n) -> p k n", k=KD)
            dn = RG(base + 4096, 2048).rearrange("p (f n) -> p f n", f=2)
            one = bass.ds(e, 1)
            g = a["moe_w_gate"][l][one].rearrange("a (k p) f -> p (a k) f", p=128)
            u = a["moe_w_up"][l][one].rearrange("a (k p) f -> p (a k) f", p=128)
            d = a["moe_w_down"][l][one].rearrange("a (f p) n -> p (a f) n", p=128)
            return ((gu[:, :, 0:DE], g), (gu[:, :, DE:2 * DE], u), (dn, d))


        asm_ = {n: sm(w) for n, w in dict(mx=4, nm=4, sums=4, rec=4, rl=4, oss=32, oms=32, osd=32, orstd=32, osc=8, lam=4, nlam=1,
                                         isc=1, dmx=3, dm=1, dnm=1, dsum=1, drec=1, drsc=1, combs=64, rss=1, rms=1, rsd=1,
                                         rrs=1, orn=128).items()}
        UNITS = [(h, i) for h in range(NH) for i in range(4)]
        N_UNITS = NSEQ // 2 * NPAGE
        LAG = 2
        FIRST_VALUES = 2 * NPAGE + LAG + 1
        QUAD0_VALUED = FIRST_VALUES + NPAGE

        def attention_pool(pool):
            pool.wait_ge(sem("k_mm"), at("k_mm", NH))
            pool.memset(qz[0][64:128, :, :], 0.0).then_inc(sem("qzero"), 1)
            pool.memset(qz[1][0:64, :, :], 0.0).then_inc(sem("qzero"), 1)
            pool.wait_ge(sem("v_mm"), at("v_mm", 2 * NT))
            pool.wait_ge(sem("qzero"), at("qzero", 2))
            pool.memset(RG(8192, 4096), 0.0).then_inc(sem("qzero"), 1)
            prompt_bias(pool)

        def attention_pe(pe):
            turn_pe(pe, "kv", xhat, NT)
            wait_turned(pe, "kv")
            for h in range(NH):
                if h % 4 == 0:
                    pe.wait_ge(sem(f"w_att{h // 4}"), at(f"w_att{h // 4}", 16))
                if h - 1 > 0:
                    pe.wait_ge(sem("kT"), at("kT", h - 1))
                w = RG(4096 * (h // 4), 4096).rearrange("p (k n) -> p k n", k=KD)
                for k in range(KD):
                    mm = all_tokens(pe, 4 + 2 * (h % 2), w[:, k, 128 * (h % 4):128 * (h % 4) + 128], xT, k)
                mm.then_inc(sem("k_mm"), 1)
            for c in range(2):
                pe.wait_ge(sem(f"w_att{2 + c}"), at(f"w_att{2 + c}", 16))
            n = 0
            for i in range(NT):
                for c in range(2):
                    if n - 3 > 0:
                        pe.wait_ge(sem("v_done"), at("v_done", n - 3))
                    w = RG(4096 * (2 + c), 4096).rearrange("p (k n) -> p k n", k=KD)
                    for k in range(KD):
                        mm = pe.matmul(ps[n % 4][0:ROWS[i], :], xT[:, k, 128 * i:128 * i + ROWS[i]], w[:, k, :], start=(k == 0), stop=(k == KD - 1))
                    mm.then_inc(sem("v_mm"), 1)
                    n += 1
            pe.wait_ge(sem("kT"), at("kT", NH))
            n = 0
            for i in range(NT):
                for b in range(2):
                    if n - 3 > 0:
                        pe.wait_ge(sem("k_rows"), at("k_rows", n - 3))
                    for h in range(4 * b, 4 * b + 4):
                        mm = pe.transpose(ps[4 + n % 4][0:ROWS[i], 128 * (h % 4):128 * (h % 4) + 128], kT[:, h, 128 * i:128 * i + ROWS[i]], ident)
                    mm.then_inc(sem("k_back"), 1)
                    n += 1
            pe.wait_ge(sem("v_done"), at("v_done", 2 * NT))
            for h in range(NH):
                if h % 4 == 0:
                    pe.wait_ge(sem(f"w_att{4 + h // 4}"), at(f"w_att{4 + h // 4}", 16))
                if h - 1 > 0:
                    pe.wait_ge(sem("qz0"), at("qz0", h - 1))
                if h - 1 > 0:
                    pe.wait_ge(sem("qz1"), at("qz1", h - 1))
                w = RG(4096 * (4 + h // 4), 4096).rearrange("p (k n) -> p k n", k=KD)
                for k in range(KD):
                    mm = all_tokens(pe, 2 * (h % 2), w[:, k, 128 * (h % 4):128 * (h % 4) + 128], xqT, k)
                mm.then_inc(sem("q_mm"), 1)

            def scores(u):
                h, i = UNITS[u]
                if 2 * (u - 1) > 0:
                    pe.wait_ge(sem("scored"), at("scored", 2 * (u - 1)))
                for c in range(2):
                    mm = pe.matmul(ps[2 * (u % 2) + c][:, 0:128 * (i + 1)], qz[c][:, h, 128 * i:128 * i + 128], kT[:, h, 0:128 * (i + 1)], start=True, stop=True)
                mm.then_inc(sem("s_mm"), 1)
            pe.wait_ge(sem("qz0"), at("qz0", NH))
            pe.wait_ge(sem("qz1"), at("qz1", NH))
            pe.wait_ge(sem("k_rows"), at("k_rows", 2 * NT))
            scores(0)
            scores(1)

            def turn_weights(u):
                h, i = UNITS[u]
                pe.wait_ge(sem("weights"), at("weights", u + 1))
                if u - 1 > 0:
                    pe.wait_ge(sem("aT"), at("aT", u - 1))
                for b in range(i + 1):
                    mm = pe.transpose(ps[4 + u % 2][:, 128 * b:128 * b + 128], tbuf[:, u % 2, 0, 128 * b:128 * b + 128], ident)
                mm.then_inc(sem("a_turned"), 1)

            def output(u):
                h, i = UNITS[u]
                pe.wait_ge(sem("aT"), at("aT", u + 1))
                if u - 1 > 0:
                    pe.wait_ge(sem("o_rows"), at("o_rows", u - 1))
                for b in range(i + 1):
                    mm = pe.matmul(ps[6 + u % 2][:, 0:128], aT[:, u % 2, 128 * b:128 * b + 128], vtok[:, b, 128 * h:128 * h + 128], start=(b == 0), stop=(b == i))
                mm.then_inc(sem("o_mm"), 1)
            for u in range(len(UNITS) + 1):
                if u + 2 < len(UNITS):
                    scores(u + 2)
                if u < len(UNITS):
                    turn_weights(u)
                if u:
                    output(u - 1)
            pe.wait_ge(sem("o_rows"), at("o_rows", len(UNITS)))

            def page_turned(g):
                pe.wait_ge(sem(f"kpage{g % 4}"), at(f"kpage{g % 4}", 16 * (g // 4 + 1)))
                for b in range(2):
                    if g > 0:
                        pe.wait_ge(sem(f"kp{b}"), at(f"kp{b}", g))
                    for h in range(4):
                        c0 = 128 * (4 * b + h)
                        mm = pe.transpose(ps[b][:, 128 * h:128 * h + 128], kring[:, g % 4, c0:c0 + 128], ident)
                    mm.then_inc(sem("kturned_half"), 1) if b == 0 else mm.then_inc(sem("kturned"), 1)

            def page_scores(n, heads):
                pair, p = divmod(n, NPAGE)
                c0 = 128 * (p % 4)
                for h in heads:
                    for j in range(2):
                        mm = pe.matmul(ps[4 + p // 4][64 * j:64 * j + 64, c0:c0 + 128], qdec[:, 2 * pair + j, h, :], kp[n % 2][j][:, h, :], start=(h == 0), stop=(h == NH - 1))
                return mm

            def unit(n):
                for j in range(2):
                    if n < N_UNITS:
                        page_turned(2 * n + j)
                    if n:
                        if j == 0:
                            for b in range(2):
                                if 2 * n > 0:
                                    pe.wait_ge(sem(f"kp{b}"), at(f"kp{b}", 2 * n))
                            pair, p = divmod(n - 1, NPAGE)
                            if 3 * (pair - 1) + (1 if p < 4 else 2) > 0:
                                pe.wait_ge(sem("dscored"), at("dscored", 3 * (pair - 1) + (1 if p < 4 else 2)))
                        mm = page_scores(n - 1, range(4 * j, 4 * j + 4))
                if n:
                    mm.then_inc(sem("dec_scores"), 1)

            def new_scores(pair):
                if 3 * pair > 0:
                    pe.wait_ge(sem("dscored"), at("dscored", 3 * pair))
                for h in range(NH):
                    for j in range(2):
                        mm = pe.matmul(ps[6][64 * j:64 * j + 64, 0:NDEC], qdec[:, 2 * pair + j, h, :], kT[:, h, SEQ:NTOK], start=(h == 0), stop=(h == NH - 1))
                mm.then_inc(sem("new_scores"), 1)

            def pair_turned(pair):
                pe.wait_ge(sem("combs"), at("combs", pair + 1))
                if pair > 0:
                    pe.wait_ge(sem("aTd"), at("aTd", pair))
                if pair == 3:
                    pe.wait_ge(sem("odec"), at("odec", 1))
                for kk in range(NPAGE):
                    mm = pe.matmul(ps[7][:, 64 * kk:64 * kk + 64], tdec[:, pair % 2, 128 * kk:128 * kk + 128], asm_["combs"], start=True, stop=True)
                mm = pe.matmul(ps[6][0:NDEC, 64:128], tdec[:, pair % 2, PAST:NKEY], asm_["combs"], start=True, stop=True)
                mm.then_inc(sem("dT"), 1)

            def values_step(quad, p):
                if p == 0:
                    pe.wait_ge(sem("aTd"), at("aTd", 2 * (quad + 1)))
                    if 2 * quad > 0:
                        pe.wait_ge(sem("headed"), at("headed", 2 * quad))
                if p < NPAGE:
                    pe.wait_ge(sem(f"vpage{p % 2}"), at(f"vpage{p % 2}", 64 * (4 * quad + p // 2 + 1)))
                for c in range(2):
                    for j in range(4):
                        if p < NPAGE:
                            mm = pe.matmul(ps[2 + c][32 * j:32 * j + 32, :], aTd(quad, p)[:, 32 * j:32 * j + 32], vring[:, 4 * (p % 2) + j, 512 * c:512 * c + 512], start=(p == 0), stop=False)
                        else:
                            mm = pe.matmul(ps[2 + c][32 * j:32 * j + 32, :], aTd(quad, p)[0:NDEC, 32 * j:32 * j + 32], vtok[0:NDEC, 4, 512 * c:512 * c + 512], start=False, stop=True, tile_position=(0, 32 * j))
                mm.then_inc(sem("pv_mm" if p < NPAGE else "pv_all"), 1)

            def quad_turned(quad):
                pe.wait_ge(sem("orn"), at("orn", quad + 1))
                if 3 + quad > 0:
                    pe.wait_ge(sem("aTd"), at("aTd", 3 + quad))
                pe.transpose(ps[7][:, 0:128], asm_["orn"], ident).then_inc(sem("orn_t"), 1)
            new_scores(0)
            for n in range(N_UNITS + 1):
                unit(n)
                pair, p = divmod(n - LAG - NPAGE, NPAGE)
                if p == 0 and 0 <= pair < 3:
                    new_scores(pair + 1)
                    pair_turned(pair)
                if 0 <= n - FIRST_VALUES <= NPAGE:
                    values_step(0, n - FIRST_VALUES)
                if n == QUAD0_VALUED + 2:
                    quad_turned(0)
            turn_pe(pe, "o", otok, 4, dec=False, turn=TURN_O)
            pair_turned(3)
            for p in range(NPAGE + 1):
                values_step(1, p)
            quad_turned(1)
            pe.wait_ge(sem("odec"), at("odec", 2))
            wait_turned(pe, "o", dec=False)
            for c in range(2):
                pe.wait_ge(sem(f"w_o{c}"), at(f"w_o{c}", 16))
            rows_out(pe, "wo", oT, [RG(4096 * c, 4096).rearrange("p (k n) -> p k n", k=KD) for c in range(2)], dec=odec)

        def attention_act(act):
            for i in range(NT):
                act.wait_ge(sem("collected@0"), at("collected@0", i + 1))
                row_squares(act, "kv", i)
            row_roots(act, "kv")
            turned_act(act, "kv", [(xT, P("g_kv")), (xqT, P("g_mix1"))])
            for h in range(NH):
                act.wait_ge(sem("k_mm"), at("k_mm", h + 1))
                act.copy(halves(kT[:, h, :]), two_banks(4 + 2 * (h % 2))).then_inc(sem("kT"), 1)
            for n in range(2 * NT):
                i, b = n // 2, n % 2
                act.wait_ge(sem("k_back"), at("k_back", n + 1))
                if b == 0 and i >= 2:
                    if 16 * (i // 2) > 0:
                        act.wait_ge(sem(f"k_out{i % 2}"), at(f"k_out{i % 2}", 16 * (i // 2)))
                act.copy(ktk[0:ROWS[i], i % 2, 512 * b:512 * b + 512], ps[4 + n % 4][0:ROWS[i], :]).then_inc(sem("k_rows"), 1)
            act.wait_ge(sem("qzero"), at("qzero", 3))
            for h in range(NH):
                act.wait_ge(sem("q_mm"), at("q_mm", h + 1))
                act.activation(qdec[0:64, :, h, 4 * h:4 * h + 4], ps[2 * (h % 2) + 1][0:64, SEQ - HTOK:HTOK].rearrange("p (s t) -> p s t", s=NSEQ), ACT.Copy, scale=HD ** -0.5)
                for c, (t0, t1) in enumerate(((0, HTOK), (HTOK, SEQ))):
                    i = act.activation(qz[0][0:64, h, t0:t1], ps[2 * (h % 2) + c][0:64, 0:t1 - t0], ACT.Copy, scale=HD ** -0.5)
                i.then_inc(sem("qz0"), 1)
            act.wait_ge(sem("lam_sum"), at("lam_sum", 1))
            act.activation(asm_["lam"][:, 2:4], asm_["lam"][:, 0:2], ACT.Exp).then_inc(sem("lam_exp"), 1)

            def exps(u):
                h, i = UNITS[u]
                act.wait_ge(sem("negmax"), at("negmax", u + 1))
                for c in range(2):
                    x = 2 * (u % 2) + c
                    t = tbuf[:, u % 2, c, 0:128 * (i + 1)]
                    act.activation(t, t, ACT.Exp, bias=asm_["nm"][:, x:x + 1], accum_out=asm_["sums"][:, x:x + 1]).then_inc(sem("exps"), 1)

            def square(u):
                h, i = UNITS[u]
                act.wait_ge(sem("o_rows"), at("o_rows", u + 1))
                if u - 7 > 0:
                    act.wait_ge(sem("oss"), at("oss", u - 7))
                act.activation(junk[:, 128 * (u % 8):128 * (u % 8) + 128], otok[:, i, 128 * h:128 * h + 128], ACT.Square,
                               accum_out=asm_["oss"][:, 8 * i + h:8 * i + h + 1]).then_inc(sem("oss"), 1)
            exps(0)
            for u, (h, i) in enumerate(UNITS):
                if u + 1 < len(UNITS):
                    exps(u + 1)
                act.wait_ge(sem("a_turned"), at("a_turned", u + 1))
                if u - 1 > 0:
                    act.wait_ge(sem("o_mm"), at("o_mm", u - 1))
                act.copy(aT[:, u % 2, 0:128 * (i + 1)], ps[4 + u % 2][:, 0:128 * (i + 1)]).then_inc(sem("aT"), 1)
                if u >= 3:
                    square(u - 3)
            for u in range(len(UNITS) - 3, len(UNITS)):
                square(u)
            act.wait_ge(sem("oms"), at("oms", 1))
            act.activation(asm_["osd"], asm_["oms"], ACT.Sqrt).then_inc(sem("osd"), 1)
            def exp_pair(pair):
                act.wait_ge(sem("dnm"), at("dnm", pair + 1))
                t = tdec[:, pair % 2, :]
                act.activation(t, t, ACT.Exp, bias=asm_["dnm"], accum_out=asm_["dsum"]).then_inc(sem("dexp"), 1)

            def turned_weights(pair):
                act.wait_ge(sem("dT"), at("dT", pair + 1))
                cols = slice(64 * (pair % 2), 64 * (pair % 2) + 64)
                groups = ps[7][:, :].rearrange("p (g r) -> p g r", g=NPAGE)
                if pair < 2:
                    act.copy(aTd0[:, 0:NPAGE, cols], groups)
                else:
                    act.copy(aTd1[:, 0:2, :, cols], groups[:, 0:6, :].rearrange("p (h g) r -> p h g r", h=2))
                    act.copy(aTd1[:, 2, 0:2, cols], groups[:, 6:NPAGE, :])
                act.copy(aTd(pair // 2, NPAGE)[0:NDEC, cols], ps[6][0:NDEC, 64:128]).then_inc(sem("aTd"), 1)

            def root(quad):
                act.wait_ge(sem("rms_row"), at("rms_row", quad + 1))
                act.activation(asm_["rsd"], asm_["rms"], ACT.Sqrt).then_inc(sem("rsd"), 1)
            for n in range(N_UNITS):
                for j in range(2):
                    act.wait_ge(sem("kturned"), at("kturned", 2 * n + j + 1))
                    if n - 1 > 0:
                        act.wait_ge(sem("dec_scores"), at("dec_scores", n - 1))
                    act.copy(kp[n % 2][j][:, 4:8, :], ps[1][:, :].rearrange("p (h n) -> p h n", h=4)).then_inc(sem("kp1"), 1)
                pair, p = divmod(n - NPAGE, NPAGE)
                if pair >= 0 and p == 1:
                    exp_pair(pair)
                if pair >= 0 and p == LAG + 1:
                    turned_weights(pair)
                if n == QUAD0_VALUED + 1:
                    root(0)
            exp_pair(3)
            turned_act(act, "o", [(oT, asm_["osc"])], dec=False, turn=TURN_O)
            turned_weights(3)
            root(1)

        def attention_dve(v):
            norm_stats(v, "kv")
            v.wait_ge(sem("rows_out@0"), at("rows_out@0", 32))
            norm_rows(v, "kv")
            lv = P("lams").rearrange("p (b c d) -> p b c d", b=2, c=2)
            for b in range(2):
                link(v, v.tensor_tensor(junk[:, 64 * b:64 * b + 64], lv[:, b, 0, :], lv[:, b, 1, :], ALU.mult))
                i = v.tensor_reduce(asm_["lam"][:, b:b + 1], junk[:, 64 * b:64 * b + 64], AX.X, ALU.add)
                if b == 0:
                    link(v, i)
            i.then_inc(sem("lam_sum"), 1)
            for h in range(NH):
                i = v.tensor_scalar(asm_["osc"][:, h:h + 1], P("subln"), 1.0 - LAM_INIT, None, ALU.mult)
            link(v, i)
            turned_dve(v, "kv", [(xT, P("g_kv")), (xqT, P("g_mix1"))])
            n = 0
            v.wait_ge(sem("t_kv"), at("t_kv", KD + 1))
            for i in range(NT):
                for c in range(2):
                    v.wait_ge(sem("v_mm"), at("v_mm", n + 1))
                    v.tensor_copy(vtok[0:ROWS[i], i, 512 * c:512 * c + 512], ps[n % 4][0:ROWS[i], :]).then_inc(sem("v_done"), 1)
                    n += 1
            v.wait_ge(sem("qzero"), at("qzero", 3))
            for h in range(NH):
                v.wait_ge(sem("q_mm"), at("q_mm", h + 1))
                b0 = 2 * (h % 2)
                v.tensor_scalar(qdec[64:128, :, h, 32 + 4 * h:36 + 4 * h], ps[b0 + 1][64:128, SEQ - HTOK:HTOK].rearrange("p (s t) -> p s t", s=NSEQ), HD ** -0.5, None, ALU.mult)
                for c, (t0, t1) in enumerate(((0, HTOK), (HTOK, SEQ))):
                    i = v.tensor_scalar(qz[1][64:128, h, t0:t1], ps[b0 + c][64:128, 0:t1 - t0], HD ** -0.5, None, ALU.mult)
                i.then_inc(sem("qz1"), 1)
            v.wait_ge(sem("lam_exp"), at("lam_exp", 1))
            link(v, v.tensor_tensor(asm_["lam"][:, 0:1], asm_["lam"][:, 3:4], asm_["lam"][:, 2:3], ALU.subtract))
            link(v, v.tensor_scalar(asm_["nlam"], asm_["lam"][:, 0:1], -LAM_INIT, None, ALU.add))
            link(v, v.scalar_tensor_tensor(asm_["isc"], C("isc1"), asm_["nlam"], C("isc0"), ALU.mult, ALU.add))
            for b in range(2):
                v.wait_ge(sem(f"k_out{b}"), at(f"k_out{b}", (48, 32)[b]))

            def score(u):
                h, i = UNITS[u]
                v.wait_ge(sem("s_mm"), at("s_mm", u + 1))
                v.wait_ge(sem("biash"), at("biash", h + 1))
                if u - 1 > 0:
                    v.wait_ge(sem("a_turned"), at("a_turned", u - 1))
                n = 128 * (i + 1)
                for c in range(2):
                    x = 2 * (u % 2) + c
                    v.tensor_tensor_reduce(tbuf[:, u % 2, c, 0:n], ps[x][:, 0:n], biash[:, h % 2, 384 - 128 * i:384 - 128 * i + n], 1.0, -3e38,
                                           ALU.add, ALU.max, asm_["mx"][:, x:x + 1]).then_inc(sem("scored"), 1)
                v.wait_ge(sem("scored"), at("scored", 2 * (u + 1)))
                x = 2 * (u % 2)
                v.tensor_scalar(asm_["nm"][:, x:x + 2], asm_["mx"][:, x:x + 2], -1.0, None, ALU.mult).then_inc(sem("negmax"), 1)

            def weights(u):
                h, i = UNITS[u]
                n = 128 * (i + 1)
                x = 2 * (u % 2)
                v.wait_ge(sem("exps"), at("exps", 2 * (u + 1)))
                link(v, v.reciprocal(asm_["rec"][:, x:x + 2], asm_["sums"][:, x:x + 2]))
                link(v, v.tensor_tensor(asm_["rl"][:, x:x + 1], asm_["rec"][:, x + 1:x + 2], asm_["nlam"], ALU.mult))
                t0, t1 = tbuf[:, u % 2, 0, 0:n], tbuf[:, u % 2, 1, 0:n]
                link(v, v.tensor_scalar(t1, t1, asm_["rl"][:, x:x + 1], None, ALU.mult))
                v.scalar_tensor_tensor(t0, t0, asm_["rec"][:, x:x + 1], t1, ALU.mult, ALU.add).then_inc(sem("weights"), 1)

            def o_rows(u):
                h, i = UNITS[u]
                v.wait_ge(sem("o_mm"), at("o_mm", u + 1))
                v.tensor_copy(otok[:, i, 128 * h:128 * h + 128], ps[6 + u % 2][:, 0:128]).then_inc(sem("o_rows"), 1)
            score(0)
            for u in range(len(UNITS)):
                if u + 1 < len(UNITS):
                    score(u + 1)
                weights(u)
                if u >= 2:
                    o_rows(u - 2)
            o_rows(len(UNITS) - 2)
            o_rows(len(UNITS) - 1)
            v.wait_ge(sem("o_rows"), at("o_rows", len(UNITS)))
            v.sem_inc(sem("prompt_done"), 1)
            v.wait_ge(sem("oss"), at("oss", len(UNITS)))
            v.tensor_scalar(asm_["oms"], asm_["oss"], 1.0 / 128, EPS, ALU.mult, ALU.add).then_inc(sem("oms"), 1)
            v.wait_ge(sem("osd"), at("osd", 1))
            link(v, v.reciprocal(asm_["orstd"], asm_["osd"]))
            for i in range(4):
                head_ = otok[:, i, :].rearrange("p (h e) -> p h e", h=NH)
                v.tensor_tensor(head_, head_, asm_["orstd"][:, 8 * i:8 * i + 8].unsqueeze(2).broadcast_to([128, NH, 128]), ALU.mult).then_inc(sem("xh_o"), 1)
            v.wait_ge(sem("past_in"), at("past_in", 16))

            def biased(pair, dst, bank, bias, x):
                v.tensor_tensor_reduce(dst, bank, bias, 1.0, -3e38, ALU.add, ALU.max, asm_["dmx"][:, x:x + 1]).then_inc(sem("dscored"), 1)

            def first_half(pair):
                v.wait_ge(sem("dec_scores"), at("dec_scores", NPAGE * pair + 4))
                if pair - 1 > 0:
                    v.wait_ge(sem("dT"), at("dT", pair - 1))
                biased(pair, tdec[:, pair % 2, 0:512], ps[4][:, :], pastb[:, 0:512], 0)

            def pair_weights(pair):
                v.wait_ge(sem("dec_scores"), at("dec_scores", NPAGE * (pair + 1)))
                biased(pair, tdec[:, pair % 2, 512:PAST], ps[5][:, :], pastb[:, 512:PAST], 1)
                v.wait_ge(sem("new_scores"), at("new_scores", pair + 1))
                biased(pair, tdec[:, pair % 2, PAST:NKEY], ps[6][:, 0:NDEC], C("newbias")[:, NDEC * pair:NDEC * pair + NDEC], 2)
                v.wait_ge(sem("dscored"), at("dscored", 3 * (pair + 1)))
                link(v, v.tensor_reduce(asm_["dm"], asm_["dmx"], AX.X, ALU.max))
                v.tensor_scalar(asm_["dnm"], asm_["dm"], -1.0, None, ALU.mult).then_inc(sem("dnm"), 1)
                v.wait_ge(sem("dexp"), at("dexp", pair + 1))
                link(v, v.reciprocal(asm_["drec"], asm_["dsum"]))
                link(v, v.tensor_tensor(asm_["drsc"], asm_["drec"], asm_["isc"], ALU.mult))
                if pair > 0:
                    v.wait_ge(sem("dT"), at("dT", pair))
                v.tensor_scalar(asm_["combs"], C("comb"), asm_["drsc"], None, ALU.mult).then_inc(sem("combs"), 1)

            def own_heads(quad):
                v.wait_ge(sem("pv_all"), at("pv_all", quad + 1))
                hmk = C("headmask")
                for c in range(2):
                    v.tensor_tensor(junk[:, 512 * c:512 * c + 512].rearrange("p (h e) -> p h e", h=4), ps[2 + c][:, :].rearrange("p (h e) -> p h e", h=4),
                                    hmk[:, 4 * c:4 * c + 4].unsqueeze(2).broadcast_to([128, 4, 128]), ALU.mult).then_inc(sem("headed"), 1)
                v.wait_ge(sem("headed"), at("headed", 2 * (quad + 1)))
                link(v, v.tensor_reduce(orow, junk[:, :].rearrange("p (h e) -> p e h", h=NH), AX.X, ALU.add))
                link(v, v.tensor_tensor(junk[:, 0:128], orow, orow, ALU.mult))
                link(v, v.tensor_reduce(asm_["rss"], junk[:, 0:128], AX.X, ALU.add))
                v.tensor_scalar(asm_["rms"], asm_["rss"], 1.0 / 128, EPS, ALU.mult, ALU.add).then_inc(sem("rms_row"), 1)

            def head_norm(quad):
                v.wait_ge(sem("rsd"), at("rsd", quad + 1))
                link(v, v.reciprocal(asm_["rrs"], asm_["rsd"]))
                v.tensor_scalar(asm_["orn"], orow, asm_["rrs"], None, ALU.mult).then_inc(sem("orn"), 1)

            def features(quad):
                v.wait_ge(sem("orn_t"), at("orn_t", quad + 1))
                dst = odec[:, :, 16 * quad:16 * quad + 16].rearrange("p h (s t) -> p s h t", s=4)
                for s in range(4):
                    i = v.tensor_scalar(dst[:, s, :, :], ps[7][:, 32 * s:32 * s + 32].rearrange("p (h t) -> p h t", h=NH), asm_["osc"][:, 0:1], None, ALU.mult)
                i.then_inc(sem("odec"), 1)
            for n in range(N_UNITS):
                for j in range(2):
                    v.wait_ge(sem("kturned_half"), at("kturned_half", 2 * n + j + 1))
                    if n - 1 > 0:
                        v.wait_ge(sem("dec_scores"), at("dec_scores", n - 1))
                    v.tensor_copy(kp[n % 2][j][:, 0:4, :], ps[0][:, :].rearrange("p (h n) -> p h n", h=4)).then_inc(sem("kp0"), 1)
                pair, p = divmod(n, NPAGE)
                if p == 5:
                    first_half(pair)
                if p == 1 and pair > 0:
                    pair_weights(pair - 1)
                if n == QUAD0_VALUED:
                    own_heads(0)
                if n == QUAD0_VALUED + 1:
                    head_norm(0)
                if n == QUAD0_VALUED + 3:
                    features(0)
            pair_weights(3)
            turned_dve(v, "o", [(oT, asm_["osc"])], dec=False, turn=TURN_O)
            own_heads(1)
            head_norm(1)
            features(1)
            rows_added(v, "wo")
            v.wait_ge(sem("wo_add"), at("wo_add", 2 * NT))

        def att_chunk(sp, c):
            wkv = a["w_kv"].rearrange("(k p) n -> p k n", p=128)
            wq = a["attn_w_q"][0].rearrange("(k p) n -> p k n", p=128)
            src = wkv[:, :, 512 * c:512 * c + 512] if c < 4 else wq[:, :, 512 * (c - 4):512 * (c - 3)]
            sp.dma_start(RG(4096 * c, 4096).rearrange("p (k n) -> p k n", k=KD), src).then_inc(sem(f"w_att{c}"), 16)

        def attention_first_loads(sp):
            for c in range(3):
                if NE - 3 + (c > 0) > 0:
                    sp.wait_ge(sem("down@0"), at("down@0", NE - 3 + (c > 0)))
                att_chunk(sp, c)

        def attention_loads(sp):
            sp.wait_ge(sem("collected@0"), at("collected@0", NT))
            for c in range(3, 6):
                att_chunk(sp, c)
            for i in range(NT):
                sp.wait_ge(sem("v_done"), at("v_done", 2 * (i + 1)))
                if i < 4:
                    sp.dma_start(o["v_prompt"][0, 128 * i:128 * i + 128].rearrange("p h e -> p (h e)"), vtok[:, i, :]).then_inc(out_sem, 16)
                else:
                    sp.dma_start(o["v_sample"].rearrange("s t h e -> (s t) (h e)"), vtok[0:NDEC, 4, :]).then_inc(out_sem, 16)
            for i in range(NT):
                sp.wait_ge(sem("k_rows"), at("k_rows", 2 * (i + 1)))
                n = ROWS[i]
                src = ktk[:, i % 2, :]
                if i < 4:
                    sp.dma_start(o["k_prompt"][0, 128 * i:128 * i + 128].rearrange("p h c d -> p (h c d)"), src).then_inc(sem(f"k_out{i % 2}"), 16)
                else:
                    sp.dma_start(o["k_sample"].rearrange("s t h c d -> (s t) (h c d)"), src[0:n, :]).then_inc(sem(f"k_out{i % 2}"), 16)
            n_out[0] += 16 * NT
            sp.wait_ge(sem("q_mm"), at("q_mm", NH))
            sp.dma_start(dist, a["c_dist"]).then_inc(sem("dist_in"), 16)
            sp.wait_ge(sem("pages_in"), at("pages_in", 16))
            sp.dma_start(pastb, a["c_past"]).then_inc(sem("past_in"), 16)
            ck = a["cache_k"].rearrange("n p h c d -> n p (h c d)")
            cvv = a["cache_v"].rearrange("n p h e -> n p (h e)")
            n_pool = a["cache_k"].shape[0]

            def page_in(src, dst, entry, s):
                reg = sp.value_load(pages[0:1, entry], min_val=0, max_val=n_pool - 1)
                sp.dma_start(dst, src[bass.ds(reg, 1)].rearrange("a p d -> p (a d)")).then_inc(s, 16)

            for u in range(4):
                page_in(ck, kring[:, u, :], slice(u, u + 1), sem(f"kpage{u}"))

            def key_groups(first, end):
                with sp.Fori(first, end) as g:
                    for u in range(4):
                        sp.wait_ge(sem("kturned"), at("kturned", 4 * g + (u - 3)))
                        page_in(ck, kring[:, u, :], bass.ds(4 * g + u, 1), sem(f"kpage{u}"))

            def values_in(n):
                if n - 1 > 0:
                    sp.wait_ge(sem("pv_mm"), at("pv_mm", n - 1))
                for j in range(4):
                    entry = NSEQ * NPAGE + 4 * n + j
                    page_in(cvv, vring[:, 4 * (n % 2) + j, :], slice(entry, entry + 1), sem(f"vpage{n % 2}"))
            key_groups(1, 6)
            sp.wait_ge(sem("prompt_done"), at("prompt_done", 1))
            values_in(0)
            key_groups(6, 8)
            values_in(1)
            key_groups(8, 11)
            for g in range(11, 16):
                for q in (2 * (g - 11), 2 * (g - 11) + 1):
                    if q < NPAGE:
                        values_in(q + 2)
                key_groups(g, g + 1)
            wo = a["attn_w_o"][0].rearrange("(k p) n -> p k n", p=128)
            for c in (1, 0):
                if c == 0:
                    sp.wait_ge(sem("dec_scores"), at("dec_scores", N_UNITS))
                sp.dma_start(RG(4096 * c, 4096).rearrange("p (k n) -> p k n", k=KD), wo[:, :, 512 * c:512 * c + 512]).then_inc(sem(f"w_o{c}"), 16)
            for n in range(10, 16):
                values_in(n)

        def prompt_bias(pool):
            pool.wait_ge(sem("dist_in"), at("dist_in", 16))
            for h in range(NH):
                if 8 * (h - 1) > 0:
                    pool.wait_ge(sem("scored"), at("scored", 8 * (h - 1)))
                pool.tensor_scalar(biash[:, h % 2, :], dist, 2.0 ** -(h + 1), None, ALU.mult).then_inc(sem("biash"), 1)

        def row_squares(act, tag, i):
            n = ROWS[i]
            act.activation(junk[0:n, :], resid[0:n, i, :], ACT.Square, accum_out=stat["ss"][0:n, i:i + 1]).then_inc(sem(f"ss_{tag}"), 1)
            act.wait_ge(sem(f"ss_{tag}"), at(f"ss_{tag}", i + 1))

        def row_roots(act, tag):
            act.wait_ge(sem(f"ms_{tag}"), at(f"ms_{tag}", 1))
            act.activation(stat["sd"], stat["ms"], ACT.Sqrt).then_inc(sem(f"sd_{tag}"), 1)

        def norm_stats(v, tag):
            v.wait_ge(sem(f"ss_{tag}"), at(f"ss_{tag}", NT))
            v.tensor_scalar(stat["ms"], stat["ss"], 1.0 / D, EPS, ALU.mult, ALU.add).then_inc(sem(f"ms_{tag}"), 1)
            v.wait_ge(sem(f"sd_{tag}"), at(f"sd_{tag}", 1))
            link(v, v.reciprocal(stat["rstd"], stat["sd"]))

        def norm_rows(v, tag):
            for i in range(NT):
                n = ROWS[i]
                v.tensor_scalar(xhat[0:n, i, :], resid[0:n, i, :], stat["rstd"][0:n, i:i + 1], None, ALU.mult).then_inc(sem(f"xh_{tag}"), 1)

        TURN, TURN_O = (0, 1, 4, 5), (0, 1)

        def turn_pe(pe, tag, src, tiles, dec=True, turn=TURN, turned=None):
            pe.wait_ge(sem(f"xh_{tag}"), at(f"xh_{tag}", tiles))
            if dec:
                for k in range(KD):
                    mm = pe.transpose(ps[2][:, NDEC * k:NDEC * k + NDEC], src[0:NDEC, 4, 128 * k:128 * k + 128], ident[0:NDEC, 0:NDEC])
                mm.then_inc(sem(f"t_{tag}"), 1)
            for k in range(KD + 2):
                if k < KD:
                    if k >= len(turn):
                        if (k - len(turn)) // 2 + 1 + (dec and k % 2 == 0) > 0:
                            pe.wait_ge(sem(f"ev{k % 2}_{tag}"), at(f"ev{k % 2}_{tag}", (k - len(turn)) // 2 + 1 + (dec and k % 2 == 0)))
                    for i in range(4):
                        mm = pe.transpose(ps[turn[k % len(turn)]][:, 128 * i:128 * i + 128], src[:, i, 128 * k:128 * k + 128], ident)
                    mm.then_inc(sem(f"t_{tag}"), 1)
                if turned and k >= 2:
                    if (k - 2) // 2 + 1 + (dec and k % 2 == 0) > 0:
                        pe.wait_ge(sem(f"ev{k % 2}_{tag}"), at(f"ev{k % 2}_{tag}", (k - 2) // 2 + 1 + (dec and k % 2 == 0)))
                    turned(k - 2)

        def turned_act(act, tag, outs, dec=True, turn=TURN):
            for k in range(1, KD, 2):
                act.wait_ge(sem(f"t_{tag}"), at(f"t_{tag}", k + 1 + dec))
                for dst, g in outs:
                    i = act.activation(dst[:, k, 0:SEQ], ps[turn[k % len(turn)]], ACT.Copy, scale=g[:, k:k + 1])
                i.then_inc(sem(f"ev1_{tag}"), 1)

        def turned_dve(v, tag, outs, dec=True, turn=TURN):
            if dec:
                v.wait_ge(sem(f"t_{tag}"), at(f"t_{tag}", 1))
                for dst, g in outs:
                    i = v.tensor_tensor(dst[:, :, SEQ:NTOK], ps[2][:, 0:KD * NDEC].rearrange("p (k t) -> p k t", k=KD),
                                        g[:, 0:KD].unsqueeze(2).broadcast_to([128, KD, NDEC]), ALU.mult)
                i.then_inc(sem(f"ev0_{tag}"), 1)
            for k in range(0, KD, 2):
                v.wait_ge(sem(f"t_{tag}"), at(f"t_{tag}", k + 1 + dec))
                for dst, g in outs:
                    i = v.tensor_scalar(dst[:, k, 0:SEQ], ps[turn[k % len(turn)]], g[:, k:k + 1], None, ALU.mult)
                i.then_inc(sem(f"ev0_{tag}"), 1)

        def wait_turned(eng, tag, dec=True):
            eng.wait_ge(sem(f"ev0_{tag}"), at(f"ev0_{tag}", KD // 2 + dec))
            eng.wait_ge(sem(f"ev1_{tag}"), at(f"ev1_{tag}", KD // 2))

        chain = [0]

        def link(v, ins):
            chain[0] += 1
            ins.then_inc(sem("dve_chain"), 1)
            v.wait_ge(sem("dve_chain"), at("dve_chain", chain[0]))

        def rows_out(pe, tag, src, w, dec=None):
            n = 0
            for i in range(NT):
                for c in range(2):
                    if n >= 4:
                        if n - 3 > 0:
                            pe.wait_ge(sem(f"{tag}_add"), at(f"{tag}_add", n - 3))
                    for k in range(KD):
                        lhs = dec[:, k, :] if (dec is not None and i == 4) else src[:, k, 128 * i:128 * i + ROWS[i]]
                        mm = pe.matmul(ps[2 + n % 4][0:ROWS[i], :], lhs, w[c][:, k, :], start=(k == 0), stop=(k == KD - 1))
                    mm.then_inc(sem(f"{tag}_mm"), 1)
                    n += 1

        def rows_added(v, tag):
            n = 0
            for i in range(NT):
                for c in range(2):
                    v.wait_ge(sem(f"{tag}_mm"), at(f"{tag}_mm", n + 1))
                    res = resid[0:ROWS[i], i, 512 * c:512 * c + 512]
                    v.tensor_tensor(res, ps[2 + n % 4][0:ROWS[i], :], res, ALU.add).then_inc(sem(f"{tag}_add"), 1)
                    n += 1

        def all_tokens(pe, b, w, x, k):
            for c in range(2):
                mm = pe.matmul(ps[b + c][:, 0:HTOK], w, x[:, k, HTOK * c:HTOK * c + HTOK], start=(k == 0), stop=(k == KD - 1))
            return mm

        def moe_pe(pe, l):
            wr = P(f"wr{l}").rearrange("p (k n) -> p k n", k=KD)

            def logits(k):
                for i in (0, 4, 1, 2, 3):
                    mm = pe.matmul(ps[3][0:ROWS[i], 20 * i:20 * i + 20], xT[:, k, 128 * i:128 * i + ROWS[i]], wr[:, k, :], start=(k == 0 and i == 0), stop=(k == KD - 1 and i == 3))
                if k == KD - 1:
                    mm.then_inc(sem(f"logits@{l}"), 1)
            turn_pe(pe, f"ffn{l}", xhat, NT, turned=logits)
            pe.wait_ge(sem(f"chosen@{l}"), at(f"chosen@{l}", 1))
            for i in range(NT):
                for q in range(i + 1):
                    n = ROWS[q]
                    mm = pe.matmul(ps[4][0:ROWS[i], NE * i:NE * i + NE], count[0:n, int(q < i), 0:ROWS[i]], chosen[0:n, q, :], start=(q == 0), stop=(q == i))
            for q in range(NT):
                mm = pe.matmul(ps[4][:, NE * NT:NE * NT + NE], count[0:ROWS[q], 1, :], chosen[0:ROWS[q], q, :], start=(q == 0), stop=(q == NT - 1))
            mm.then_inc(sem(f"ranks@{l}"), 1)

            def turn(e, par_, half):
                pe.wait_ge(sem(f"xg_{par_}@{l}"), at(f"xg_{par_}@{l}", 16 * (half + 1)))
                for k in range(KD):
                    mm = pe.transpose(ps[k // 4][:, 128 * (k % 4):128 * (k % 4) + 128], xg[:, par_, 128 * k:128 * k + 128], ident)
                mm.then_inc(sem(f"turned@{l}"), 1)

            def gate_up(e, slot, par_, quarter):
                pe.wait_ge(sem(f"w_moe_{slot}@{l}"), at(f"w_moe_{slot}@{l}", 48 * (quarter + 1)))
                pe.wait_ge(sem(f"xgT@{l}"), at(f"xgT@{l}", 2 * (e + 1)))
                if e - 1 > 0:
                    pe.wait_ge(sem(f"hidden@{l}"), at(f"hidden@{l}", e - 1))
                gu = RG(slot * SLOT, 4096).rearrange("p (k n) -> p k n", k=KD)
                for k in range(KD):
                    mm = pe.matmul(ps[2 + par_][:, :], xgT[:, k, :], gu[:, k, :], start=(k == 0), stop=(k == KD - 1))
                mm.then_inc(sem(f"gu@{l}"), 1)

            def hidden_turn(e, par_):
                pe.wait_ge(sem(f"hidden@{l}"), at(f"hidden@{l}", e + 1))
                for f in range(2):
                    mm = pe.transpose(ps[4][:, 128 * f:128 * f + 128], hm[:, par_, 128 * f:128 * f + 128], ident)
                mm.then_inc(sem(f"ht@{l}"), 1)

            def down(e, slot):
                pe.wait_ge(sem(f"hT@{l}"), at(f"hT@{l}", e + 1))
                if e > 0:
                    pe.wait_ge(sem(f"y_a@{l}"), at(f"y_a@{l}", e))
                if e > 0:
                    pe.wait_ge(sem(f"y_v@{l}"), at(f"y_v@{l}", e))
                dn = RG(slot * SLOT + 4096, 2048).rearrange("p (f n) -> p f n", f=2)
                for c in range(2):
                    for f in range(2):
                        mm = pe.matmul(ps[5 + c][:, :], hT[:, f, :], dn[:, f, 512 * c:512 * c + 512], start=(f == 0), stop=(f == 1))
                mm.then_inc(sem(f"down@{l}"), 1)

            turn(0, 0, 0)
            gate_up(0, 0, 0, 0)
            turn(1, 1, 0)
            for e in range(1, NE):
                gate_up(e, e % 4, e % 2, e // 4)
                hidden_turn(e - 1, (e - 1) % 2)
                if e < NE - 1:
                    turn(e + 1, (e + 1) % 2, (e + 1) // 2)
                down(e - 1, (e - 1) % 4)
            hidden_turn(NE - 1, 1)
            down(NE - 1, 3)

            pe.wait_ge(sem(f"extra_tab@{l}"), at(f"extra_tab@{l}", 1))
            n_extra = pe.value_load(extra_tab[0:1, EXTRA:EXTRA + 1], min_val=0, max_val=EXTRA)
            for x in range(EXTRA):
                with pe.If(n_extra > x):
                    slot = EXTRA_SLOTS[l] + x % 2
                    gu = RG(slot * SLOT, 4096).rearrange("p (k n) -> p k n", k=KD)
                    dn = RG(slot * SLOT + 4096, 2048).rearrange("p (f n) -> p f n", f=2)
                    done = sem(f"x{l}_pe")
                    pe.wait_ge(sem(f"x{l}_rows"), at(f"x{l}_rows", 16 * (x + 1)))
                    for k in range(KD):
                        mm = pe.transpose(ps[k // 4][:, 128 * (k % 4):128 * (k % 4) + 128], xg[:, 0, 128 * k:128 * k + 128], ident)
                    mm.then_inc(done, 1)
                    pe.wait_ge(sem(f"x{l}_w{x % 2}"), at(f"x{l}_w{x % 2}", 48 * (x // 2 + 1)))
                    pe.wait_ge(sem(f"x{l}_dve"), at(f"x{l}_dve", 3 * x + 1))
                    if x == 0:
                        pe.wait_ge(sem(f"hidden@{l}"), at(f"hidden@{l}", NE))
                    for k in range(KD):
                        mm = pe.matmul(ps[2][:, :], xgT[:, k, :], gu[:, k, :], start=(k == 0), stop=(k == KD - 1))
                    mm.then_inc(done, 1)
                    pe.wait_ge(sem(f"x{l}_dve"), at(f"x{l}_dve", 3 * x + 2))
                    for f in range(2):
                        mm = pe.transpose(ps[4][:, 128 * f:128 * f + 128], hm[:, 0, 128 * f:128 * f + 128], ident)
                    mm.then_inc(done, 1)
                    pe.wait_ge(sem(f"x{l}_act"), at(f"x{l}_act", 3 * x + 2))
                    if x == 0:
                        pe.wait_ge(sem(f"y_a@{l}"), at(f"y_a@{l}", NE))
                        pe.wait_ge(sem(f"y_v@{l}"), at(f"y_v@{l}", NE))
                    else:
                        if 3 * x > 0:
                            pe.wait_ge(sem(f"x{l}_dve"), at(f"x{l}_dve", 3 * x))
                    for c in range(2):
                        for f in range(2):
                            mm = pe.matmul(ps[5 + c][:, :], hT[:, f, :], dn[:, f, 512 * c:512 * c + 512], start=(f == 0), stop=(f == 1))
                    mm.then_inc(done, 1)

        def moe_act(act, l):
            turned_act(act, f"ffn{l}", [(xT, P(f"g_ffn{l}"))])
            act.wait_ge(sem(f"gd@{l}"), at(f"gd@{l}", 1))
            act.activation(r["gex"], r["gd"], ACT.Exp).then_inc(sem(f"gex@{l}"), 1)
            act.wait_ge(sem(f"ed@{l}"), at(f"ed@{l}", 1))
            act.activation(r["eex"], r["ed"], ACT.Exp).then_inc(sem(f"eex@{l}"), 1)

            def silu(e, par_):
                act.wait_ge(sem(f"gu@{l}"), at(f"gu@{l}", e + 1))
                if e - 1 > 0:
                    act.wait_ge(sem(f"hidden@{l}"), at(f"hidden@{l}", e - 1))
                act.activation(sil[:, par_, :], ps[2 + par_][:, 0:DE], ACT.Silu).then_inc(sem(f"silu@{l}"), 1)

            def finish(e, par_):
                act.wait_ge(sem(f"ht@{l}"), at(f"ht@{l}", e + 1))
                if e > 0:
                    act.wait_ge(sem(f"down@{l}"), at(f"down@{l}", e))
                act.copy(hT[:, :, :].rearrange("p f s -> p (f s)"), ps[4][:, 0:256]).then_inc(sem(f"hT@{l}"), 1)
                act.wait_ge(sem(f"down@{l}"), at(f"down@{l}", e + 1))
                if e >= 2:
                    if 16 * (e // 2) > 0:
                        act.wait_ge(sem(f"y_out_{par_}@{l}"), at(f"y_out_{par_}@{l}", 16 * (e // 2)))
                act.copy(yrow[:, par_, 512:1024], ps[6][:, :]).then_inc(sem(f"y_a@{l}"), 1)
                act.wait_ge(sem(f"y_a@{l}"), at(f"y_a@{l}", e + 1))
                act.wait_ge(sem(f"y_v@{l}"), at(f"y_v@{l}", e + 1))
                yd = scratch["y"][0:MAIN].rearrange("(q e) d -> q e d", e=NE)
                act.dma_start(yd[0:128, e, :], yrow[:, par_, :]).then_inc(sem(f"y_out_{par_}@{l}"), 16)
            silu(0, 0)
            for e in range(1, NE):
                silu(e, e % 2)
                finish(e - 1, (e - 1) % 2)
            finish(NE - 1, 1)
            act.wait_ge(sem(f"extra_tab@{l}"), at(f"extra_tab@{l}", 1))
            n_extra = act.value_load(extra_tab[0:1, EXTRA:EXTRA + 1], min_val=0, max_val=EXTRA)
            for x in range(EXTRA):
                with act.If(n_extra > x):
                    done = sem(f"x{l}_act")
                    act.wait_ge(sem(f"x{l}_pe"), at(f"x{l}_pe", 4 * x + 2))
                    act.activation(sil[:, 0, :], ps[2][:, 0:DE], ACT.Silu).then_inc(done, 1)
                    act.wait_ge(sem(f"x{l}_pe"), at(f"x{l}_pe", 4 * x + 3))
                    act.copy(hT[:, :, :].rearrange("p f s -> p (f s)"), ps[4][:, 0:256]).then_inc(done, 1)
                    act.wait_ge(sem(f"x{l}_pe"), at(f"x{l}_pe", 4 * x + 4))
                    if x == 0:
                        act.wait_ge(sem(f"y_out_0@{l}"), at(f"y_out_0@{l}", 16 * NE // 2))
                    else:
                        if 16 * x > 0:
                            act.wait_ge(sem(f"x{l}_y"), at(f"x{l}_y", 16 * x))
                    act.copy(yrow[:, 0, 512:1024], ps[6][:, :]).then_inc(done, 1)
                    act.wait_ge(sem(f"x{l}_act"), at(f"x{l}_act", 3 * x + 3))
                    act.wait_ge(sem(f"x{l}_dve"), at(f"x{l}_dve", 3 * x + 3))
                    act.dma_start(scratch["y"][MAIN:SLOTS].rearrange("(p x) d -> p x d", p=128)[:, x, :], yrow[:, 0, :]).then_inc(sem(f"x{l}_y"), 16)

        def moe_dve(v, l):
            turned_dve(v, f"ffn{l}", [(xT, P(f"g_ffn{l}"))])
            link(v, v.memset(WK(6400, 100), 0.0))
            link(v, v.memset(r["rank"], 0.0))
            v.wait_ge(sem(f"logits@{l}"), at(f"logits@{l}", 1))
            br = P(f"br{l}")
            link(v, v.tensor_tensor(logit[:, 0:4, :], ps[3][:, 0:80].rearrange("p (i n) -> p i n", i=4),
                                    br.unsqueeze(1).broadcast_to([128, 4, 20]), ALU.add))
            link(v, v.tensor_tensor(logit[0:NDEC, 4, :], ps[3][0:NDEC, 80:100], br[0:NDEC, :], ALU.add))
            G = logit[:, :, 0:NG]
            E_ = logit[:, :, NG:].rearrange("p i (g e) -> p i e g", g=NG)
            v4 = {n: r[n].rearrange("p (i n) -> p i n", i=NT) for n in
                  ("geq", "gsel", "goh", "gd", "gex", "es", "ed", "eex", "pe", "eq1", "sel1", "oh1", "pe2", "eq2", "sel2", "oh2")}

            def b4(x):
                return x.unsqueeze(2).broadcast_to([128, NT, 4])
            rev = C("rev4").unsqueeze(1).broadcast_to([128, NT, 4])

            def first_max(vals, mx, eq, sel, smx, oh):
                link(v, v.tensor_reduce(r[mx], vals, AX.X, ALU.max))
                link(v, v.tensor_tensor(v4[eq], vals, b4(r[mx]), ALU.is_equal))
                link(v, v.tensor_tensor(v4[sel], v4[eq], rev, ALU.mult))
                link(v, v.tensor_reduce(r[smx], v4[sel], AX.X, ALU.max))
                link(v, v.tensor_tensor(v4[oh], v4[sel], b4(r[smx]), ALU.is_equal))
            first_max(G, "gmax", "geq", "gsel", "gmx", "goh")
            v.tensor_tensor(v4["gd"], G, b4(r["gmax"]), ALU.subtract).then_inc(sem(f"gd@{l}"), 1)
            et = r["etmp"].rearrange("p (i e g) -> p i e g", i=NT, e=EPG)
            link(v, v.tensor_tensor(et, E_, v4["goh"].unsqueeze(2).broadcast_to([128, NT, EPG, NG]), ALU.mult))
            link(v, v.tensor_reduce(v4["es"], et, AX.X, ALU.add))
            link(v, v.tensor_reduce(r["em"], v4["es"], AX.X, ALU.max))
            v.tensor_tensor(v4["ed"], v4["es"], b4(r["em"]), ALU.subtract).then_inc(sem(f"ed@{l}"), 1)
            v.wait_ge(sem(f"gex@{l}"), at(f"gex@{l}", 1))
            link(v, v.tensor_reduce(r["gsum"], v4["gex"], AX.X, ALU.add))
            link(v, v.reciprocal(r["pg"], r["gsum"]))
            v.wait_ge(sem(f"eex@{l}"), at(f"eex@{l}", 1))
            link(v, v.tensor_reduce(r["esum"], v4["eex"], AX.X, ALU.add))
            link(v, v.reciprocal(r["er"], r["esum"]))
            link(v, v.tensor_tensor(v4["pe"], v4["eex"], b4(r["er"]), ALU.mult))
            first_max(v4["pe"], "p1", "eq1", "sel1", "mx1", "oh1")
            link(v, v.scalar_tensor_tensor(r["pe2"], r["oh1"], -2.0, r["pe"], ALU.mult, ALU.add))
            first_max(v4["pe2"], "p2", "eq2", "sel2", "mx2", "oh2")
            for oh, full in (("oh1", "OH1"), ("oh2", "OH2")):
                link(v, v.tensor_tensor(r[full].rearrange("p (i g e) -> p i g e", i=NT, g=NG),
                                        v4["goh"].unsqueeze(3).broadcast_to([128, NT, NG, EPG]),
                                        v4[oh].unsqueeze(2).broadcast_to([128, NT, NG, EPG]), ALU.mult))
            v.tensor_tensor(chosen[:, :, :].rearrange("p i e -> p (i e)"), r["OH1"], r["OH2"], ALU.add).then_inc(sem(f"chosen@{l}"), 1)
            link(v, v.tensor_tensor(r["s12"], r["p1"], r["p2"], ALU.add))
            link(v, v.reciprocal(r["rs"], r["s12"]))
            link(v, v.tensor_tensor(r["rsg"], r["rs"], r["pg"], ALU.mult))
            v.tensor_tensor(r["gate1"], r["p1"], r["rsg"], ALU.mult)
            link(v, v.tensor_tensor(r["gate2"], r["p2"], r["rsg"], ALU.mult))
            v.wait_ge(sem(f"ranks@{l}"), at(f"ranks@{l}", 1))
            rk = r["rank"].rearrange("p (i e) -> p i e", i=NT)
            link(v, v.tensor_copy(rk[:, 0:4, :], ps[4][:, 0:64].rearrange("p (i e) -> p i e", i=4)))
            link(v, v.tensor_copy(rk[0:NDEC, 4, :], ps[4][0:NDEC, 64:80]))
            link(v, v.tensor_copy(r["cnt"], ps[4][:, 80:96]))
            a_, b_ = r["nx"], r["nx2"]
            link(v, v.tensor_scalar(a_, r["cnt"], 128.0, None, ALU.is_gt))
            for q in range(2, 5):
                link(v, v.scalar_tensor_tensor(b_, r["cnt"], 128.0 * q, a_, ALU.is_gt, ALU.add))
                a_, b_ = b_, a_
            up = WK(7600, 256).rearrange("p (e f) -> p e f", e=NE)
            link(v, v.tensor_tensor(up, a_.unsqueeze(1).broadcast_to([128, NE, NE]), C("upto").rearrange("p (e f) -> p e f", e=NE), ALU.mult))
            link(v, v.tensor_reduce(r["cx"], up, AX.X, ALU.add))
            link(v, v.tensor_tensor(r["px"], r["cx"], a_, ALU.subtract))
            cmp = r["cmp"].rearrange("p (x e) -> p x e", x=EXTRA)
            link(v, v.tensor_tensor(cmp, r["cx"].unsqueeze(1).broadcast_to([128, EXTRA, NE]), C("tile").unsqueeze(2).broadcast_to([128, EXTRA, NE]), ALU.is_le))
            link(v, v.tensor_reduce(r["xe"][:, 0:EXTRA], cmp, AX.X, ALU.add))
            link(v, v.tensor_scalar(r["xe"][:, 0:EXTRA], r["xe"][:, 0:EXTRA], float(NE - 1), None, ALU.min))
            link(v, v.tensor_copy(r["xe"][:, EXTRA:EXTRA + 1], r["cx"][:, NE - 1:NE]))
            v.tensor_copy(extra_tab[:, :], r["xe"]).then_inc(sem(f"extra_tab@{l}"), 1)
            link(v, v.tensor_scalar(r["xbase"], r["px"], float(MAIN - 1), None, ALU.add))

            def per_token(x):
                return x.unsqueeze(1).broadcast_to([128, NT, NE])
            main = r["slot"].rearrange("p (i e) -> p i e", i=NT)
            link(v, v.scalar_tensor_tensor(main, rk, float(NE), per_token(C("expert")), ALU.mult, ALU.add))
            a_, b_ = r["ext"], r["diff"]
            link(v, v.tensor_scalar(a_, r["rank"], 128.0, None, ALU.is_ge))
            for q in range(2, 5):
                link(v, v.scalar_tensor_tensor(b_, r["rank"], 128.0 * q, a_, ALU.is_ge, ALU.add))
                a_, b_ = b_, a_
            link(v, v.tensor_scalar(b_, a_, float(1 - 128 * EXTRA), None, ALU.mult))
            link(v, v.scalar_tensor_tensor(r["ext"], r["rank"], float(EXTRA), b_, ALU.mult, ALU.add))
            ext = r["ext"].rearrange("p (i e) -> p i e", i=NT)
            link(v, v.tensor_tensor(ext, ext, per_token(r["xbase"]), ALU.add))
            link(v, v.tensor_tensor(r["diff"], r["ext"], r["slot"], ALU.subtract))
            link(v, v.scalar_tensor_tensor(r["ext"], r["rank"], 128.0, r["diff"], ALU.is_ge, ALU.mult))
            link(v, v.tensor_tensor(r["slot"], r["slot"], r["ext"], ALU.add))
            for c, (oh, s) in enumerate((("OH1", "s1"), ("OH2", "s2"))):
                link(v, v.tensor_tensor(r["t1"], r[oh], r["slot"], ALU.mult))
                link(v, v.tensor_reduce(r[s], r["t1"].rearrange("p (i e) -> p i e", i=NT), AX.X, ALU.add))
                link(v, v.tensor_copy(slot_i[:, c, :], r[s]))
            v.sem_inc(sem(f"slots@{l}"), 1)

            gT = P(f"g_ffn{l}")

            def xgT_out(e):
                v.wait_ge(sem(f"turned@{l}"), at(f"turned@{l}", e + 1))
                if e > 0:
                    v.wait_ge(sem(f"gu@{l}"), at(f"gu@{l}", e))
                for b in range(2):
                    v.tensor_tensor(xgT[:, 4 * b:4 * b + 4, :], ps[b][:, :].rearrange("p (k s) -> p k s", k=4),
                                    gT[:, 4 * b:4 * b + 4].unsqueeze(2).broadcast_to([128, 4, 128]), ALU.mult).then_inc(sem(f"xgT@{l}"), 1)

            def hidden(e, par_):
                v.wait_ge(sem(f"silu@{l}"), at(f"silu@{l}", e + 1))
                if e - 1 > 0:
                    v.wait_ge(sem(f"ht@{l}"), at(f"ht@{l}", e - 1))
                v.tensor_tensor(hm[:, par_, :], ps[2 + par_][:, DE:2 * DE], sil[:, par_, :], ALU.mult).then_inc(sem(f"hidden@{l}"), 1)

            def y_half(e, par_):
                v.wait_ge(sem(f"down@{l}"), at(f"down@{l}", e + 1))
                if e >= 2:
                    if 16 * (e // 2) > 0:
                        v.wait_ge(sem(f"y_out_{par_}@{l}"), at(f"y_out_{par_}@{l}", 16 * (e // 2)))
                v.tensor_copy(yrow[:, par_, 0:512], ps[5][:, :]).then_inc(sem(f"y_v@{l}"), 1)
            xgT_out(0)
            xgT_out(1)
            hidden(0, 0)
            for e in range(1, NE):
                if e < NE - 1:
                    xgT_out(e + 1)
                y_half(e - 1, (e - 1) % 2)
                hidden(e, e % 2)
            y_half(NE - 1, 1)
            n_extra = v.value_load(extra_tab[0:1, EXTRA:EXTRA + 1], min_val=0, max_val=EXTRA)
            for x in range(EXTRA):
                with v.If(n_extra > x):
                    done = sem(f"x{l}_dve")
                    v.wait_ge(sem(f"x{l}_pe"), at(f"x{l}_pe", 4 * x + 1))
                    for b in range(2):
                        i = v.tensor_tensor(xgT[:, 4 * b:4 * b + 4, :], ps[b][:, :].rearrange("p (k s) -> p k s", k=4),
                                            gT[:, 4 * b:4 * b + 4].unsqueeze(2).broadcast_to([128, 4, 128]), ALU.mult)
                    i.then_inc(done, 1)
                    v.wait_ge(sem(f"x{l}_act"), at(f"x{l}_act", 3 * x + 1))
                    v.tensor_tensor(hm[:, 0, :], ps[2][:, DE:2 * DE], sil[:, 0, :], ALU.mult).then_inc(done, 1)
                    v.wait_ge(sem(f"x{l}_pe"), at(f"x{l}_pe", 4 * x + 4))
                    if x == 0:
                        v.wait_ge(sem(f"y_out_0@{l}"), at(f"y_out_0@{l}", 16 * NE // 2))
                    else:
                        if 16 * x > 0:
                            v.wait_ge(sem(f"x{l}_y"), at(f"x{l}_y", 16 * x))
                    v.tensor_copy(yrow[:, 0, 0:512], ps[5][:, :]).then_inc(done, 1)
            for i in range(NT):
                n = ROWS[i]
                v.wait_ge(sem(f"ygat_{i % 3}@{l}"), at(f"ygat_{i % 3}@{l}", 32 * (i // 3 + 1)))
                res = resid[0:n, i, :]
                link(v, v.scalar_tensor_tensor(res, ygat[0:n, i % 3, 0, :], r["gate1"][0:n, i:i + 1], res, ALU.mult, ALU.add))
                v.scalar_tensor_tensor(res, ygat[0:n, i % 3, 1, :], r["gate2"][0:n, i:i + 1], res, ALU.mult, ALU.add).then_inc(sem(f"collected@{l}"), 1)
                if l == 1 and i:
                    final_rows(v, i - 1)
            if l == 1:
                final_rows(v, NT - 1)

        def final_rows(v, i):
            n = ROWS[i]
            v.wait_ge(sem("ss_final"), at("ss_final", i + 1))
            v.tensor_scalar(stat["ms"][0:n, i:i + 1], stat["ss"][0:n, i:i + 1], 1.0 / D, EPS, ALU.mult, ALU.add).then_inc(sem("ms_final"), 1)
            v.wait_ge(sem("sd_final"), at("sd_final", i + 1))
            link(v, v.reciprocal(stat["rstd"][0:n, i:i + 1], stat["sd"][0:n, i:i + 1]))
            v.wait_ge(sem("gfinal_in"), at("gfinal_in", 16))
            v.scalar_tensor_tensor(resid[0:n, i, :], resid[0:n, i, :], stat["rstd"][0:n, i:i + 1], gfin[0:n, :], ALU.mult, ALU.mult).then_inc(sem("y_done"), 1)

        block = ctx.enter_context(nc.Block())

        @block.sync
        def _(sp):
            sp.dma_start(con[:, :], a["c_table"]).then_inc(sem("con_in"), 16)
            sp.dma_start(resid[:, 0:4, :], a["x_prompt"][0].rearrange("(i p) d -> p i d", p=128)).then_inc(sem("x_in"), 16)
            sp.dma_start(resid[0:NDEC, 4, :], a["x_sample"].rearrange("s t d -> (s t) d")).then_inc(sem("x_in"), 16)
            sp.dma_start(par[:, :], a["params"]).then_inc(sem("par_in"), 16)
            w1 = a["conv_w_pw1"][0].rearrange("(k p) (b n) -> p k b n", p=128, b=2)
            for c in range(4):
                dst = RG(c * SLOT, 4096).rearrange("p (k b n) -> p k b n", k=KD, b=2)
                for b in range(2):
                    sp.dma_start(dst[:, :, b, :], w1[:, :, b, 256 * c:256 * c + 256]).then_inc(sem(f"w_pw1_{c}"), 16)
                if c == 0:
                    sp.dma_start(state[0:120, :, :], a["state_conv"][0].rearrange("(a s) t d -> (s t) a d", a=2)).then_inc(sem("state_in"), 16)
            sp.wait_ge(sem("extra_zero"), at("extra_zero", 1))
            for x in range(EXTRA):
                sp.dma_start(scratch["y"][MAIN + 128 * x:MAIN + 128 * x + 128], last_p).then_inc(sem("y_zero"), 16)
            sp.dma_start(bpw2, a["b_pw2_rows"]).then_inc(sem("bpw2_in"), 16)
            sp.dma_start(ids[:, :], a["c_ids"]).then_inc(sem("ids_in"), 16)
            sp.dma_start(pages[:, :], a["page_order"]).then_inc(sem("pages_in"), 16)
            for l in LAYERS:
                sp.dma_start(scratch[f"owner{l}"].rearrange("(p n) x -> p (n x)", p=128), a["c_zero"]).then_inc(sem("owner_zero"), 16)
            cs = o["conv_sample"][0]
            sp.dma_start(cs[:, 0:PASTC - DSEQ, :], a["state_conv"][0][:, DSEQ:, :]).then_inc(out_sem, 16)
            w2 = a["conv_w_pw2"][0].rearrange("(k p) n -> p k n", p=128)
            for c in range(2):
                sp.wait_ge(sem("pw1_mm"), at("pw1_mm", 2 * (c + 1)))
                dst = RG(c * SLOT, 4096).rearrange("p (k n) -> p k n", k=KD)
                sp.dma_start(dst, w2[:, :, 512 * c:512 * c + 512]).then_inc(sem(f"w_pw2_{c}"), 16)
            sp.wait_ge(sem("last_rows"), at("last_rows", 4))
            sp.dma_start(o["conv_prompt"][0, 0], last_p[2:32, :]).then_inc(out_sem, 16)
            for s in range(NSEQ):
                sp.dma_start(cs[s, PASTC - DSEQ:, :], last_s[4 * s:4 * s + 4, :]).then_inc(out_sem, 16)
            n_out[0] = 16 * (1 + 1 + NSEQ)

            for l in LAYERS:
                if l == 1:
                    sp.wait_ge(sem("t_o"), at("t_o", KD))
                    sp.wait_ge(sem("pv_all"), at("pv_all", 2))
                    sp.dma_start(gfin, a["g_final_rows"]).then_inc(sem("gfinal_in"), 16)
                for u in (2, 3, 0, 1):
                    if l == 0:
                        if u == 2:
                            sp.wait_ge(sem("pw1_mm"), at("pw1_mm", KD))
                            sp.wait_ge(sem("prod_used"), at("prod_used", KD))
                        elif u == 3:
                            sp.wait_ge(sem("bpw2_used"), at("bpw2_used", 1))
                        elif u == 0:
                            sp.wait_ge(sem("pw2_mm"), at("pw2_mm", 2 * NT))
                        else:
                            sp.wait_ge(out_sem, n_out[0])
                    elif u == 0:
                        sp.wait_ge(sem("wo_mm"), at("wo_mm", 2 * NT))
                    for dst, src in wload(l, u, u):
                        sp.dma_start(dst, src).then_inc(sem(f"w_moe_{u}@{l}"), 16)
                sp.wait_ge(sem(f"xh_ffn{l}"), at(f"xh_ffn{l}", NT))
                sp.dma_start(scratch[f"rows{l}"][0:SEQ].rearrange("(i p) d -> p i d", p=128), xhat[:, 0:4, :]).then_inc(sem(f"rows_out@{l}"), 16)
                sp.dma_start(scratch[f"rows{l}"][SEQ:NTOK], xhat[0:NDEC, 4, :]).then_inc(sem(f"rows_out@{l}"), 16)
                with sp.Fori(0, 3) as j:
                    for u in range(4):
                        sp.wait_ge(sem(f"down@{l}"), at(f"down@{l}", 4 * j + (u + 1)))
                        for dst, src in wload(l, 4 * j + (4 + u), u):
                            sp.dma_start(dst, src).then_inc(sem(f"w_moe_{u}@{l}"), 16)
                if l == 0:
                    attention_first_loads(sp)
                sp.wait_ge(sem(f"extra_tab@{l}"), at(f"extra_tab@{l}", 1))
                n_extra = sp.value_load(extra_tab[0:1, EXTRA:EXTRA + 1], min_val=0, max_val=EXTRA)
                for x in range(EXTRA):
                    with sp.If(n_extra > x):
                        if x < 2:
                            if NE - 3 + EXTRA_SLOTS[l] + x > 0:
                                sp.wait_ge(sem(f"down@{l}"), at(f"down@{l}", NE - 3 + EXTRA_SLOTS[l] + x))
                        else:
                            if 4 * (x - 1) > 0:
                                sp.wait_ge(sem(f"x{l}_pe"), at(f"x{l}_pe", 4 * (x - 1)))
                        e = sp.value_load(extra_tab[0:1, x:x + 1], min_val=0, max_val=NE - 1)
                        for dst, src in wload(l, e, EXTRA_SLOTS[l] + x % 2):
                            sp.dma_start(dst, src).then_inc(sem(f"x{l}_w{x % 2}"), 16)
                if l == 0:
                    attention_loads(sp)
            for i in range(4):
                sp.wait_ge(sem("y_done"), at("y_done", i + 1))
                sp.dma_start(o["y_prompt"][0, 128 * i:128 * i + 128], resid[:, i, :]).then_inc(out_sem, 16)
            sp.wait_ge(sem("y_done"), at("y_done", NT))
            sp.dma_start(o["y_sample"].rearrange("s t d -> (s t) d"), resid[0:NDEC, 4, :]).then_inc(out_sem, 16)
            n_out[0] += 16 * NT
            sp.wait_ge(out_sem, n_out[0])

        @block.gpsimd
        def _(pool):
            pool.memset(gp[:, :, 0:PASTC], 0.0).then_inc(sem("pad"), 1)
            pool.memset(last_p, 0.0).then_inc(sem("extra_zero"), 1)
            pool.memset(stat["ss"], 1.0).then_inc(sem("pad"), 1)
            wdw = P("w_dw").rearrange("p (m x) -> p m x", m=8)
            pool.wait_ge(sem("par_in"), at("par_in", 16))

            def pool_conv(n, taps):
                out = cv[:, POOL_TILES[n], 0:SEQ]
                for x in taps:
                    pool.wait_ge(sem("tapped"), at("tapped", CONVW * n + x + 1))
                    if (CONVW - 1) * n + x - 1 > 0:
                        pool.wait_ge(sem("taps"), at("taps", (CONVW - 1) * n + x - 1))
                    pool.tensor_tensor(out, out, junk[:, SEQ * (x % 2):SEQ * (x % 2) + SEQ], ALU.add).then_inc(sem("taps"), 1)

            def products(m):
                pool.wait_ge(sem("past0"), at("past0", m + 1))
                pool.wait_ge(sem("past1"), at("past1", m + 1))
                pool.wait_ge(sem("windows"), at("windows", m + 1))
                if m - 1 > 0:
                    pool.wait_ge(sem("prod_used"), at("prod_used", m - 1))
                w = gw[:, m, :, 0:CONVW]
                win = bass.AP(tensor=w.tensor, offset=w.offset, ap=[w.ap[0], w.ap[1], [1, DSEQ], [1, CONVW]])
                pool.tensor_tensor(prod[:, m % 2, :, :].rearrange("p (s t) x -> p s t x", s=NSEQ), win,
                                   wdw[:, m, :].unsqueeze(1).unsqueeze(1).broadcast_to([128, NSEQ, DSEQ, CONVW]), ALU.mult).then_inc(sem("prod"), 1)
            products(0)
            products(1)
            pool_conv(0, range(1, CONVW))
            products(2)
            products(3)
            pool_conv(1, range(1, 20))
            products(4)
            products(5)
            pool_conv(1, range(20, CONVW))
            products(6)
            products(7)
            pool.wait_ge(sem("xh_mix0"), at("xh_mix0", NT))
            pool.wait_ge(sem("bpw2_in"), at("bpw2_in", 16))
            for i in range(NT):
                n = ROWS[i]
                ins = pool.tensor_tensor(resid[0:n, i, :], resid[0:n, i, :], bpw2[0:n, :], ALU.add)
                ins.then_inc(sem("bias_added"), 1)
            pool.wait_ge(sem("bias_added"), at("bias_added", NT))
            pool.sem_inc(sem("bpw2_used"), 1)

            for l in LAYERS:
                if l == 1:
                    attention_pool(pool)
                pool.wait_ge(sem("ids_in"), at("ids_in", 16))
                pool.wait_ge(sem("owner_zero"), at("owner_zero", 32))
                pool.wait_ge(sem(f"slots@{l}"), at(f"slots@{l}", 1))
                for i in range(NT):
                    for c in range(2):
                        n = ROWS[i]
                        pool.indirect_dma_start(scratch[f"owner{l}"], bass.IndirectOffsetOnAxis(ap=slot_i[0:n, c, i:i + 1], axis=0),
                                                ids[0:n, i:i + 1], None).then_inc(sem(f"owner_out@{l}"), 16)
                pool.wait_ge(sem(f"owner_out@{l}"), at(f"owner_out@{l}", 16 * 2 * NT))
                pool.dma_start(tokrow[:, :], scratch[f"owner{l}"][0:128 * NE].rearrange("(p n) x -> p (n x)", p=128)).then_inc(sem(f"tokrow@{l}"), 16)
                pool.wait_ge(sem(f"tokrow@{l}"), at(f"tokrow@{l}", 16))
                pool.wait_ge(sem(f"rows_out@{l}"), at(f"rows_out@{l}", 32))
                for e in range(NE):
                    if e - 1 > 0:
                        pool.wait_ge(sem(f"turned@{l}"), at(f"turned@{l}", e - 1))
                    pool.indirect_dma_start(xg[:, e % 2, :], None, scratch[f"rows{l}"], bass.IndirectOffsetOnAxis(ap=tokrow[:, e:e + 1], axis=0)).then_inc(sem(f"xg_{e % 2}@{l}"), 16)
                pool.dma_start(extra_tok[:, :], scratch[f"owner{l}"][MAIN:SLOTS].rearrange("(p x) a -> p (x a)", p=128)).then_inc(sem(f"extra_tok@{l}"), 16)
                pool.wait_ge(sem(f"extra_tok@{l}"), at(f"extra_tok@{l}", 16))
                pool.wait_ge(sem(f"extra_tab@{l}"), at(f"extra_tab@{l}", 1))
                pool.wait_ge(sem(f"turned@{l}"), at(f"turned@{l}", NE))
                n_extra = pool.value_load(extra_tab[0:1, EXTRA:EXTRA + 1], min_val=0, max_val=EXTRA)
                for x in range(EXTRA):
                    with pool.If(n_extra > x):
                        if 4 * x - 3 > 0:
                            pool.wait_ge(sem(f"x{l}_pe"), at(f"x{l}_pe", 4 * x - 3))
                        pool.indirect_dma_start(xg[:, 0, :], None, scratch[f"rows{l}"], bass.IndirectOffsetOnAxis(ap=extra_tok[:, x:x + 1], axis=0)).then_inc(sem(f"x{l}_rows"), 16)
                for b in range(2):
                    pool.wait_ge(sem(f"y_out_{b}@{l}"), at(f"y_out_{b}@{l}", 16 * NE // 2))
                for x in range(EXTRA):
                    with pool.If(n_extra > x):
                        pool.wait_ge(sem(f"x{l}_y"), at(f"x{l}_y", 16 * (x + 1)))
                        pool.nop()
                for i in range(NT):
                    n = ROWS[i]
                    if i - 2 > 0:
                        pool.wait_ge(sem(f"collected@{l}"), at(f"collected@{l}", i - 2))
                    for c in range(2):
                        pool.indirect_dma_start(ygat[0:n, i % 3, c, :], None, scratch["y"], bass.IndirectOffsetOnAxis(ap=slot_i[0:n, c, i:i + 1], axis=0)).then_inc(sem(f"ygat_{i % 3}@{l}"), 16)

        @block.tensor
        def _(pe):
            pe.wait_ge(sem("con_in"), at("con_in", 16))
            turn_pe(pe, "mix0", xhat, NT)
            pe.wait_ge(sem("state_in"), at("state_in", 16))
            for k in range(KD):
                for b in range(2):
                    if k > 0:
                        pe.wait_ge(sem(f"past{b}"), at(f"past{b}", k))
                    pe.transpose(ps[6 + b][:, 0:120], state[0:120, b, 128 * k:128 * k + 128], ident[0:120, 0:120]).then_inc(sem("state_t"), 1)
            wait_turned(pe, "mix0")
            for m in range(KD):
                c = m // 2
                if m % 2 == 0:
                    pe.wait_ge(sem(f"w_pw1_{c}"), at(f"w_pw1_{c}", 32))
                if m - 1 > 0:
                    pe.wait_ge(sem("glu"), at("glu", m - 1))
                if m == 1:
                    pe.wait_ge(sem("past0"), at("past0", KD))
                    pe.wait_ge(sem("past1"), at("past1", KD))
                w = RG(c * SLOT, 4096).rearrange("p (k b n) -> p k b n", k=KD, b=2)
                for b in range(2):
                    for k in range(KD):
                        mm = all_tokens(pe, 4 * (m % 2) + 2 * b, w[:, k, b, 128 * (m % 2):128 * (m % 2) + 128], xT, k)
                mm.then_inc(sem("pw1_mm"), 1)
            pe.wait_ge(sem("glu"), at("glu", KD))
            for half in range(2):
                for m in range(4 * half, 4 * half + 4):
                    c0 = 128 * (m % 4)
                    pe.transpose(ps[half][0:32, c0:c0 + 128], gp[:, m, 510:542], ident)
                    mm = pe.transpose(ps[2 + half][0:32, c0:c0 + 128], gp[:, m, PASTC + SEQ:], ident)
                mm.then_inc(sem("last_t"), 1)
            for m in range(KD):
                if m in DVE_TILES:
                    pe.wait_ge(sem("conv"), at("conv", DVE_TILES.index(m) + 1))
                if m in POOL_TILES:
                    if (CONVW - 1) * (POOL_TILES.index(m) + 1) > 0:
                        pe.wait_ge(sem("taps"), at("taps", (CONVW - 1) * (POOL_TILES.index(m) + 1)))
                pe.wait_ge(sem("conv_s"), at("conv_s", m + 1))
                mm = all_tokens(pe, 6, C("mean"), cv, m)
            mm.then_inc(sem("mean"), 1)
            pe.wait_ge(sem("last_rows"), at("last_rows", 4))
            for m in range(KD):
                pe.wait_ge(sem("sq"), at("sq", m + 1))
                mm = all_tokens(pe, 0, C("mean"), sq, m)
            mm.then_inc(sem("var"), 1)
            for c in range(2):
                pe.wait_ge(sem(f"w_pw2_{c}"), at(f"w_pw2_{c}", 16))
            pe.wait_ge(sem("conv_h"), at("conv_h", KD))
            rows_out(pe, "pw2", xT, [RG(c * SLOT, 4096).rearrange("p (k n) -> p k n", k=KD) for c in range(2)])
            for l in LAYERS:
                moe_pe(pe, l)
                if l == 0:
                    attention_pe(pe)

        @block.scalar
        def _(act):
            act.wait_ge(sem("pad"), at("pad", 2))
            for i in range(NT):
                act.wait_ge(sem("x_in"), at("x_in", 32))
                row_squares(act, "mix0", i)
            row_roots(act, "mix0")
            act.wait_ge(sem("par_in"), at("par_in", 16))
            turned_act(act, "mix0", [(xT, P("g_mix0"))])
            for k in range(KD):
                act.wait_ge(sem("state_t"), at("state_t", 2 * k + 2))
                act.copy(gw[:, k, 4:8, 0:PASTC], ps[7][:, 0:120].rearrange("p (s t) -> p s t", s=4)).then_inc(sem("past1"), 1)
            bp = P("b_pw1")
            wdw = P("w_dw").rearrange("p (m x) -> p m x", m=8)

            def sigmoid(m):
                act.wait_ge(sem("pw1_mm"), at("pw1_mm", m + 1))
                if m - 1 > 0:
                    act.wait_ge(sem("glu"), at("glu", m - 1))
                act.activation(halves(sig[:, m % 2, :]), two_banks(4 * (m % 2) + 2), ACT.Sigmoid, bias=bp[:, 8 + m:9 + m]).then_inc(sem("sig"), 1)

            def tapped(n, taps):
                m = POOL_TILES[n]
                act.wait_ge(sem("glu"), at("glu", m + 1))
                act.wait_ge(sem("t_mix0"), at("t_mix0", KD + 1))
                act.wait_ge(sem("pad"), at("pad", 1))
                for x in taps:
                    src = gp[:, m, x:x + SEQ]
                    if x == 0:
                        i = act.activation(cv[:, m, 0:SEQ], src, ACT.Identity, bias=P("b_dw")[:, m:m + 1], scale=wdw[:, m, 0:1])
                    else:
                        if (CONVW - 1) * n + max(x - 2, 0) > 0:
                            act.wait_ge(sem("taps"), at("taps", (CONVW - 1) * n + max(x - 2, 0)))
                        i = act.activation(junk[:, SEQ * (x % 2):SEQ * (x % 2) + SEQ], src, ACT.Copy, scale=wdw[:, m, x:x + 1])
                    i.then_inc(sem("tapped"), 1)
            for m in range(3):
                sigmoid(m)
            for n in range(2):
                tapped(n, range(0, 10))
                sigmoid(3 * n + 3)
                tapped(n, range(10, 21))
                sigmoid(3 * n + 4)
                tapped(n, range(21, CONVW))
                if n == 0:
                    sigmoid(5)
            for half in range(2):
                act.wait_ge(sem("last_t"), at("last_t", half + 1))
                act.wait_ge(sem("y_zero"), at("y_zero", 16 * EXTRA))
                act.copy(last_p[0:32, 512 * half:512 * half + 512], ps[half][0:32, :]).then_inc(sem("last_rows"), 1)
                act.copy(last_s[0:32, 512 * half:512 * half + 512], ps[2 + half][0:32, :]).then_inc(sem("last_rows"), 1)
            for m in range(KD):
                act.wait_ge(sem("centred"), at("centred", m + 1))
                act.activation(sq[:, m, :], cv[:, m, :], ACT.Square).then_inc(sem("sq"), 1)
            act.wait_ge(sem("var_eps"), at("var_eps", 1))
            act.activation(lnr, lnr, ACT.Sqrt).then_inc(sem("ln_sd"), 1)
            for m in range(KD):
                act.wait_ge(sem("scaled"), at("scaled", m + 1))
                act.activation(xT[:, m, :], cv[:, m, :], ACT.Silu, bias=P("ln_b")[:, m:m + 1], scale=P("ln_g")[:, m:m + 1]).then_inc(sem("conv_h"), 1)
            for i in range(NT):
                act.wait_ge(sem("pw2_add"), at("pw2_add", 2 * (i + 1)))
                row_squares(act, "ffn0", i)
            row_roots(act, "ffn0")
            for l in LAYERS:
                moe_act(act, l)
                if l == 0:
                    attention_act(act)
                    for i in range(NT):
                        act.wait_ge(sem("wo_add"), at("wo_add", 2 * (i + 1)))
                        row_squares(act, "ffn1", i)
                    row_roots(act, "ffn1")
            for i in range(NT):
                act.wait_ge(sem("collected@1"), at("collected@1", i + 1))
                row_squares(act, "final", i)
                n = ROWS[i]
                act.wait_ge(sem("ms_final"), at("ms_final", i + 1))
                act.activation(stat["sd"][0:n, i:i + 1], stat["ms"][0:n, i:i + 1], ACT.Sqrt).then_inc(sem("sd_final"), 1)

        @block.vector
        def _(v):
            v.wait_ge(sem("con_in"), at("con_in", 16))
            v.tensor_copy(count[:, 0, :], C("before"))
            v.tensor_copy(count[:, 1, :], C("ones"))
            norm_stats(v, "mix0")
            norm_rows(v, "mix0")
            v.wait_ge(sem("par_in"), at("par_in", 16))
            turned_dve(v, "mix0", [(xT, P("g_mix0"))])
            for k in range(KD):
                v.wait_ge(sem("state_t"), at("state_t", 2 * k + 1))
                v.tensor_copy(gw[:, k, 0:4, 0:PASTC], ps[6][:, 0:120].rearrange("p (s t) -> p s t", s=4)).then_inc(sem("past0"), 1)
            bp = P("b_pw1")
            wdw = P("w_dw").rearrange("p (m x) -> p m x", m=8)
            v.wait_ge(sem("pad"), at("pad", 1))

            def glu(m):
                v.wait_ge(sem("sig"), at("sig", m + 1))
                link(v, v.scalar_tensor_tensor(halves(gp[:, m, PASTC:]), two_banks(4 * (m % 2)), bp[:, m:m + 1], halves(sig[:, m % 2, :]), ALU.add, ALU.mult))
                v.tensor_copy(gw[:, m, :, PASTC:], gp[:, m, PASTC + SEQ:].rearrange("p (s t) -> p s t", s=NSEQ)).then_inc(sem("windows"), 1)
                v.sem_inc(sem("glu"), 1)

            def conv(tiles, between):
                last = {}
                for x in range(CONVW):
                    for m in tiles:
                        out = cv[:, m, 0:SEQ]
                        if x == 0:
                            i = v.tensor_scalar(out, gp[:, m, 0:SEQ], wdw[:, m, 0:1], P("b_dw")[:, m:m + 1], ALU.mult, ALU.add)
                        else:
                            if last[m] > 0:
                                v.wait_ge(sem("dve_chain"), at("dve_chain", last[m]))
                            i = v.scalar_tensor_tensor(out, gp[:, m, x:x + SEQ], wdw[:, m, x:x + 1], out, ALU.mult, ALU.add)
                        i.then_inc(sem("dve_chain"), 1)
                        chain[0] += 1
                        last[m] = chain[0]
                    for step, m in between.get(x, ()):
                        step(m)
                v.wait_ge(sem("dve_chain"), at("dve_chain", chain[0]))
                for _ in tiles:
                    v.sem_inc(sem("conv"), 1)

            def conv_sampled(m):
                v.wait_ge(sem("prod"), at("prod", m + 1))
                link(v, v.tensor_reduce(cv[:, m, SEQ:NTOK], prod[:, m % 2, :, :], AX.X, ALU.add))
                v.sem_inc(sem("prod_used"), 1)
                v.tensor_scalar(cv[:, m, SEQ:NTOK], cv[:, m, SEQ:NTOK], P("b_dw")[:, m:m + 1], None, ALU.add).then_inc(sem("conv_s"), 1)

            v.wait_ge(sem("t_mix0"), at("t_mix0", KD + 1))
            glu(0)
            glu(1)
            conv((0, 1), {12: [(glu, 2)], 25: [(glu, 3)]})
            conv_sampled(0)
            conv_sampled(1)
            glu(4)
            conv((3, 4), {13: [(glu, 5)], 25: [(glu, 6)]})
            conv_sampled(2)
            conv_sampled(3)
            glu(7)
            conv((6, 7), {14: [(conv_sampled, 4), (conv_sampled, 5)]})
            conv_sampled(6)
            conv_sampled(7)
            v.wait_ge(sem("mean"), at("mean", 1))
            v.wait_ge(sem("conv_s"), at("conv_s", KD))
            if (CONVW - 1) * len(POOL_TILES) > 0:
                v.wait_ge(sem("taps"), at("taps", (CONVW - 1) * len(POOL_TILES)))
            for m in range(KD):
                v.tensor_tensor(halves(cv[:, m, :]), halves(cv[:, m, :]), two_banks(6), ALU.subtract).then_inc(sem("centred"), 1)
            v.wait_ge(sem("var"), at("var", 1))
            v.tensor_scalar(halves(lnr), two_banks(0), EPS, None, ALU.add).then_inc(sem("var_eps"), 1)
            v.wait_ge(sem("ln_sd"), at("ln_sd", 1))
            link(v, v.reciprocal(lnr, lnr))
            v.wait_ge(sem("centred"), at("centred", KD))
            for m in range(KD):
                v.tensor_tensor(cv[:, m, :], cv[:, m, :], lnr, ALU.mult).then_inc(sem("scaled"), 1)
            v.wait_ge(sem("bias_added"), at("bias_added", NT))
            rows_added(v, "pw2")
            v.wait_ge(sem("pw2_add"), at("pw2_add", 10))
            norm_stats(v, "ffn0")
            v.wait_ge(sem("conv_h"), at("conv_h", KD))
            norm_rows(v, "ffn0")
            for l in LAYERS:
                moe_dve(v, l)
                if l == 0:
                    attention_dve(v)
                    norm_stats(v, "ffn1")
                    norm_rows(v, "ffn1")


_INS = ["x_prompt", "x_sample", "cache_k", "cache_v", "state_conv", "conv_w_pw1", "conv_w_pw2", "w_kv", "attn_w_q", "attn_w_o",
        "moe_w_gate", "moe_w_up", "moe_w_down"]
_OUTS = [("y_prompt", (1, SEQ, D)), ("y_sample", (NSEQ, DSEQ, D)), ("conv_prompt", (1, 1, PASTC, D)), ("conv_sample", (1, NSEQ, PASTC, D)),
         ("k_prompt", (1, SEQ, NH, 2, HD)), ("v_prompt", (1, SEQ, NH, 2 * HD)), ("k_sample", (NSEQ, DSEQ, NH, 2, HD)),
         ("v_sample", (NSEQ, DSEQ, NH, 2 * HD))]


def laid_out(inp):
    def feat(x):
        x = np.asarray(x)
        return x.reshape(-1, 128).T

    def rows(x):
        return np.tile(np.asarray(x).reshape(1, -1), (128, 1))
    t = {}
    for l in range(2):
        t[f"g_mix{l}"] = feat(inp["norm_mix"][l])
        t[f"g_ffn{l}"] = feat(inp["norm_ffn"][l])
        wr = np.concatenate([np.asarray(inp["moe_w_grp"][l]), np.asarray(inp["moe_w_exp_router"][l]).reshape(D, NE)], axis=1)
        t[f"wr{l}"] = wr.reshape(KD, 128, 20).transpose(1, 0, 2).reshape(128, -1)
        t[f"br{l}"] = rows(np.concatenate([np.asarray(inp["moe_b_grp"][l]), np.asarray(inp["moe_b_exp_router"][l]).reshape(-1)]))
    t["g_kv"] = feat(inp["norm_kv"])
    t["b_pw1"] = feat(inp["conv_b_pw1"][0])
    t["b_dw"] = feat(inp["conv_b_dw"][0])
    t["ln_g"] = feat(inp["conv_ln_g"][0])
    t["ln_b"] = feat(inp["conv_ln_b"][0])
    t["subln"] = feat(inp["attn_subln_g"][0])
    t["w_dw"] = np.asarray(inp["conv_w_dw"][0]).reshape(CONVW, KD, 128).transpose(2, 1, 0).reshape(128, -1)
    t["lams"] = rows(np.concatenate([np.asarray(inp[f"attn_lambda_{n}"][0]) for n in ("q1", "k1", "q2", "k2")]))
    pt = np.asarray(inp["page_table"])
    order = np.concatenate([pt.reshape(4, 2, 8).transpose(0, 2, 1).reshape(-1), pt.reshape(2, 4, 8).transpose(0, 2, 1).reshape(-1)])
    return {"params": np.concatenate([t[n] for n in PCOL], axis=1), "page_order": order.reshape(1, -1),
            "b_pw2_rows": rows(inp["conv_b_pw2"][0]), "g_final_rows": rows(inp["norm_final"])}


def kernel(**inputs):
    import concourse.bacc as bacc
    from concourse.bass_utils import run_bass_kernel_spmd

    nc = bacc.Bacc("TRN2", target_bir_lowering=False, num_devices=1)
    arrays = {n: np.ascontiguousarray(inputs[n]) for n in _INS}
    arrays.update({n: np.ascontiguousarray(x) for n, x in {**laid_out(inputs), **constants()}.items()})
    a = {n: nc.dram_tensor(f"in_{n}", x.shape, mybir.dt.from_np(x.dtype), kind="ExternalInput").ap() for n, x in arrays.items()}
    o = {n: nc.dram_tensor(f"out_{n}", s, F32, kind="ExternalOutput").ap() for n, s in _OUTS}
    scratch = {"y": nc.dram_tensor("y_rows", (SLOTS, D), F32, kind="Internal").ap()}
    for l in range(2):
        scratch[f"owner{l}"] = nc.dram_tensor(f"owner{l}", (SLOTS, 1), I32, kind="Internal").ap()
        scratch[f"rows{l}"] = nc.dram_tensor(f"rows{l}", (NTOK, D), F32, kind="Internal").ap()
    program(nc, a, o, scratch)
    nc.compile()
    r = run_bass_kernel_spmd(nc, [{f"in_{n}": x for n, x in arrays.items()}], core_ids=[0])
    return tuple(r.results[0][f"out_{n}"] for n, _ in _OUTS)
```

```python
import math
from contextlib import ExitStack

import numpy as np

import concourse.bass as bass
from concourse import mybir

F32, I32, BF16 = mybir.dt.float32, mybir.dt.int32, mybir.dt.bfloat16
ALU, ACT, AX = mybir.AluOpType, mybir.ActivationFunctionType, mybir.AxisListType

D = 1024
KD = D // 128
SEQ = 512
NSEQ, DSEQ = 8, 4
NDEC = NSEQ * DSEQ
NTOK = SEQ + NDEC
HTOK = NTOK // 2
NT = 5
ROWS = [128, 128, 128, 128, NDEC]
N_ROWS = 2 * 4 + 1
CONVW = 31
PASTC = CONVW - 1
NH, HD = 8, 64
NG, EPG = 4, 4
NE = NG * EPG
DE = 256
PAGE, NPAGE = 128, 8
PAST = PAGE * NPAGE
EPS = 1e-6
LAM_INIT = 0.8 - 0.6 * math.exp(-0.3)
NEG = -1e30
MAIN = 128 * NE
EXTRA = 2 * NTOK // 128
SLOTS = MAIN + 128 * EXTRA
NKEY = PAST + NDEC

PCOL = {}
_at = 0
for _n, _w in (("g_mix0", 8), ("g_mix1", 8), ("g_ffn0", 8), ("g_ffn1", 8), ("g_kv", 8), ("b_pw1", 16),
               ("b_dw", 8), ("ln_g", 8), ("ln_b", 8), ("subln", 1), ("w_dw", 8 * CONVW),
               ("wr0", 160), ("wr1", 160), ("br0", 20), ("br1", 20), ("lams", 256)):
    PCOL[_n] = (_at, _w)
    _at += _w
NPCOL = _at
CCOL = {}
_at = 0
for _n, _w in (("ident", 128), ("before", 128), ("ones", 128), ("mean", 128), ("rev4", 4), ("expert", 16),
               ("upto", 256), ("tile", 8), ("comb", 64), ("isc0", 1), ("isc1", 1), ("headmask", 8), ("newbias", 4 * NDEC)):
    CCOL[_n] = (_at, _w)
    _at += _w
NCCOL = _at


def constants():
    p = np.arange(128)
    t = {}
    t["ident"] = np.eye(128)
    t["before"] = p[:, None] < p[None, :]
    t["ones"] = np.ones((128, 128))
    t["mean"] = np.full((128, 128), 1.0 / D)
    t["rev4"] = np.tile(np.array([4, 3, 2, 1]), (128, 1))
    t["expert"] = np.tile(np.arange(16), (128, 1))
    e = np.arange(NE)
    t["upto"] = np.tile((e[None, :] <= e[:, None]).reshape(1, -1), (128, 1))
    t["tile"] = np.tile(np.arange(EXTRA), (128, 1))
    row_s, row_c, row_ht = p // 64, p // 32 % 2, p % 32
    col = np.arange(64)
    t["comb"] = (row_s[:, None] == col[None, :] // 32) & (row_ht[:, None] == col[None, :] % 32)
    t["isc0"] = (row_c == 0)[:, None]
    t["isc1"] = (row_c == 1)[:, None]
    t["headmask"] = (p // 4 % 8)[:, None] == np.arange(8)[None, :]
    slope = 2.0 ** -(p // 4 % 8 + 1.0)
    tok = p % 4
    nb = np.empty((128, 4, NDEC))
    k = np.arange(NDEC)
    for pair in range(4):
        own = (2 * pair + row_s)[:, None] == k[None, :] // DSEQ
        ahead = tok[:, None] - (k % DSEQ)[None, :]
        nb[:, pair] = np.where(own & (ahead >= 0), -slope[:, None] * ahead, NEG)
    t["newbias"] = nb.reshape(128, -1)
    table = np.concatenate([np.asarray(t[n], np.float32).reshape(128, -1) for n in CCOL], axis=1)
    past = (-slope[:, None] * (PAST + tok[:, None] - np.arange(PAST)[None, :])).astype(np.float32)
    j = np.arange(896)[None, :] - 384
    dist = np.where(j <= p[:, None], j - p[:, None], NEG).astype(np.float32)
    ids = (np.arange(NT)[None, :] * 128 + p[:, None]).astype(np.int32)
    zero = np.zeros((128, SLOTS // 128), np.int32)
    return {"c_table": table, "c_past": past, "c_dist": dist, "c_ids": ids, "c_zero": zero}


def program(nc, a, o, scratch):
    with ExitStack() as ctx:
        def sb(name, shape, dt=F32):
            return ctx.enter_context(nc.sbuf_tensor(name, shape, dt))

        sems = {}

        TAGS = ("mix0", "ffn0", "kv", "o", "ffn1", "final")
        PER_TAG = {"ss": NT, "ms": NT, "sd": NT, "xh": NT, "t": KD + 1, "ev0": KD // 2 + 1, "ev1": KD // 2}
        PER_O = {"ss": 0, "ms": 0, "sd": 0, "xh": 4, "t": KD, "ev0": KD // 2, "ev1": KD // 2}
        PER_LAYER = {"gd": 1, "ed": 1, "gex": 1, "eex": 1, "logits": 1, "chosen": 1, "ranks": 1, "slots": 2, "extra_tab": 1, "extra_tok": 16, "turned": NE,
                     "xgT": 2 * NE, "gu": NE, "silu": NE, "hidden": NE, "ht": NE, "hT": NE, "down": NE, "y_v": NE, "y_a": NE,
                     "y_out_0": 8 * NE, "y_out_1": 8 * NE, "xg_0": 8 * NE, "xg_1": 8 * NE, "tokrow": 16,
                     "owner_out": 32 * NT, "rows_out": 32, "collected": NT, "ygat_0": 64, "ygat_1": 64, "ygat_2": 32,
                     "w_moe_0": 12 * NE, "w_moe_1": 12 * NE, "w_moe_2": 12 * NE, "w_moe_3": 12 * NE}

        IN_ORDER = {
            "pe_conv": (("state_t", 2 * KD), ("pw1_mm", KD), ("last_t", 2), ("mean", 1), ("var", 1)),
            "dve_ln": (("centred", KD), ("var_eps", 1), ("scaled", KD)),
            "act_conv": (("sig", KD), ("last_rows", 4), ("sq", KD), ("ln_sd", 1), ("conv_h", KD)),
            "pe_qkv": (("k_mm", NH), ("v_mm", N_ROWS), ("k_back", 2 * NT), ("q_mm", NH)),
            "dve_qkv": (("lam_sum", 1), ("v_done", N_ROWS), ("qz1", NH)),
            "act_qkv": (("kT", NH), ("k_rows", 2 * NT), ("qz0", NH), ("lam_exp", 1)),
            "chunk0": (("w_pw1_0", 32), ("w_pw2_0", 16), ("w_att0", 16), ("w_o0", 16)),
            "chunk1": (("w_pw1_1", 32), ("w_pw2_1", 16), ("w_att1", 16), ("w_o1", 16)),
            "chunk2": (("w_pw1_2", 32), ("w_att2", 16)),
            "chunk3": (("w_pw1_3", 32), ("w_att3", 16)),
        }
        BASE = {n: (s, sum(c for _, c in names[:q])) for s, names in IN_ORDER.items() for q, (n, _) in enumerate(names)}

        def place(name):
            if name in BASE:
                return BASE[name]
            stem, _, tag = name.partition("_")
            if stem in PER_TAG and tag in TAGS:
                return stem, sum((PER_O if x == "o" else PER_TAG)[stem] for x in TAGS[:TAGS.index(tag)])
            stem, _, layer = name.partition("@")
            return stem, PER_LAYER[stem] * int(layer) if layer else 0

        def sem(name):
            real = place(name)[0]
            if real not in sems:
                sems[real] = ctx.enter_context(nc.semaphore(real))
            return sems[real]

        resid = sb("resid", [128, NT, D])
        xhat = sb("xhat", [128, NT, D])
        xT = sb("xT", [128, KD, NTOK])
        ring = sb("ring", [128, 24576])
        work = sb("work", [128, 8704])
        par = sb("par", [128, NPCOL])
        con = sb("con", [128, NCCOL])
        junk = sb("junk", [128, D])
        small = sb("small", [128, 1970])
        ids = sb("ids", [128, NT], I32)
        slot_i = sb("slot_i", [128, 2, NT], I32)
        extra_tok = sb("extra_tok", [128, EXTRA], I32)
        extra_tab = sb("extra_tab", [128, EXTRA + 1], I32)
        chosen = sb("chosen", [128, NT, NE], BF16)
        count = sb("count", [128, 2, 128], BF16)
        tokrow = sb("tokrow", [128, NE], I32)
        pages = sb("pages", [1, 2 * NSEQ * NPAGE], I32)
        banks = ctx.enter_context(nc.psum_tensor("banks", [128, 8, 512], F32))
        ps = [banks[:, i, :] for i in range(8)]

        def two_banks(b):
            return banks[:, b:b + 2, 0:HTOK]

        def halves(x):
            return x.rearrange("p (c t) -> p c t", c=2)

        def P(name):
            s, w = PCOL[name]
            return par[:, s:s + w]

        def C(name):
            s, w = CCOL[name]
            return con[:, s:s + w]

        used = [0]

        def sm(n):
            used[0] += n
            assert used[0] <= 1970
            return small[:, used[0] - n:used[0]]

        def WK(s, n):
            return work[:, s:s + n]

        def RG(s, n):
            return ring[:, s:s + n]

        ident = C("ident")
        SLOT = 6144

        def xTd(k):
            return xT[:, k, SEQ:NTOK]

        gp = WK(0, KD * (PASTC + NTOK)).rearrange("p (m t) -> p m t", m=KD)
        gw = WK(4592, 8 * 272).rearrange("p (m s t) -> p m s t", m=8, s=NSEQ)
        sig = WK(6768, 2 * NTOK).rearrange("p (b t) -> p b t", b=2)
        cv = xhat[:, :, :].rearrange("p a d -> p (a d)")[:, 0:KD * NTOK].rearrange("p (m t) -> p m t", m=8)
        POOL_TILES = (2, 5)
        DVE_TILES = (0, 1, 3, 4, 6, 7)
        sq = WK(0, KD * NTOK).rearrange("p (m t) -> p m t", m=8)
        lnr = WK(6768, NTOK)
        state = RG(4096, 2048).rearrange("p (a d) -> p a d", a=2)
        last_p = RG(SLOT + 4096, 1024)
        last_s = RG(SLOT + 5120, 1024)
        prod = RG(2 * SLOT + 4096, 2 * 992).rearrange("p (b s x) -> p b s x", b=2, s=NDEC)
        bpw2 = RG(3 * SLOT + 4096, 1024)
        xg = WK(0, 2048).rearrange("p (b d) -> p b d", b=2)
        xgT = WK(2048, 1024).rearrange("p (k s) -> p k s", k=KD)
        hm = WK(3072, 512).rearrange("p (b f) -> p b f", b=2)
        hT = WK(3584, 256).rearrange("p (f s) -> p f s", f=2)
        sil = WK(3840, 512).rearrange("p (b f) -> p b f", b=2)
        yrow = WK(4352, 2048).rearrange("p (b d) -> p b d", b=2)
        ygat = WK(0, 6144).rearrange("p (b c d) -> p b c d", b=3, c=2)
        logit = WK(6400, 100).rearrange("p (i n) -> p i n", i=NT)
        gfin = WK(6528, 1024)
        xqT = WK(0, KD * NTOK).rearrange("p (k t) -> p k t", k=KD)
        kT = WK(4352, KD * NTOK).rearrange("p (h t) -> p h t", h=NH)
        vtok = xhat
        qz = [RG(4096 * c, 4096).rearrange("p (h t) -> p h t", h=NH) for c in range(2)]
        qdec = RG(8192, 4096).rearrange("p (s h r) -> p s h r", s=NSEQ, h=NH)
        otok = RG(12288, 4096).rearrange("p (i d) -> p i d", i=4)
        tbuf = RG(16384, 2048).rearrange("p (b c n) -> p b c n", b=2, c=2)
        aT = RG(18432, 1024).rearrange("p (b n) -> p b n", b=2)
        biash = RG(19456, 1792).rearrange("p (b n) -> p b n", b=2)
        dist = RG(21248, 896)
        ktk = RG(14336, 2048).rearrange("p (b d) -> p b d", b=2)
        kp = [[RG(1024 * (2 * b + j), 1024).rearrange("p (h n) -> p h n", h=NH) for j in range(2)] for b in range(2)]
        kring = WK(0, 4096).rearrange("p (b d) -> p b d", b=4)
        vring = RG(16384, 8192).rearrange("p (b d) -> p b d", b=8)
        xTflat = xT[:, :, :].rearrange("p k t -> p (k t)")
        tdec = xTflat[:, 0:2 * NKEY].rearrange("p (b n) -> p b n", b=2)
        aTd0 = xTflat[:, 2112:2112 + 9 * 128].rearrange("p (g r) -> p g r", g=9)
        aTd1 = kT[:, 0:3, 0:384].rearrange("p h (g r) -> p h g r", g=3)

        def aTd(quad, g):
            return aTd1[:, g // 3, g % 3, :] if quad else aTd0[:, g, :]
        oT = WK(0, KD * SEQ).rearrange("p (k t) -> p k t", k=KD)
        pastb = xTflat[:, 3264:3264 + PAST]
        odec = WK(4096, 256).rearrange("p (h t) -> p h t", h=NH)
        orow = sm(128)

        stat = {n: sm(w) for n, w in dict(ss=5, ms=5, sd=5, rstd=5).items()}
        r = {n: sm(w) for n, w in dict(
            gmax=5, geq=20, gsel=20, gmx=5, goh=20, gd=20, gex=20, gsum=5, pg=5, etmp=80, es=20, em=5, ed=20,
            eex=20, esum=5, er=5, pe=20, p1=5, eq1=20, sel1=20, mx1=5, oh1=20, pe2=20, p2=5, eq2=20, sel2=20,
            mx2=5, oh2=20, s12=5, rs=5, rsg=5, gate1=5, gate2=5, OH1=80, OH2=80, slot=80, s1=5,
            s2=5, cnt=16, nx=16, nx2=16, cx=16, px=16, xbase=16, cmp=128, xe=9, rank=80, ext=80, diff=80).items()}

        r["t1"] = r["etmp"]
        out_sem = sem("outputs")
        n_out = [0]


        def at(name, count):
            return count + place(name)[1]

        LAYERS = (0, 1)
        EXTRA_SLOTS = (2, 0)

        def wload(l, e, slot):
            base = slot * SLOT
            gu = RG(base, 4096).rearrange("p (k n) -> p k n", k=KD)
            dn = RG(base + 4096, 2048).rearrange("p (f n) -> p f n", f=2)
            one = bass.ds(e, 1)
            g = a["moe_w_gate"][l][one].rearrange("a (k p) f -> p (a k) f", p=128)
            u = a["moe_w_up"][l][one].rearrange("a (k p) f -> p (a k) f", p=128)
            d = a["moe_w_down"][l][one].rearrange("a (f p) n -> p (a f) n", p=128)
            return ((gu[:, :, 0:DE], g), (gu[:, :, DE:2 * DE], u), (dn, d))


        att = {n: sm(w) for n, w in dict(mx=4, nm=4, sums=4, rec=4, rl=4, oss=32, oms=32, osd=32, orstd=32, osc=8, lam=4, nlam=1,
                                         isc=1, dmx=3, dm=1, dnm=1, dsum=1, drec=1, drsc=1, combs=64, rss=1, rms=1, rsd=1,
                                         rrs=1, orn=128).items()}
        UNITS = [(h, i) for h in range(NH) for i in range(4)]
        WO_BANKS = (4, 5, 0, 1)
        N_UNITS = NSEQ // 2 * NPAGE
        LAG = 2
        FIRST_VALUES = 2 * NPAGE + LAG + 1
        QUAD0_VALUED = FIRST_VALUES + NPAGE

        def attention_pool(pool):
            pool.wait_ge(sem("k_mm"), at("k_mm", NH))
            pool.memset(qz[0][64:128, :, :], 0.0).then_inc(sem("qzero"), 1)
            pool.memset(qz[1][0:64, :, :], 0.0).then_inc(sem("qzero"), 1)
            pool.wait_ge(sem("v_mm"), at("v_mm", N_ROWS))
            pool.wait_ge(sem("qzero"), at("qzero", 2))
            pool.memset(RG(8192, 4096), 0.0).then_inc(sem("qzero"), 1)
            prompt_bias(pool)

        def attention_pe(pe):
            def key_head(h, k):
                w = RG(4096 * (h // 4), 4096).rearrange("p (k n) -> p k n", k=KD)
                mm = all_tokens(pe, 4 + 2 * (h % 2), w[:, k, 128 * (h % 4):128 * (h % 4) + 128], xT, k)
                if k == KD - 1:
                    mm.then_inc(sem("k_mm"), 1)

            def first_heads(k):
                pe.wait_ge(sem("w_att0"), at("w_att0", 16))
                key_head(0, k)
                key_head(1, k)
            turn_pe(pe, "kv", xhat, NT, turn=TURN_KV, turned=first_heads)
            for h in range(2, NH):
                if h == 4:
                    pe.wait_ge(sem("w_att1"), at("w_att1", 16))
                if h - 1 > 0:
                    pe.wait_ge(sem("kT"), at("kT", h - 1))
                for k in range(KD):
                    key_head(h, k)
            for c in range(2):
                pe.wait_ge(sem(f"w_att{2 + c}"), at(f"w_att{2 + c}", 16))
            n = 0
            for i in range(4):
                for c in range(2):
                    if n - 3 > 0:
                        pe.wait_ge(sem("v_done"), at("v_done", n - 3))
                    w = RG(4096 * (2 + c), 4096).rearrange("p (k n) -> p k n", k=KD)
                    for k in range(KD):
                        mm = pe.matmul(ps[n % 4][0:ROWS[i], :], xT[:, k, 128 * i:128 * i + ROWS[i]], w[:, k, :], start=(k == 0), stop=(k == KD - 1))
                    mm.then_inc(sem("v_mm"), 1)
                    n += 1
            if n - 3 > 0:
                pe.wait_ge(sem("v_done"), at("v_done", n - 3))
            sampled_rows(pe, ps[0], xTd, [RG(4096 * (2 + c), 4096).rearrange("p (k n) -> p k n", k=KD) for c in range(2)]).then_inc(sem("v_mm"), 1)
            pe.wait_ge(sem("kT"), at("kT", NH))
            n = 0
            for i in range(NT):
                for b in range(2):
                    if n - 3 > 0:
                        pe.wait_ge(sem("k_rows"), at("k_rows", n - 3))
                    for h in range(4 * b, 4 * b + 4):
                        mm = pe.transpose(ps[4 + n % 4][0:ROWS[i], 128 * (h % 4):128 * (h % 4) + 128], kT[:, h, 128 * i:128 * i + ROWS[i]], ident)
                    mm.then_inc(sem("k_back"), 1)
                    n += 1
            pe.wait_ge(sem("v_done"), at("v_done", N_ROWS))
            for h in range(NH):
                if h % 4 == 0:
                    pe.wait_ge(sem(f"w_att{4 + h // 4}"), at(f"w_att{4 + h // 4}", 16))
                if h - 1 > 0:
                    pe.wait_ge(sem("qz0"), at("qz0", h - 1))
                if h - 1 > 0:
                    pe.wait_ge(sem("qz1"), at("qz1", h - 1))
                w = RG(4096 * (4 + h // 4), 4096).rearrange("p (k n) -> p k n", k=KD)
                for k in range(KD):
                    mm = all_tokens(pe, 2 * (h % 2), w[:, k, 128 * (h % 4):128 * (h % 4) + 128], xqT, k)
                mm.then_inc(sem("q_mm"), 1)

            def scores(u):
                h, i = UNITS[u]
                if 2 * (u - 1) > 0:
                    pe.wait_ge(sem("scored"), at("scored", 2 * (u - 1)))
                for c in range(2):
                    mm = pe.matmul(ps[2 * (u % 2) + c][:, 0:128 * (i + 1)], qz[c][:, h, 128 * i:128 * i + 128], kT[:, h, 0:128 * (i + 1)], start=True, stop=True)
                mm.then_inc(sem("s_mm"), 1)
            pe.wait_ge(sem("qz0"), at("qz0", NH))
            pe.wait_ge(sem("qz1"), at("qz1", NH))
            pe.wait_ge(sem("k_rows"), at("k_rows", 2 * NT))
            scores(0)
            scores(1)

            def turn_weights(u):
                h, i = UNITS[u]
                pe.wait_ge(sem("weights"), at("weights", u + 1))
                if u - 1 > 0:
                    pe.wait_ge(sem("aT"), at("aT", u - 1))
                for b in range(i + 1):
                    mm = pe.transpose(ps[4 + u % 2][:, 128 * b:128 * b + 128], tbuf[:, u % 2, 0, 128 * b:128 * b + 128], ident)
                mm.then_inc(sem("a_turned"), 1)

            def output(u):
                h, i = UNITS[u]
                pe.wait_ge(sem("aT"), at("aT", u + 1))
                if u - 1 > 0:
                    pe.wait_ge(sem("o_rows"), at("o_rows", u - 1))
                for b in range(i + 1):
                    mm = pe.matmul(ps[6 + u % 2][:, 0:128], aT[:, u % 2, 128 * b:128 * b + 128], vtok[:, b, 128 * h:128 * h + 128], start=(b == 0), stop=(b == i))
                mm.then_inc(sem("o_mm"), 1)
            for u in range(len(UNITS) + 1):
                if u + 2 < len(UNITS):
                    scores(u + 2)
                if u < len(UNITS):
                    turn_weights(u)
                if u:
                    output(u - 1)
            pe.wait_ge(sem("o_rows"), at("o_rows", len(UNITS)))

            def page_turned(g):
                pe.wait_ge(sem(f"kpage{g % 4}"), at(f"kpage{g % 4}", 16 * (g // 4 + 1)))
                for b in range(2):
                    if g > 0:
                        pe.wait_ge(sem(f"kp{b}"), at(f"kp{b}", g))
                    for h in range(4):
                        c0 = 128 * (4 * b + h)
                        mm = pe.transpose(ps[b][:, 128 * h:128 * h + 128], kring[:, g % 4, c0:c0 + 128], ident)
                    mm.then_inc(sem("kturned_half"), 1) if b == 0 else mm.then_inc(sem("kturned"), 1)

            def page_scores(n, heads):
                pair, p = divmod(n, NPAGE)
                c0 = 128 * (p % 4)
                for h in heads:
                    for j in range(2):
                        mm = pe.matmul(ps[4 + p // 4][64 * j:64 * j + 64, c0:c0 + 128], qdec[:, 2 * pair + j, h, :], kp[n % 2][j][:, h, :], start=(h == 0), stop=(h == NH - 1))
                return mm

            def unit(n):
                for j in range(2):
                    if n < N_UNITS:
                        page_turned(2 * n + j)
                    if n:
                        if j == 0:
                            for b in range(2):
                                if 2 * n > 0:
                                    pe.wait_ge(sem(f"kp{b}"), at(f"kp{b}", 2 * n))
                            pair, p = divmod(n - 1, NPAGE)
                            if 3 * (pair - 1) + (1 if p < 4 else 2) > 0:
                                pe.wait_ge(sem("dscored"), at("dscored", 3 * (pair - 1) + (1 if p < 4 else 2)))
                        mm = page_scores(n - 1, range(4 * j, 4 * j + 4))
                if n:
                    mm.then_inc(sem("dec_scores"), 1)

            def new_scores(pair):
                if 3 * pair > 0:
                    pe.wait_ge(sem("dscored"), at("dscored", 3 * pair))
                for h in range(NH):
                    for j in range(2):
                        mm = pe.matmul(ps[6][64 * j:64 * j + 64, 0:NDEC], qdec[:, 2 * pair + j, h, :], kT[:, h, SEQ:NTOK], start=(h == 0), stop=(h == NH - 1))
                mm.then_inc(sem("new_scores"), 1)

            def pair_turned(pair):
                pe.wait_ge(sem("combs"), at("combs", pair + 1))
                if pair > 0:
                    pe.wait_ge(sem("aTd"), at("aTd", pair))
                if pair == 3:
                    pe.wait_ge(sem("odec"), at("odec", 1))
                for kk in range(NPAGE):
                    mm = pe.matmul(ps[7][:, 64 * kk:64 * kk + 64], tdec[:, pair % 2, 128 * kk:128 * kk + 128], att["combs"], start=True, stop=True)
                mm = pe.matmul(ps[6][0:NDEC, 64:128], tdec[:, pair % 2, PAST:NKEY], att["combs"], start=True, stop=True)
                mm.then_inc(sem("dT"), 1)

            def values_step(quad, p):
                if p == 0:
                    pe.wait_ge(sem("aTd"), at("aTd", 2 * (quad + 1)))
                    if 2 * quad > 0:
                        pe.wait_ge(sem("headed"), at("headed", 2 * quad))
                if p < NPAGE:
                    pe.wait_ge(sem(f"vpage{p % 2}"), at(f"vpage{p % 2}", 64 * (4 * quad + p // 2 + 1)))
                for c in range(2):
                    for j in range(4):
                        if p < NPAGE:
                            mm = pe.matmul(ps[2 + c][32 * j:32 * j + 32, :], aTd(quad, p)[:, 32 * j:32 * j + 32], vring[:, 4 * (p % 2) + j, 512 * c:512 * c + 512], start=(p == 0), stop=False)
                        else:
                            mm = pe.matmul(ps[2 + c][32 * j:32 * j + 32, :], aTd(quad, p)[0:NDEC, 32 * j:32 * j + 32], vtok[0:NDEC, 4, 512 * c:512 * c + 512], start=False, stop=True, tile_position=(0, 32 * j))
                mm.then_inc(sem("pv_mm" if p < NPAGE else "pv_all"), 1)

            def quad_turned(quad):
                pe.wait_ge(sem("orn"), at("orn", quad + 1))
                pe.wait_ge(sem("aTd"), at("aTd", 3 + quad))
                pe.transpose(ps[7][:, 0:128], att["orn"], ident).then_inc(sem("orn_t"), 1)
            new_scores(0)
            for n in range(N_UNITS + 1):
                unit(n)
                pair, p = divmod(n - LAG - NPAGE, NPAGE)
                if p == 0 and 0 <= pair < 3:
                    new_scores(pair + 1)
                    pair_turned(pair)
                if 0 <= n - FIRST_VALUES <= NPAGE:
                    values_step(0, n - FIRST_VALUES)
                if n == QUAD0_VALUED + 2:
                    quad_turned(0)
            turn_pe(pe, "o", otok, 4, dec=False, turn=TURN_O)
            pair_turned(3)
            wait_turned(pe, "o", dec=False)
            wo = [RG(4096 * c, 4096).rearrange("p (k n) -> p k n", k=KD) for c in range(2)]

            def wo_product(n):
                i, c = n // 2, n % 2
                if n - 3 > 0:
                    pe.wait_ge(sem("wo_add"), at("wo_add", n - 3))
                for k in range(KD):
                    mm = pe.matmul(ps[WO_BANKS[n % 4]], oT[:, k, 128 * i:128 * i + 128], wo[c][:, k, :], start=(k == 0), stop=(k == KD - 1))
                mm.then_inc(sem("wo_mm"), 1)
            values_step(1, 0)
            values_step(1, 1)
            for c in range(2):
                pe.wait_ge(sem(f"w_o{c}"), at(f"w_o{c}", 16))
            for p in range(2, NPAGE):
                wo_product(p - 2)
                values_step(1, p)
            values_step(1, NPAGE)
            wo_product(6)
            quad_turned(1)
            wo_product(7)
            pe.wait_ge(sem("odec"), at("odec", 2))
            pe.wait_ge(sem("wo_add"), at("wo_add", 5))
            sampled_rows(pe, ps[WO_BANKS[0]], lambda k: odec[:, k, :], wo).then_inc(sem("wo_mm"), 1)

        def attention_act(act):
            for i in range(NT):
                act.wait_ge(sem("collected@0"), at("collected@0", i + 1))
                row_squares(act, "kv", i)
            row_roots(act, "kv", NT - 1)
            turned_act(act, "kv", [(xT, P("g_kv")), (xqT, P("g_mix1"))], turn=TURN_KV)
            for h in range(NH):
                act.wait_ge(sem("k_mm"), at("k_mm", h + 1))
                act.copy(halves(kT[:, h, :]), two_banks(4 + 2 * (h % 2))).then_inc(sem("kT"), 1)
            for n in range(2 * NT):
                i, b = n // 2, n % 2
                act.wait_ge(sem("k_back"), at("k_back", n + 1))
                if b == 0 and i >= 2:
                    if 16 * (i // 2) > 0:
                        act.wait_ge(sem(f"k_out{i % 2}"), at(f"k_out{i % 2}", 16 * (i // 2)))
                act.copy(ktk[0:ROWS[i], i % 2, 512 * b:512 * b + 512], ps[4 + n % 4][0:ROWS[i], :]).then_inc(sem("k_rows"), 1)
            act.wait_ge(sem("qzero"), at("qzero", 3))
            for h in range(NH):
                act.wait_ge(sem("q_mm"), at("q_mm", h + 1))
                act.activation(qdec[0:64, :, h, 4 * h:4 * h + 4], ps[2 * (h % 2) + 1][0:64, SEQ - HTOK:HTOK].rearrange("p (s t) -> p s t", s=NSEQ), ACT.Copy, scale=HD ** -0.5)
                for c, (t0, t1) in enumerate(((0, HTOK), (HTOK, SEQ))):
                    i = act.activation(qz[0][0:64, h, t0:t1], ps[2 * (h % 2) + c][0:64, 0:t1 - t0], ACT.Copy, scale=HD ** -0.5)
                i.then_inc(sem("qz0"), 1)
            act.wait_ge(sem("lam_sum"), at("lam_sum", 1))
            act.activation(att["lam"][:, 2:4], att["lam"][:, 0:2], ACT.Exp).then_inc(sem("lam_exp"), 1)

            def exps(u):
                h, i = UNITS[u]
                act.wait_ge(sem("negmax"), at("negmax", u + 1))
                for c in range(2):
                    x = 2 * (u % 2) + c
                    t = tbuf[:, u % 2, c, 0:128 * (i + 1)]
                    act.activation(t, t, ACT.Exp, bias=att["nm"][:, x:x + 1], accum_out=att["sums"][:, x:x + 1]).then_inc(sem("exps"), 1)

            def square(u):
                h, i = UNITS[u]
                act.wait_ge(sem("o_rows"), at("o_rows", u + 1))
                if u - 7 > 0:
                    act.wait_ge(sem("oss"), at("oss", u - 7))
                act.activation(junk[:, 128 * (u % 8):128 * (u % 8) + 128], otok[:, i, 128 * h:128 * h + 128], ACT.Square,
                               accum_out=att["oss"][:, 8 * i + h:8 * i + h + 1]).then_inc(sem("oss"), 1)
            exps(0)
            for u, (h, i) in enumerate(UNITS):
                if u + 1 < len(UNITS):
                    exps(u + 1)
                act.wait_ge(sem("a_turned"), at("a_turned", u + 1))
                if u - 1 > 0:
                    act.wait_ge(sem("o_mm"), at("o_mm", u - 1))
                act.copy(aT[:, u % 2, 0:128 * (i + 1)], ps[4 + u % 2][:, 0:128 * (i + 1)]).then_inc(sem("aT"), 1)
                if u >= 3:
                    square(u - 3)
            for u in range(len(UNITS) - 3, len(UNITS)):
                square(u)
            act.wait_ge(sem("oms"), at("oms", 1))
            act.activation(att["osd"], att["oms"], ACT.Sqrt).then_inc(sem("osd"), 1)
            def exp_pair(pair):
                act.wait_ge(sem("dnm"), at("dnm", pair + 1))
                t = tdec[:, pair % 2, :]
                act.activation(t, t, ACT.Exp, bias=att["dnm"], accum_out=att["dsum"]).then_inc(sem("dexp"), 1)

            def turned_weights(pair):
                act.wait_ge(sem("dT"), at("dT", pair + 1))
                cols = slice(64 * (pair % 2), 64 * (pair % 2) + 64)
                groups = ps[7][:, :].rearrange("p (g r) -> p g r", g=NPAGE)
                if pair < 2:
                    act.copy(aTd0[:, 0:NPAGE, cols], groups)
                else:
                    act.copy(aTd1[:, 0:2, :, cols], groups[:, 0:6, :].rearrange("p (h g) r -> p h g r", h=2))
                    act.copy(aTd1[:, 2, 0:2, cols], groups[:, 6:NPAGE, :])
                act.copy(aTd(pair // 2, NPAGE)[0:NDEC, cols], ps[6][0:NDEC, 64:128]).then_inc(sem("aTd"), 1)

            def root(quad):
                act.wait_ge(sem("rms_row"), at("rms_row", quad + 1))
                act.activation(att["rsd"], att["rms"], ACT.Sqrt).then_inc(sem("rsd"), 1)
            for n in range(N_UNITS):
                for j in range(2):
                    act.wait_ge(sem("kturned"), at("kturned", 2 * n + j + 1))
                    if n - 1 > 0:
                        act.wait_ge(sem("dec_scores"), at("dec_scores", n - 1))
                    act.copy(kp[n % 2][j][:, 4:8, :], ps[1][:, :].rearrange("p (h n) -> p h n", h=4)).then_inc(sem("kp1"), 1)
                pair, p = divmod(n - NPAGE, NPAGE)
                if pair >= 0 and p == 1:
                    exp_pair(pair)
                if pair >= 0 and p == LAG + 1:
                    turned_weights(pair)
                if n == QUAD0_VALUED + 1:
                    root(0)
            exp_pair(3)
            turned_act(act, "o", [(oT, att["osc"])], dec=False, turn=TURN_O)
            turned_weights(3)
            for i in range(2):
                act.wait_ge(sem("wo_add"), at("wo_add", 2 * (i + 1)))
                row_squares(act, "ffn1", i)
            root(1)

        def attention_dve(v):
            lv = P("lams").rearrange("p (b c d) -> p b c d", b=2, c=2)
            for b in range(2):
                link(v, v.tensor_tensor(junk[:, 64 * b:64 * b + 64], lv[:, b, 0, :], lv[:, b, 1, :], ALU.mult))
                i = v.tensor_reduce(att["lam"][:, b:b + 1], junk[:, 64 * b:64 * b + 64], AX.X, ALU.add)
                if b == 0:
                    link(v, i)
            i.then_inc(sem("lam_sum"), 1)
            for h in range(NH):
                i = v.tensor_scalar(att["osc"][:, h:h + 1], P("subln"), 1.0 - LAM_INIT, None, ALU.mult)
            link(v, i)
            turned_dve(v, "kv", [(xT, P("g_kv")), (xqT, P("g_mix1"))], turn=TURN_KV)
            n = 0
            v.wait_ge(sem("t_kv"), at("t_kv", KD + 1))
            for i in range(4):
                for c in range(2):
                    v.wait_ge(sem("v_mm"), at("v_mm", n + 1))
                    v.tensor_copy(vtok[:, i, 512 * c:512 * c + 512], ps[n % 4]).then_inc(sem("v_done"), 1)
                    n += 1
            v.wait_ge(sem("v_mm"), at("v_mm", N_ROWS))
            for j in range(4):
                i = v.tensor_copy(vtok[0:NDEC, 4, 256 * j:256 * j + 256], ps[0][32 * j:32 * j + 32, 0:256])
            i.then_inc(sem("v_done"), 1)
            v.wait_ge(sem("qzero"), at("qzero", 3))
            for h in range(NH):
                v.wait_ge(sem("q_mm"), at("q_mm", h + 1))
                b0 = 2 * (h % 2)
                v.tensor_scalar(qdec[64:128, :, h, 32 + 4 * h:36 + 4 * h], ps[b0 + 1][64:128, SEQ - HTOK:HTOK].rearrange("p (s t) -> p s t", s=NSEQ), HD ** -0.5, None, ALU.mult)
                for c, (t0, t1) in enumerate(((0, HTOK), (HTOK, SEQ))):
                    i = v.tensor_scalar(qz[1][64:128, h, t0:t1], ps[b0 + c][64:128, 0:t1 - t0], HD ** -0.5, None, ALU.mult)
                i.then_inc(sem("qz1"), 1)
            v.wait_ge(sem("lam_exp"), at("lam_exp", 1))
            link(v, v.tensor_tensor(att["lam"][:, 0:1], att["lam"][:, 3:4], att["lam"][:, 2:3], ALU.subtract))
            link(v, v.tensor_scalar(att["nlam"], att["lam"][:, 0:1], -LAM_INIT, None, ALU.add))
            link(v, v.scalar_tensor_tensor(att["isc"], C("isc1"), att["nlam"], C("isc0"), ALU.mult, ALU.add))
            for b in range(2):
                v.wait_ge(sem(f"k_out{b}"), at(f"k_out{b}", (48, 32)[b]))

            def score(u):
                h, i = UNITS[u]
                v.wait_ge(sem("s_mm"), at("s_mm", u + 1))
                v.wait_ge(sem("biash"), at("biash", h + 1))
                if u - 1 > 0:
                    v.wait_ge(sem("a_turned"), at("a_turned", u - 1))
                n = 128 * (i + 1)
                for c in range(2):
                    x = 2 * (u % 2) + c
                    v.tensor_tensor_reduce(tbuf[:, u % 2, c, 0:n], ps[x][:, 0:n], biash[:, h % 2, 384 - 128 * i:384 - 128 * i + n], 1.0, -3e38,
                                           ALU.add, ALU.max, att["mx"][:, x:x + 1]).then_inc(sem("scored"), 1)
                v.wait_ge(sem("scored"), at("scored", 2 * (u + 1)))
                x = 2 * (u % 2)
                v.tensor_scalar(att["nm"][:, x:x + 2], att["mx"][:, x:x + 2], -1.0, None, ALU.mult).then_inc(sem("negmax"), 1)

            def weights(u):
                h, i = UNITS[u]
                n = 128 * (i + 1)
                x = 2 * (u % 2)
                v.wait_ge(sem("exps"), at("exps", 2 * (u + 1)))
                link(v, v.reciprocal(att["rec"][:, x:x + 2], att["sums"][:, x:x + 2]))
                link(v, v.tensor_tensor(att["rl"][:, x:x + 1], att["rec"][:, x + 1:x + 2], att["nlam"], ALU.mult))
                t0, t1 = tbuf[:, u % 2, 0, 0:n], tbuf[:, u % 2, 1, 0:n]
                link(v, v.tensor_scalar(t1, t1, att["rl"][:, x:x + 1], None, ALU.mult))
                v.scalar_tensor_tensor(t0, t0, att["rec"][:, x:x + 1], t1, ALU.mult, ALU.add).then_inc(sem("weights"), 1)

            def o_rows(u):
                h, i = UNITS[u]
                v.wait_ge(sem("o_mm"), at("o_mm", u + 1))
                v.tensor_copy(otok[:, i, 128 * h:128 * h + 128], ps[6 + u % 2][:, 0:128]).then_inc(sem("o_rows"), 1)
            score(0)
            for u in range(len(UNITS)):
                if u + 1 < len(UNITS):
                    score(u + 1)
                weights(u)
                if u >= 2:
                    o_rows(u - 2)
            o_rows(len(UNITS) - 2)
            o_rows(len(UNITS) - 1)
            v.wait_ge(sem("o_rows"), at("o_rows", len(UNITS)))
            v.sem_inc(sem("prompt_done"), 1)
            v.wait_ge(sem("oss"), at("oss", len(UNITS)))
            v.tensor_scalar(att["oms"], att["oss"], 1.0 / 128, EPS, ALU.mult, ALU.add).then_inc(sem("oms"), 1)
            v.wait_ge(sem("osd"), at("osd", 1))
            link(v, v.reciprocal(att["orstd"], att["osd"]))
            for i in range(4):
                head_ = otok[:, i, :].rearrange("p (h e) -> p h e", h=NH)
                v.tensor_tensor(head_, head_, att["orstd"][:, 8 * i:8 * i + 8].unsqueeze(2).broadcast_to([128, NH, 128]), ALU.mult).then_inc(sem("xh_o"), 1)
            v.wait_ge(sem("past_in"), at("past_in", 16))

            def biased(dst, bank, bias, x):
                v.tensor_tensor_reduce(dst, bank, bias, 1.0, -3e38, ALU.add, ALU.max, att["dmx"][:, x:x + 1]).then_inc(sem("dscored"), 1)

            def first_half(pair):
                v.wait_ge(sem("dec_scores"), at("dec_scores", NPAGE * pair + 4))
                if pair - 1 > 0:
                    v.wait_ge(sem("dT"), at("dT", pair - 1))
                biased(tdec[:, pair % 2, 0:512], ps[4][:, :], pastb[:, 0:512], 0)

            def pair_weights(pair):
                v.wait_ge(sem("dec_scores"), at("dec_scores", NPAGE * (pair + 1)))
                biased(tdec[:, pair % 2, 512:PAST], ps[5][:, :], pastb[:, 512:PAST], 1)
                v.wait_ge(sem("new_scores"), at("new_scores", pair + 1))
                biased(tdec[:, pair % 2, PAST:NKEY], ps[6][:, 0:NDEC], C("newbias")[:, NDEC * pair:NDEC * pair + NDEC], 2)
                v.wait_ge(sem("dscored"), at("dscored", 3 * (pair + 1)))
                link(v, v.tensor_reduce(att["dm"], att["dmx"], AX.X, ALU.max))
                v.tensor_scalar(att["dnm"], att["dm"], -1.0, None, ALU.mult).then_inc(sem("dnm"), 1)
                v.wait_ge(sem("dexp"), at("dexp", pair + 1))
                link(v, v.reciprocal(att["drec"], att["dsum"]))
                link(v, v.tensor_tensor(att["drsc"], att["drec"], att["isc"], ALU.mult))
                if pair > 0:
                    v.wait_ge(sem("dT"), at("dT", pair))
                v.tensor_scalar(att["combs"], C("comb"), att["drsc"], None, ALU.mult).then_inc(sem("combs"), 1)

            def own_heads(quad):
                v.wait_ge(sem("pv_all"), at("pv_all", quad + 1))
                hmk = C("headmask")
                kept = tdec[:, 0, 0:D]
                for c in range(2):
                    v.tensor_tensor(kept[:, 512 * c:512 * c + 512].rearrange("p (h e) -> p h e", h=4), ps[2 + c][:, :].rearrange("p (h e) -> p h e", h=4),
                                    hmk[:, 4 * c:4 * c + 4].unsqueeze(2).broadcast_to([128, 4, 128]), ALU.mult).then_inc(sem("headed"), 1)
                v.wait_ge(sem("headed"), at("headed", 2 * (quad + 1)))
                link(v, v.tensor_reduce(orow, kept.rearrange("p (h e) -> p e h", h=NH), AX.X, ALU.add))
                link(v, v.tensor_tensor(kept[:, 0:128], orow, orow, ALU.mult))
                link(v, v.tensor_reduce(att["rss"], kept[:, 0:128], AX.X, ALU.add))
                v.tensor_scalar(att["rms"], att["rss"], 1.0 / 128, EPS, ALU.mult, ALU.add).then_inc(sem("rms_row"), 1)

            def head_norm(quad):
                v.wait_ge(sem("rsd"), at("rsd", quad + 1))
                link(v, v.reciprocal(att["rrs"], att["rsd"]))
                v.tensor_scalar(att["orn"], orow, att["rrs"], None, ALU.mult).then_inc(sem("orn"), 1)

            def features(quad):
                v.wait_ge(sem("orn_t"), at("orn_t", quad + 1))
                dst = odec[:, :, 16 * quad:16 * quad + 16].rearrange("p h (s t) -> p s h t", s=4)
                for s in range(4):
                    i = v.tensor_scalar(dst[:, s, :, :], ps[7][:, 32 * s:32 * s + 32].rearrange("p (h t) -> p h t", h=NH), att["osc"][:, 0:1], None, ALU.mult)
                i.then_inc(sem("odec"), 1)
            for n in range(N_UNITS):
                for j in range(2):
                    v.wait_ge(sem("kturned_half"), at("kturned_half", 2 * n + j + 1))
                    if n - 1 > 0:
                        v.wait_ge(sem("dec_scores"), at("dec_scores", n - 1))
                    v.tensor_copy(kp[n % 2][j][:, 0:4, :], ps[0][:, :].rearrange("p (h n) -> p h n", h=4)).then_inc(sem("kp0"), 1)
                pair, p = divmod(n, NPAGE)
                if p == 5:
                    first_half(pair)
                if p == 1 and pair > 0:
                    pair_weights(pair - 1)
                if n == QUAD0_VALUED:
                    own_heads(0)
                if n == QUAD0_VALUED + 1:
                    head_norm(0)
                if n == QUAD0_VALUED + 3:
                    features(0)
            pair_weights(3)
            turned_dve(v, "o", [(oT, att["osc"])], dec=False, turn=TURN_O)
            for n in range(6):
                row_added(v, "wo", "ffn1", WO_BANKS, n)
            own_heads(1)
            head_norm(1)
            row_added(v, "wo", "ffn1", WO_BANKS, 6)
            features(1)
            row_added(v, "wo", "ffn1", WO_BANKS, 7)
            sampled_added(v, "wo", "ffn1", WO_BANKS)

        def att_chunk(sp, c):
            wkv = a["w_kv"].rearrange("(k p) n -> p k n", p=128)
            wq = a["attn_w_q"][0].rearrange("(k p) n -> p k n", p=128)
            src = wkv[:, :, 512 * c:512 * c + 512] if c < 4 else wq[:, :, 512 * (c - 4):512 * (c - 3)]
            sp.dma_start(RG(4096 * c, 4096).rearrange("p (k n) -> p k n", k=KD), src).then_inc(sem(f"w_att{c}"), 16)

        def attention_first_loads(sp):
            for c in range(3):
                sp.wait_ge(sem("down@0"), at("down@0", NE - 3 + (c > 0)))
                att_chunk(sp, c)

        def attention_loads(sp):
            sp.wait_ge(sem("collected@0"), at("collected@0", NT))
            for c in range(3, 6):
                att_chunk(sp, c)
            for i in range(NT):
                sp.wait_ge(sem("v_done"), at("v_done", min(2 * (i + 1), N_ROWS)))
                if i < 4:
                    sp.dma_start(o["v_prompt"][0, 128 * i:128 * i + 128].rearrange("p h e -> p (h e)"), vtok[:, i, :]).then_inc(out_sem, 16)
                else:
                    sp.dma_start(o["v_sample"].rearrange("s t h e -> (s t) (h e)"), vtok[0:NDEC, 4, :]).then_inc(out_sem, 16)
            for i in range(NT):
                sp.wait_ge(sem("k_rows"), at("k_rows", 2 * (i + 1)))
                n = ROWS[i]
                src = ktk[:, i % 2, :]
                if i < 4:
                    sp.dma_start(o["k_prompt"][0, 128 * i:128 * i + 128].rearrange("p h c d -> p (h c d)"), src).then_inc(sem(f"k_out{i % 2}"), 16)
                else:
                    sp.dma_start(o["k_sample"].rearrange("s t h c d -> (s t) (h c d)"), src[0:n, :]).then_inc(sem(f"k_out{i % 2}"), 16)
            n_out[0] += 16 * NT
            sp.wait_ge(sem("q_mm"), at("q_mm", NH))
            sp.dma_start(dist, a["c_dist"]).then_inc(sem("dist_in"), 16)
            sp.wait_ge(sem("pages_in"), at("pages_in", 16))
            sp.dma_start(pastb, a["c_past"]).then_inc(sem("past_in"), 16)
            ck = a["cache_k"].rearrange("n p h c d -> n p (h c d)")
            cvv = a["cache_v"].rearrange("n p h e -> n p (h e)")
            n_pool = a["cache_k"].shape[0]

            def page_in(src, dst, entry, s):
                reg = sp.value_load(pages[0:1, entry], min_val=0, max_val=n_pool - 1)
                sp.dma_start(dst, src[bass.ds(reg, 1)].rearrange("a p d -> p (a d)")).then_inc(s, 16)

            for u in range(4):
                page_in(ck, kring[:, u, :], slice(u, u + 1), sem(f"kpage{u}"))

            def key_groups(first, end):
                with sp.Fori(first, end) as g:
                    for u in range(4):
                        sp.wait_ge(sem("kturned"), at("kturned", 4 * g + (u - 3)))
                        page_in(ck, kring[:, u, :], bass.ds(4 * g + u, 1), sem(f"kpage{u}"))

            def values_in(n):
                if n - 1 > 0:
                    sp.wait_ge(sem("pv_mm"), at("pv_mm", n - 1))
                for j in range(4):
                    entry = NSEQ * NPAGE + 4 * n + j
                    page_in(cvv, vring[:, 4 * (n % 2) + j, :], slice(entry, entry + 1), sem(f"vpage{n % 2}"))
            key_groups(1, 6)
            sp.wait_ge(sem("prompt_done"), at("prompt_done", 1))
            values_in(0)
            key_groups(6, 8)
            values_in(1)
            key_groups(8, 11)
            for g in range(11, 16):
                for q in (2 * (g - 11), 2 * (g - 11) + 1):
                    if q < NPAGE:
                        values_in(q + 2)
                key_groups(g, g + 1)
            wo = a["attn_w_o"][0].rearrange("(k p) n -> p k n", p=128)
            for c in (1, 0):
                if c == 0:
                    sp.wait_ge(sem("dec_scores"), at("dec_scores", N_UNITS))
                sp.dma_start(RG(4096 * c, 4096).rearrange("p (k n) -> p k n", k=KD), wo[:, :, 512 * c:512 * c + 512]).then_inc(sem(f"w_o{c}"), 16)
            for n in range(10, 16):
                values_in(n)

        def prompt_bias(pool):
            pool.wait_ge(sem("dist_in"), at("dist_in", 16))
            for h in range(NH):
                if 8 * (h - 1) > 0:
                    pool.wait_ge(sem("scored"), at("scored", 8 * (h - 1)))
                pool.tensor_scalar(biash[:, h % 2, :], dist, 2.0 ** -(h + 1), None, ALU.mult).then_inc(sem("biash"), 1)

        def row_squares(act, tag, i):
            n = ROWS[i]
            act.activation(junk[0:n, :], resid[0:n, i, :], ACT.Square, accum_out=stat["ss"][0:n, i:i + 1]).then_inc(sem(f"ss_{tag}"), 1)
            if i:
                row_roots(act, tag, i - 1)
            act.wait_ge(sem(f"ss_{tag}"), at(f"ss_{tag}", i + 1))

        def row_roots(act, tag, i):
            n = ROWS[i]
            act.wait_ge(sem(f"ms_{tag}"), at(f"ms_{tag}", i + 1))
            act.activation(stat["sd"][0:n, i:i + 1], stat["ms"][0:n, i:i + 1], ACT.Sqrt).then_inc(sem(f"sd_{tag}"), 1)

        def mean_squares(v, tag, i):
            n = ROWS[i]
            v.wait_ge(sem(f"ss_{tag}"), at(f"ss_{tag}", i + 1))
            v.tensor_scalar(stat["ms"][0:n, i:i + 1], stat["ss"][0:n, i:i + 1], 1.0 / D, EPS, ALU.mult, ALU.add).then_inc(sem(f"ms_{tag}"), 1)

        def norm_rows(v, tag, i):
            n = ROWS[i]
            v.wait_ge(sem(f"sd_{tag}"), at(f"sd_{tag}", i + 1))
            link(v, v.reciprocal(stat["rstd"][0:n, i:i + 1], stat["sd"][0:n, i:i + 1]))
            if tag == "final":
                v.wait_ge(sem("gfinal_in"), at("gfinal_in", 16))
                v.scalar_tensor_tensor(resid[0:n, i, :], resid[0:n, i, :], stat["rstd"][0:n, i:i + 1], gfin[0:n, :], ALU.mult, ALU.mult).then_inc(sem("y_done"), 1)
                return
            if tag == "kv":
                v.wait_ge(sem("rows_out@0"), at("rows_out@0", 32))
            v.tensor_scalar(xhat[0:n, i, :], resid[0:n, i, :], stat["rstd"][0:n, i:i + 1], None, ALU.mult).then_inc(sem(f"xh_{tag}"), 1)

        def norm_step(v, tag, i):
            if 1 <= i <= NT:
                mean_squares(v, tag, i - 1)
            if i >= 2:
                norm_rows(v, tag, i - 2)

        TURN, TURN_KV, TURN_O = (0, 1, 4, 5), (0, 1, 3), (0, 1)

        def turn_pe(pe, tag, src, tiles, dec=True, turn=TURN, turned=None):
            pe.wait_ge(sem(f"xh_{tag}"), at(f"xh_{tag}", tiles))
            if dec:
                for k in range(KD):
                    mm = pe.transpose(ps[2][:, NDEC * k:NDEC * k + NDEC], src[0:NDEC, 4, 128 * k:128 * k + 128], ident[0:NDEC, 0:NDEC])
                mm.then_inc(sem(f"t_{tag}"), 1)

            def in_sbuf(k):
                pe.wait_ge(sem(f"ev{k % 2}_{tag}"), at(f"ev{k % 2}_{tag}", k // 2 + 1 + (dec and k % 2 == 0)))
            for k in range(KD + 2):
                if k < KD:
                    if k >= len(turn):
                        in_sbuf(k - len(turn))
                    for i in range(4):
                        mm = pe.transpose(ps[turn[k % len(turn)]][:, 128 * i:128 * i + 128], src[:, i, 128 * k:128 * k + 128], ident)
                    mm.then_inc(sem(f"t_{tag}"), 1)
                if turned and k >= 2:
                    in_sbuf(k - 2)
                    turned(k - 2)

        def turned_act(act, tag, outs, dec=True, turn=TURN):
            for k in range(1, KD, 2):
                act.wait_ge(sem(f"t_{tag}"), at(f"t_{tag}", k + 1 + dec))
                for dst, g in outs:
                    i = act.activation(dst[:, k, 0:SEQ], ps[turn[k % len(turn)]], ACT.Copy, scale=g[:, k:k + 1])
                i.then_inc(sem(f"ev1_{tag}"), 1)

        def turned_dve(v, tag, outs, dec=True, turn=TURN):
            if dec:
                v.wait_ge(sem(f"t_{tag}"), at(f"t_{tag}", 1))
                for dst, g in outs:
                    i = v.tensor_tensor(dst[:, :, SEQ:NTOK], ps[2][:, 0:KD * NDEC].rearrange("p (k t) -> p k t", k=KD),
                                        g[:, 0:KD].unsqueeze(2).broadcast_to([128, KD, NDEC]), ALU.mult)
                i.then_inc(sem(f"ev0_{tag}"), 1)
            for k in range(0, KD, 2):
                v.wait_ge(sem(f"t_{tag}"), at(f"t_{tag}", k + 1 + dec))
                for dst, g in outs:
                    i = v.tensor_scalar(dst[:, k, 0:SEQ], ps[turn[k % len(turn)]], g[:, k:k + 1], None, ALU.mult)
                i.then_inc(sem(f"ev0_{tag}"), 1)

        def wait_turned(eng, tag, dec=True):
            eng.wait_ge(sem(f"ev0_{tag}"), at(f"ev0_{tag}", KD // 2 + dec))
            eng.wait_ge(sem(f"ev1_{tag}"), at(f"ev1_{tag}", KD // 2))

        chain = [0]

        def link(v, ins):
            chain[0] += 1
            ins.then_inc(sem("dve_chain"), 1)
            v.wait_ge(sem("dve_chain"), at("dve_chain", chain[0]))

        def sampled_rows(pe, bank, x, w):
            for k in range(KD):
                for j in range(4):
                    mm = pe.matmul(bank[32 * j:32 * j + 32, 0:256], x(k), w[j // 2][:, k, 256 * (j % 2):256 * (j % 2) + 256], start=(k == 0), stop=(k == KD - 1), tile_position=(0, 32 * j))
            return mm

        PW2_BANKS = (2, 3, 4, 5)

        def pw2_rows(pe):
            w = [RG(c * SLOT, 4096).rearrange("p (k n) -> p k n", k=KD) for c in range(2)]

            def product(n, k):
                i, c = n // 2, n % 2
                mm = pe.matmul(ps[PW2_BANKS[n % 4]], xT[:, k, 128 * i:128 * i + 128], w[c][:, k, :], start=(k == 0), stop=(k == KD - 1))
                if k == KD - 1:
                    mm.then_inc(sem("pw2_mm"), 1)
            for k in range(KD):
                pe.wait_ge(sem("conv_h"), at("conv_h", k + 1))
                for n in range(4):
                    product(n, k)
            for n in range(4, 8):
                if n - 3 > 0:
                    pe.wait_ge(sem("pw2_add"), at("pw2_add", n - 3))
                for k in range(KD):
                    product(n, k)
            pe.wait_ge(sem("pw2_add"), at("pw2_add", 5))
            sampled_rows(pe, ps[PW2_BANKS[0]], xTd, w).then_inc(sem("pw2_mm"), 1)

        def row_added(v, tag, norm, at_banks, n):
            i, c = n // 2, n % 2
            v.wait_ge(sem(f"{tag}_mm"), at(f"{tag}_mm", n + 1))
            res = resid[:, i, 512 * c:512 * c + 512]
            v.tensor_tensor(res, ps[at_banks[n % 4]], res, ALU.add).then_inc(sem(f"{tag}_add"), 1)
            if c:
                norm_step(v, norm, i)

        def sampled_added(v, tag, norm, at_banks):
            v.wait_ge(sem(f"{tag}_mm"), at(f"{tag}_mm", N_ROWS))
            for j in range(4):
                res = resid[0:NDEC, 4, 256 * j:256 * j + 256]
                i = v.tensor_tensor(res, ps[at_banks[0]][32 * j:32 * j + 32, 0:256], res, ALU.add)
            i.then_inc(sem(f"{tag}_add"), 1)
            for i in range(4, NT + 2):
                norm_step(v, norm, i)

        def keep_clock(pe, n):
            for _ in range(n):
                pe.matmul(ps[7], ident, con[:, 0:512], start=True, stop=True)

        def all_tokens(pe, b, w, x, k):
            for c in range(2):
                mm = pe.matmul(ps[b + c][:, 0:HTOK], w, x[:, k, HTOK * c:HTOK * c + HTOK], start=(k == 0), stop=(k == KD - 1))
            return mm

        def moe_pe(pe, l):
            wr = P(f"wr{l}").rearrange("p (k n) -> p k n", k=KD)

            def logits(k):
                for i in (0, 4, 1, 2, 3):
                    mm = pe.matmul(ps[3][0:ROWS[i], 20 * i:20 * i + 20], xT[:, k, 128 * i:128 * i + ROWS[i]], wr[:, k, :], start=(k == 0 and i == 0), stop=(k == KD - 1 and i == 3))
                if k == KD - 1:
                    mm.then_inc(sem(f"logits@{l}"), 1)
            keep_clock(pe, 5)
            turn_pe(pe, f"ffn{l}", xhat, NT, turned=logits)
            pe.wait_ge(sem(f"chosen@{l}"), at(f"chosen@{l}", 1))
            for i in range(NT):
                for q in range(i + 1):
                    n = ROWS[q]
                    mm = pe.matmul(ps[4][0:ROWS[i], NE * i:NE * i + NE], count[0:n, int(q < i), 0:ROWS[i]], chosen[0:n, q, :], start=(q == 0), stop=(q == i))
            for q in range(NT):
                mm = pe.matmul(ps[4][:, NE * NT:NE * NT + NE], count[0:ROWS[q], 1, :], chosen[0:ROWS[q], q, :], start=(q == 0), stop=(q == NT - 1))
            mm.then_inc(sem(f"ranks@{l}"), 1)

            keep_clock(pe, 28)

            def turn(e, par_, half):
                pe.wait_ge(sem(f"xg_{par_}@{l}"), at(f"xg_{par_}@{l}", 16 * (half + 1)))
                for k in range(KD):
                    mm = pe.transpose(ps[k // 4][:, 128 * (k % 4):128 * (k % 4) + 128], xg[:, par_, 128 * k:128 * k + 128], ident)
                mm.then_inc(sem(f"turned@{l}"), 1)

            def gate_up(e, slot, par_, quarter):
                pe.wait_ge(sem(f"w_moe_{slot}@{l}"), at(f"w_moe_{slot}@{l}", 48 * (quarter + 1)))
                pe.wait_ge(sem(f"xgT@{l}"), at(f"xgT@{l}", 2 * (e + 1)))
                if e - 1 > 0:
                    pe.wait_ge(sem(f"hidden@{l}"), at(f"hidden@{l}", e - 1))
                gu = RG(slot * SLOT, 4096).rearrange("p (k n) -> p k n", k=KD)
                for k in range(KD):
                    mm = pe.matmul(ps[2 + par_][:, :], xgT[:, k, :], gu[:, k, :], start=(k == 0), stop=(k == KD - 1))
                mm.then_inc(sem(f"gu@{l}"), 1)

            def hidden_turn(e, par_):
                pe.wait_ge(sem(f"hidden@{l}"), at(f"hidden@{l}", e + 1))
                for f in range(2):
                    mm = pe.transpose(ps[4][:, 128 * f:128 * f + 128], hm[:, par_, 128 * f:128 * f + 128], ident)
                mm.then_inc(sem(f"ht@{l}"), 1)

            def down(e, slot):
                pe.wait_ge(sem(f"hT@{l}"), at(f"hT@{l}", e + 1))
                if e > 0:
                    pe.wait_ge(sem(f"y_a@{l}"), at(f"y_a@{l}", e))
                if e > 0:
                    pe.wait_ge(sem(f"y_v@{l}"), at(f"y_v@{l}", e))
                dn = RG(slot * SLOT + 4096, 2048).rearrange("p (f n) -> p f n", f=2)
                for c in range(2):
                    for f in range(2):
                        mm = pe.matmul(ps[5 + c][:, :], hT[:, f, :], dn[:, f, 512 * c:512 * c + 512], start=(f == 0), stop=(f == 1))
                mm.then_inc(sem(f"down@{l}"), 1)

            turn(0, 0, 0)
            gate_up(0, 0, 0, 0)
            turn(1, 1, 0)
            for e in range(1, NE):
                gate_up(e, e % 4, e % 2, e // 4)
                hidden_turn(e - 1, (e - 1) % 2)
                if e < NE - 1:
                    turn(e + 1, (e + 1) % 2, (e + 1) // 2)
                down(e - 1, (e - 1) % 4)
            hidden_turn(NE - 1, 1)
            down(NE - 1, 3)

            pe.wait_ge(sem(f"extra_tab@{l}"), at(f"extra_tab@{l}", 1))
            n_extra = pe.value_load(extra_tab[0:1, EXTRA:EXTRA + 1], min_val=0, max_val=EXTRA)
            for x in range(EXTRA):
                with pe.If(n_extra > x):
                    slot = EXTRA_SLOTS[l] + x % 2
                    gu = RG(slot * SLOT, 4096).rearrange("p (k n) -> p k n", k=KD)
                    dn = RG(slot * SLOT + 4096, 2048).rearrange("p (f n) -> p f n", f=2)
                    done = sem(f"x{l}_pe")
                    pe.wait_ge(sem(f"x{l}_rows"), at(f"x{l}_rows", 16 * (x + 1)))
                    for k in range(KD):
                        mm = pe.transpose(ps[k // 4][:, 128 * (k % 4):128 * (k % 4) + 128], xg[:, 0, 128 * k:128 * k + 128], ident)
                    mm.then_inc(done, 1)
                    pe.wait_ge(sem(f"x{l}_w{x % 2}"), at(f"x{l}_w{x % 2}", 48 * (x // 2 + 1)))
                    pe.wait_ge(sem(f"x{l}_dve"), at(f"x{l}_dve", 3 * x + 1))
                    if x == 0:
                        pe.wait_ge(sem(f"hidden@{l}"), at(f"hidden@{l}", NE))
                    for k in range(KD):
                        mm = pe.matmul(ps[2][:, :], xgT[:, k, :], gu[:, k, :], start=(k == 0), stop=(k == KD - 1))
                    mm.then_inc(done, 1)
                    pe.wait_ge(sem(f"x{l}_dve"), at(f"x{l}_dve", 3 * x + 2))
                    for f in range(2):
                        mm = pe.transpose(ps[4][:, 128 * f:128 * f + 128], hm[:, 0, 128 * f:128 * f + 128], ident)
                    mm.then_inc(done, 1)
                    pe.wait_ge(sem(f"x{l}_act"), at(f"x{l}_act", 3 * x + 2))
                    if x == 0:
                        pe.wait_ge(sem(f"y_a@{l}"), at(f"y_a@{l}", NE))
                        pe.wait_ge(sem(f"y_v@{l}"), at(f"y_v@{l}", NE))
                    else:
                        if 3 * x > 0:
                            pe.wait_ge(sem(f"x{l}_dve"), at(f"x{l}_dve", 3 * x))
                    for c in range(2):
                        for f in range(2):
                            mm = pe.matmul(ps[5 + c][:, :], hT[:, f, :], dn[:, f, 512 * c:512 * c + 512], start=(f == 0), stop=(f == 1))
                    mm.then_inc(done, 1)

        def moe_act(act, l):
            turned_act(act, f"ffn{l}", [(xT, P(f"g_ffn{l}"))])
            act.wait_ge(sem(f"gd@{l}"), at(f"gd@{l}", 1))
            act.activation(r["gex"], r["gd"], ACT.Exp).then_inc(sem(f"gex@{l}"), 1)
            act.wait_ge(sem(f"ed@{l}"), at(f"ed@{l}", 1))
            act.activation(r["eex"], r["ed"], ACT.Exp).then_inc(sem(f"eex@{l}"), 1)

            def silu(e, par_):
                act.wait_ge(sem(f"gu@{l}"), at(f"gu@{l}", e + 1))
                if e - 1 > 0:
                    act.wait_ge(sem(f"hidden@{l}"), at(f"hidden@{l}", e - 1))
                act.activation(sil[:, par_, :], ps[2 + par_][:, 0:DE], ACT.Silu).then_inc(sem(f"silu@{l}"), 1)

            def finish(e, par_):
                act.wait_ge(sem(f"ht@{l}"), at(f"ht@{l}", e + 1))
                if e > 0:
                    act.wait_ge(sem(f"down@{l}"), at(f"down@{l}", e))
                act.copy(hT[:, :, :].rearrange("p f s -> p (f s)"), ps[4][:, 0:256]).then_inc(sem(f"hT@{l}"), 1)
                act.wait_ge(sem(f"down@{l}"), at(f"down@{l}", e + 1))
                if e >= 2:
                    if 16 * (e // 2) > 0:
                        act.wait_ge(sem(f"y_out_{par_}@{l}"), at(f"y_out_{par_}@{l}", 16 * (e // 2)))
                act.copy(yrow[:, par_, 512:1024], ps[6][:, :]).then_inc(sem(f"y_a@{l}"), 1)
                act.wait_ge(sem(f"y_a@{l}"), at(f"y_a@{l}", e + 1))
                act.wait_ge(sem(f"y_v@{l}"), at(f"y_v@{l}", e + 1))
                yd = scratch["y"][0:MAIN].rearrange("(q e) d -> q e d", e=NE)
                act.dma_start(yd[0:128, e, :], yrow[:, par_, :]).then_inc(sem(f"y_out_{par_}@{l}"), 16)
            silu(0, 0)
            for e in range(1, NE):
                silu(e, e % 2)
                finish(e - 1, (e - 1) % 2)
            finish(NE - 1, 1)
            act.wait_ge(sem(f"extra_tab@{l}"), at(f"extra_tab@{l}", 1))
            n_extra = act.value_load(extra_tab[0:1, EXTRA:EXTRA + 1], min_val=0, max_val=EXTRA)
            for x in range(EXTRA):
                with act.If(n_extra > x):
                    done = sem(f"x{l}_act")
                    act.wait_ge(sem(f"x{l}_pe"), at(f"x{l}_pe", 4 * x + 2))
                    act.activation(sil[:, 0, :], ps[2][:, 0:DE], ACT.Silu).then_inc(done, 1)
                    act.wait_ge(sem(f"x{l}_pe"), at(f"x{l}_pe", 4 * x + 3))
                    act.copy(hT[:, :, :].rearrange("p f s -> p (f s)"), ps[4][:, 0:256]).then_inc(done, 1)
                    act.wait_ge(sem(f"x{l}_pe"), at(f"x{l}_pe", 4 * x + 4))
                    if x == 0:
                        act.wait_ge(sem(f"y_out_0@{l}"), at(f"y_out_0@{l}", 16 * NE // 2))
                    else:
                        if 16 * x > 0:
                            act.wait_ge(sem(f"x{l}_y"), at(f"x{l}_y", 16 * x))
                    act.copy(yrow[:, 0, 512:1024], ps[6][:, :]).then_inc(done, 1)
                    act.wait_ge(sem(f"x{l}_act"), at(f"x{l}_act", 3 * x + 3))
                    act.wait_ge(sem(f"x{l}_dve"), at(f"x{l}_dve", 3 * x + 3))
                    act.dma_start(scratch["y"][MAIN:SLOTS].rearrange("(p x) d -> p x d", p=128)[:, x, :], yrow[:, 0, :]).then_inc(sem(f"x{l}_y"), 16)

        def moe_dve(v, l):
            turned_dve(v, f"ffn{l}", [(xT, P(f"g_ffn{l}"))])
            link(v, v.memset(WK(6400, 100), 0.0))
            link(v, v.memset(r["rank"], 0.0))
            v.wait_ge(sem(f"logits@{l}"), at(f"logits@{l}", 1))
            br = P(f"br{l}")
            link(v, v.tensor_tensor(logit[:, 0:4, :], ps[3][:, 0:80].rearrange("p (i n) -> p i n", i=4),
                                    br.unsqueeze(1).broadcast_to([128, 4, 20]), ALU.add))
            link(v, v.tensor_tensor(logit[0:NDEC, 4, :], ps[3][0:NDEC, 80:100], br[0:NDEC, :], ALU.add))
            G = logit[:, :, 0:NG]
            E_ = logit[:, :, NG:].rearrange("p i (g e) -> p i e g", g=NG)
            v4 = {n: r[n].rearrange("p (i n) -> p i n", i=NT) for n in
                  ("geq", "gsel", "goh", "gd", "gex", "es", "ed", "eex", "pe", "eq1", "sel1", "oh1", "pe2", "eq2", "sel2", "oh2")}

            def b4(x):
                return x.unsqueeze(2).broadcast_to([128, NT, 4])
            rev = C("rev4").unsqueeze(1).broadcast_to([128, NT, 4])

            def first_max(vals, mx, eq, sel, smx, oh):
                link(v, v.tensor_reduce(r[mx], vals, AX.X, ALU.max))
                link(v, v.tensor_tensor(v4[eq], vals, b4(r[mx]), ALU.is_equal))
                link(v, v.tensor_tensor(v4[sel], v4[eq], rev, ALU.mult))
                link(v, v.tensor_reduce(r[smx], v4[sel], AX.X, ALU.max))
                link(v, v.tensor_tensor(v4[oh], v4[sel], b4(r[smx]), ALU.is_equal))
            first_max(G, "gmax", "geq", "gsel", "gmx", "goh")
            v.tensor_tensor(v4["gd"], G, b4(r["gmax"]), ALU.subtract).then_inc(sem(f"gd@{l}"), 1)
            et = r["etmp"].rearrange("p (i e g) -> p i e g", i=NT, e=EPG)
            link(v, v.tensor_tensor(et, E_, v4["goh"].unsqueeze(2).broadcast_to([128, NT, EPG, NG]), ALU.mult))
            link(v, v.tensor_reduce(v4["es"], et, AX.X, ALU.add))
            link(v, v.tensor_reduce(r["em"], v4["es"], AX.X, ALU.max))
            v.tensor_tensor(v4["ed"], v4["es"], b4(r["em"]), ALU.subtract).then_inc(sem(f"ed@{l}"), 1)
            v.wait_ge(sem(f"gex@{l}"), at(f"gex@{l}", 1))
            link(v, v.tensor_reduce(r["gsum"], v4["gex"], AX.X, ALU.add))
            link(v, v.reciprocal(r["pg"], r["gsum"]))
            v.wait_ge(sem(f"eex@{l}"), at(f"eex@{l}", 1))
            link(v, v.tensor_reduce(r["esum"], v4["eex"], AX.X, ALU.add))
            link(v, v.reciprocal(r["er"], r["esum"]))
            link(v, v.tensor_tensor(v4["pe"], v4["eex"], b4(r["er"]), ALU.mult))
            first_max(v4["pe"], "p1", "eq1", "sel1", "mx1", "oh1")
            link(v, v.scalar_tensor_tensor(r["pe2"], r["oh1"], -2.0, r["pe"], ALU.mult, ALU.add))
            first_max(v4["pe2"], "p2", "eq2", "sel2", "mx2", "oh2")
            for oh, full in (("oh1", "OH1"), ("oh2", "OH2")):
                link(v, v.tensor_tensor(r[full].rearrange("p (i g e) -> p i g e", i=NT, g=NG),
                                        v4["goh"].unsqueeze(3).broadcast_to([128, NT, NG, EPG]),
                                        v4[oh].unsqueeze(2).broadcast_to([128, NT, NG, EPG]), ALU.mult))
            v.tensor_tensor(chosen[:, :, :].rearrange("p i e -> p (i e)"), r["OH1"], r["OH2"], ALU.add).then_inc(sem(f"chosen@{l}"), 1)
            link(v, v.tensor_tensor(r["s12"], r["p1"], r["p2"], ALU.add))
            link(v, v.reciprocal(r["rs"], r["s12"]))
            link(v, v.tensor_tensor(r["rsg"], r["rs"], r["pg"], ALU.mult))
            v.tensor_tensor(r["gate1"], r["p1"], r["rsg"], ALU.mult)
            link(v, v.tensor_tensor(r["gate2"], r["p2"], r["rsg"], ALU.mult))
            v.wait_ge(sem(f"ranks@{l}"), at(f"ranks@{l}", 1))
            rk = r["rank"].rearrange("p (i e) -> p i e", i=NT)
            link(v, v.tensor_copy(rk[:, 0:4, :], ps[4][:, 0:64].rearrange("p (i e) -> p i e", i=4)))
            link(v, v.tensor_copy(rk[0:NDEC, 4, :], ps[4][0:NDEC, 64:80]))
            link(v, v.tensor_copy(r["cnt"], ps[4][:, 80:96]))
            a_, b_ = r["nx"], r["nx2"]
            link(v, v.tensor_scalar(a_, r["cnt"], 128.0, None, ALU.is_gt))
            for q in range(2, 5):
                link(v, v.scalar_tensor_tensor(b_, r["cnt"], 128.0 * q, a_, ALU.is_gt, ALU.add))
                a_, b_ = b_, a_
            up = WK(7600, 256).rearrange("p (e f) -> p e f", e=NE)
            link(v, v.tensor_tensor(up, a_.unsqueeze(1).broadcast_to([128, NE, NE]), C("upto").rearrange("p (e f) -> p e f", e=NE), ALU.mult))
            link(v, v.tensor_reduce(r["cx"], up, AX.X, ALU.add))
            link(v, v.tensor_tensor(r["px"], r["cx"], a_, ALU.subtract))
            link(v, v.tensor_scalar(r["xbase"], r["px"], float(MAIN - 1), None, ALU.add))

            def per_token(x):
                return x.unsqueeze(1).broadcast_to([128, NT, NE])
            main = r["slot"].rearrange("p (i e) -> p i e", i=NT)
            link(v, v.scalar_tensor_tensor(main, rk, float(NE), per_token(C("expert")), ALU.mult, ALU.add))
            a_, b_ = r["ext"], r["diff"]
            link(v, v.tensor_scalar(a_, r["rank"], 128.0, None, ALU.is_ge))
            for q in range(2, 5):
                link(v, v.scalar_tensor_tensor(b_, r["rank"], 128.0 * q, a_, ALU.is_ge, ALU.add))
                a_, b_ = b_, a_
            link(v, v.tensor_scalar(b_, a_, float(1 - 128 * EXTRA), None, ALU.mult))
            link(v, v.scalar_tensor_tensor(r["ext"], r["rank"], float(EXTRA), b_, ALU.mult, ALU.add))
            ext = r["ext"].rearrange("p (i e) -> p i e", i=NT)
            link(v, v.tensor_tensor(ext, ext, per_token(r["xbase"]), ALU.add))
            link(v, v.tensor_tensor(r["diff"], r["ext"], r["slot"], ALU.subtract))
            link(v, v.scalar_tensor_tensor(r["ext"], r["rank"], 128.0, r["diff"], ALU.is_ge, ALU.mult))
            link(v, v.tensor_tensor(r["slot"], r["slot"], r["ext"], ALU.add))
            for c, (oh, s) in enumerate((("OH1", "s1"), ("OH2", "s2"))):
                link(v, v.tensor_tensor(r["t1"], r[oh], r["slot"], ALU.mult))
                link(v, v.tensor_reduce(r[s], r["t1"].rearrange("p (i e) -> p i e", i=NT), AX.X, ALU.add))
                v.tensor_copy(slot_i[:, c, :], r[s]).then_inc(sem(f"slots@{l}"), 1)
            cmp = r["cmp"].rearrange("p (x e) -> p x e", x=EXTRA)
            link(v, v.tensor_tensor(cmp, r["cx"].unsqueeze(1).broadcast_to([128, EXTRA, NE]), C("tile").unsqueeze(2).broadcast_to([128, EXTRA, NE]), ALU.is_le))
            link(v, v.tensor_reduce(r["xe"][:, 0:EXTRA], cmp, AX.X, ALU.add))
            link(v, v.tensor_scalar(r["xe"][:, 0:EXTRA], r["xe"][:, 0:EXTRA], float(NE - 1), None, ALU.min))
            link(v, v.tensor_copy(r["xe"][:, EXTRA:EXTRA + 1], r["cx"][:, NE - 1:NE]))
            v.tensor_copy(extra_tab[:, :], r["xe"]).then_inc(sem(f"extra_tab@{l}"), 1)

            gT = P(f"g_ffn{l}")

            def xgT_out(e):
                v.wait_ge(sem(f"turned@{l}"), at(f"turned@{l}", e + 1))
                if e > 0:
                    v.wait_ge(sem(f"gu@{l}"), at(f"gu@{l}", e))
                for b in range(2):
                    v.tensor_tensor(xgT[:, 4 * b:4 * b + 4, :], ps[b][:, :].rearrange("p (k s) -> p k s", k=4),
                                    gT[:, 4 * b:4 * b + 4].unsqueeze(2).broadcast_to([128, 4, 128]), ALU.mult).then_inc(sem(f"xgT@{l}"), 1)

            def hidden(e, par_):
                v.wait_ge(sem(f"silu@{l}"), at(f"silu@{l}", e + 1))
                if e - 1 > 0:
                    v.wait_ge(sem(f"ht@{l}"), at(f"ht@{l}", e - 1))
                v.tensor_tensor(hm[:, par_, :], ps[2 + par_][:, DE:2 * DE], sil[:, par_, :], ALU.mult).then_inc(sem(f"hidden@{l}"), 1)

            def y_half(e, par_):
                v.wait_ge(sem(f"down@{l}"), at(f"down@{l}", e + 1))
                if e >= 2:
                    if 16 * (e // 2) > 0:
                        v.wait_ge(sem(f"y_out_{par_}@{l}"), at(f"y_out_{par_}@{l}", 16 * (e // 2)))
                v.tensor_copy(yrow[:, par_, 0:512], ps[5][:, :]).then_inc(sem(f"y_v@{l}"), 1)
            xgT_out(0)
            xgT_out(1)
            hidden(0, 0)
            for e in range(1, NE):
                if e < NE - 1:
                    xgT_out(e + 1)
                y_half(e - 1, (e - 1) % 2)
                hidden(e, e % 2)
            y_half(NE - 1, 1)
            n_extra = v.value_load(extra_tab[0:1, EXTRA:EXTRA + 1], min_val=0, max_val=EXTRA)
            for x in range(EXTRA):
                with v.If(n_extra > x):
                    done = sem(f"x{l}_dve")
                    v.wait_ge(sem(f"x{l}_pe"), at(f"x{l}_pe", 4 * x + 1))
                    for b in range(2):
                        i = v.tensor_tensor(xgT[:, 4 * b:4 * b + 4, :], ps[b][:, :].rearrange("p (k s) -> p k s", k=4),
                                            gT[:, 4 * b:4 * b + 4].unsqueeze(2).broadcast_to([128, 4, 128]), ALU.mult)
                    i.then_inc(done, 1)
                    v.wait_ge(sem(f"x{l}_act"), at(f"x{l}_act", 3 * x + 1))
                    v.tensor_tensor(hm[:, 0, :], ps[2][:, DE:2 * DE], sil[:, 0, :], ALU.mult).then_inc(done, 1)
                    v.wait_ge(sem(f"x{l}_pe"), at(f"x{l}_pe", 4 * x + 4))
                    if x == 0:
                        v.wait_ge(sem(f"y_out_0@{l}"), at(f"y_out_0@{l}", 16 * NE // 2))
                    else:
                        if 16 * x > 0:
                            v.wait_ge(sem(f"x{l}_y"), at(f"x{l}_y", 16 * x))
                    v.tensor_copy(yrow[:, 0, 0:512], ps[5][:, :]).then_inc(done, 1)
            for i in range(NT):
                n = ROWS[i]
                v.wait_ge(sem(f"ygat_{i % 3}@{l}"), at(f"ygat_{i % 3}@{l}", 32 * (i // 3 + 1)))
                res = resid[0:n, i, :]
                link(v, v.scalar_tensor_tensor(res, ygat[0:n, i % 3, 0, :], r["gate1"][0:n, i:i + 1], res, ALU.mult, ALU.add))
                v.scalar_tensor_tensor(res, ygat[0:n, i % 3, 1, :], r["gate2"][0:n, i:i + 1], res, ALU.mult, ALU.add).then_inc(sem(f"collected@{l}"), 1)
                norm_step(v, ("kv", "final")[l], i)
            for i in range(NT, NT + 2):
                norm_step(v, ("kv", "final")[l], i)

        block = ctx.enter_context(nc.Block())

        @block.sync
        def _(sp):
            xp = a["x_prompt"][0].rearrange("(i p) d -> p i d", p=128)
            for i in range(2):
                sp.dma_start(resid[:, 2 * i:2 * i + 2, :], xp[:, 2 * i:2 * i + 2, :]).then_inc(sem(f"x_in{i}"), 16)
            sp.dma_start(con[:, :], a["c_table"]).then_inc(sem("con_in"), 16)
            sp.dma_start(resid[0:NDEC, 4, :], a["x_sample"].rearrange("s t d -> (s t) d")).then_inc(sem("x_in2"), 16)
            sp.dma_start(par[:, :], a["params"]).then_inc(sem("par_in"), 16)
            w1 = a["conv_w_pw1"][0].rearrange("(k p) (b n) -> p k b n", p=128, b=2)
            for c in range(4):
                dst = RG(c * SLOT, 4096).rearrange("p (k b n) -> p k b n", k=KD, b=2)
                for b in range(2):
                    sp.dma_start(dst[:, :, b, :], w1[:, :, b, 256 * c:256 * c + 256]).then_inc(sem(f"w_pw1_{c}"), 16)
                if c == 0:
                    sp.dma_start(state[0:120, :, :], a["state_conv"][0].rearrange("(a s) t d -> (s t) a d", a=2)).then_inc(sem("state_in"), 16)
            sp.wait_ge(sem("extra_zero"), at("extra_zero", 1))
            for x in range(EXTRA):
                sp.dma_start(scratch["y"][MAIN + 128 * x:MAIN + 128 * x + 128], last_p).then_inc(sem("y_zero"), 16)
            sp.dma_start(bpw2, a["b_pw2_rows"]).then_inc(sem("bpw2_in"), 16)
            sp.dma_start(ids[:, :], a["c_ids"]).then_inc(sem("ids_in"), 16)
            sp.dma_start(pages[:, :], a["page_order"]).then_inc(sem("pages_in"), 16)
            for l in LAYERS:
                sp.dma_start(scratch[f"owner{l}"].rearrange("(p n) x -> p (n x)", p=128), a["c_zero"]).then_inc(sem("owner_zero"), 16)
            cs = o["conv_sample"][0]
            sp.dma_start(cs[:, 0:PASTC - DSEQ, :], a["state_conv"][0][:, DSEQ:, :]).then_inc(out_sem, 16)
            w2 = a["conv_w_pw2"][0].rearrange("(k p) n -> p k n", p=128)
            for c in range(2):
                sp.wait_ge(sem("pw1_mm"), at("pw1_mm", 2 * (c + 1)))
                dst = RG(c * SLOT, 4096).rearrange("p (k n) -> p k n", k=KD)
                sp.dma_start(dst, w2[:, :, 512 * c:512 * c + 512]).then_inc(sem(f"w_pw2_{c}"), 16)
            sp.wait_ge(sem("last_rows"), at("last_rows", 4))
            sp.dma_start(o["conv_prompt"][0, 0], last_p[2:32, :]).then_inc(out_sem, 16)
            for s in range(NSEQ):
                sp.dma_start(cs[s, PASTC - DSEQ:, :], last_s[4 * s:4 * s + 4, :]).then_inc(out_sem, 16)
            n_out[0] = 16 * (1 + 1 + NSEQ)

            for l in LAYERS:
                if l == 1:
                    sp.wait_ge(sem("t_o"), at("t_o", KD))
                    sp.wait_ge(sem("pv_all"), at("pv_all", 2))
                    sp.dma_start(gfin, a["g_final_rows"]).then_inc(sem("gfinal_in"), 16)
                for u in (2, 3, 0, 1):
                    if l == 0:
                        if u == 2:
                            sp.wait_ge(sem("pw1_mm"), at("pw1_mm", KD))
                            sp.wait_ge(sem("prod_used"), at("prod_used", KD))
                        elif u == 3:
                            sp.wait_ge(sem("bpw2_used"), at("bpw2_used", 1))
                        elif u == 0:
                            sp.wait_ge(sem("pw2_mm"), at("pw2_mm", N_ROWS))
                        else:
                            sp.wait_ge(out_sem, n_out[0])
                    elif u == 0:
                        sp.wait_ge(sem("wo_mm"), at("wo_mm", N_ROWS))
                    for dst, src in wload(l, u, u):
                        sp.dma_start(dst, src).then_inc(sem(f"w_moe_{u}@{l}"), 16)
                sp.wait_ge(sem(f"xh_ffn{l}"), at(f"xh_ffn{l}", NT))
                sp.dma_start(scratch[f"rows{l}"][0:SEQ].rearrange("(i p) d -> p i d", p=128), xhat[:, 0:4, :]).then_inc(sem(f"rows_out@{l}"), 16)
                sp.dma_start(scratch[f"rows{l}"][SEQ:NTOK], xhat[0:NDEC, 4, :]).then_inc(sem(f"rows_out@{l}"), 16)
                with sp.Fori(0, 3) as j:
                    for u in range(4):
                        sp.wait_ge(sem(f"down@{l}"), at(f"down@{l}", 4 * j + (u + 1)))
                        for dst, src in wload(l, 4 * j + (4 + u), u):
                            sp.dma_start(dst, src).then_inc(sem(f"w_moe_{u}@{l}"), 16)
                if l == 0:
                    attention_first_loads(sp)
                sp.wait_ge(sem(f"extra_tab@{l}"), at(f"extra_tab@{l}", 1))
                n_extra = sp.value_load(extra_tab[0:1, EXTRA:EXTRA + 1], min_val=0, max_val=EXTRA)
                for x in range(EXTRA):
                    with sp.If(n_extra > x):
                        if x < 2:
                            sp.wait_ge(sem(f"down@{l}"), at(f"down@{l}", NE - 3 + EXTRA_SLOTS[l] + x))
                        else:
                            if 4 * (x - 1) > 0:
                                sp.wait_ge(sem(f"x{l}_pe"), at(f"x{l}_pe", 4 * (x - 1)))
                        e = sp.value_load(extra_tab[0:1, x:x + 1], min_val=0, max_val=NE - 1)
                        for dst, src in wload(l, e, EXTRA_SLOTS[l] + x % 2):
                            sp.dma_start(dst, src).then_inc(sem(f"x{l}_w{x % 2}"), 16)
                if l == 0:
                    attention_loads(sp)
            for i in range(4):
                sp.wait_ge(sem("y_done"), at("y_done", i + 1))
                sp.dma_start(o["y_prompt"][0, 128 * i:128 * i + 128], resid[:, i, :]).then_inc(out_sem, 16)
            sp.wait_ge(sem("y_done"), at("y_done", NT))
            sp.dma_start(o["y_sample"].rearrange("s t d -> (s t) d"), resid[0:NDEC, 4, :]).then_inc(out_sem, 16)
            n_out[0] += 16 * NT
            sp.wait_ge(out_sem, n_out[0])

        @block.gpsimd
        def _(pool):
            pool.memset(gp[:, :, 0:PASTC], 0.0).then_inc(sem("pad"), 1)
            pool.memset(last_p, 0.0).then_inc(sem("extra_zero"), 1)
            pool.memset(stat["ss"], 1.0).then_inc(sem("pad"), 1)
            wdw = P("w_dw").rearrange("p (m x) -> p m x", m=8)
            pool.wait_ge(sem("par_in"), at("par_in", 16))

            def pool_conv(n, taps):
                out = cv[:, POOL_TILES[n], 0:SEQ]
                for x in taps:
                    pool.wait_ge(sem("tapped"), at("tapped", CONVW * n + x + 1))
                    if (CONVW - 1) * n + x - 1 > 0:
                        pool.wait_ge(sem("taps"), at("taps", (CONVW - 1) * n + x - 1))
                    pool.tensor_tensor(out, out, junk[:, SEQ * (x % 2):SEQ * (x % 2) + SEQ], ALU.add).then_inc(sem("taps"), 1)

            def products(m):
                pool.wait_ge(sem("past0"), at("past0", m + 1))
                pool.wait_ge(sem("past1"), at("past1", m + 1))
                pool.wait_ge(sem("windows"), at("windows", m + 1))
                if m - 1 > 0:
                    pool.wait_ge(sem("prod_used"), at("prod_used", m - 1))
                w = gw[:, m, :, 0:CONVW]
                win = bass.AP(tensor=w.tensor, offset=w.offset, ap=[w.ap[0], w.ap[1], [1, DSEQ], [1, CONVW]])
                pool.tensor_tensor(prod[:, m % 2, :, :].rearrange("p (s t) x -> p s t x", s=NSEQ), win,
                                   wdw[:, m, :].unsqueeze(1).unsqueeze(1).broadcast_to([128, NSEQ, DSEQ, CONVW]), ALU.mult).then_inc(sem("prod"), 1)
            products(0)
            products(1)
            pool_conv(0, range(1, CONVW))
            products(2)
            products(3)
            pool_conv(1, range(1, 20))
            products(4)
            products(5)
            pool_conv(1, range(20, CONVW))
            products(6)
            products(7)
            pool.wait_ge(sem("xh_mix0"), at("xh_mix0", NT))
            pool.wait_ge(sem("bpw2_in"), at("bpw2_in", 16))
            for i in range(NT):
                n = ROWS[i]
                ins = pool.tensor_tensor(resid[0:n, i, :], resid[0:n, i, :], bpw2[0:n, :], ALU.add)
                ins.then_inc(sem("bias_added"), 1)
            pool.wait_ge(sem("bias_added"), at("bias_added", NT))
            pool.sem_inc(sem("bpw2_used"), 1)

            for l in LAYERS:
                if l == 1:
                    attention_pool(pool)
                pool.wait_ge(sem("ids_in"), at("ids_in", 16))
                pool.wait_ge(sem("owner_zero"), at("owner_zero", 32))
                for c in range(2):
                    pool.wait_ge(sem(f"slots@{l}"), at(f"slots@{l}", c + 1))
                    for i in range(NT):
                        n = ROWS[i]
                        pool.indirect_dma_start(scratch[f"owner{l}"], bass.IndirectOffsetOnAxis(ap=slot_i[0:n, c, i:i + 1], axis=0),
                                                ids[0:n, i:i + 1], None).then_inc(sem(f"owner_out@{l}"), 16)
                pool.wait_ge(sem(f"owner_out@{l}"), at(f"owner_out@{l}", 16 * 2 * NT))
                pool.dma_start(tokrow[:, :], scratch[f"owner{l}"][0:128 * NE].rearrange("(p n) x -> p (n x)", p=128)).then_inc(sem(f"tokrow@{l}"), 16)
                pool.wait_ge(sem(f"tokrow@{l}"), at(f"tokrow@{l}", 16))
                pool.wait_ge(sem(f"rows_out@{l}"), at(f"rows_out@{l}", 32))
                for e in range(NE):
                    if e - 1 > 0:
                        pool.wait_ge(sem(f"turned@{l}"), at(f"turned@{l}", e - 1))
                    pool.indirect_dma_start(xg[:, e % 2, :], None, scratch[f"rows{l}"], bass.IndirectOffsetOnAxis(ap=tokrow[:, e:e + 1], axis=0)).then_inc(sem(f"xg_{e % 2}@{l}"), 16)
                pool.dma_start(extra_tok[:, :], scratch[f"owner{l}"][MAIN:SLOTS].rearrange("(p x) a -> p (x a)", p=128)).then_inc(sem(f"extra_tok@{l}"), 16)
                pool.wait_ge(sem(f"extra_tok@{l}"), at(f"extra_tok@{l}", 16))
                pool.wait_ge(sem(f"extra_tab@{l}"), at(f"extra_tab@{l}", 1))
                pool.wait_ge(sem(f"turned@{l}"), at(f"turned@{l}", NE))
                n_extra = pool.value_load(extra_tab[0:1, EXTRA:EXTRA + 1], min_val=0, max_val=EXTRA)
                for x in range(EXTRA):
                    with pool.If(n_extra > x):
                        if 4 * x - 3 > 0:
                            pool.wait_ge(sem(f"x{l}_pe"), at(f"x{l}_pe", 4 * x - 3))
                        pool.indirect_dma_start(xg[:, 0, :], None, scratch[f"rows{l}"], bass.IndirectOffsetOnAxis(ap=extra_tok[:, x:x + 1], axis=0)).then_inc(sem(f"x{l}_rows"), 16)
                for b in range(2):
                    pool.wait_ge(sem(f"y_out_{b}@{l}"), at(f"y_out_{b}@{l}", 16 * NE // 2))
                for x in range(EXTRA):
                    with pool.If(n_extra > x):
                        pool.wait_ge(sem(f"x{l}_y"), at(f"x{l}_y", 16 * (x + 1)))
                        pool.nop()
                for i in range(NT):
                    n = ROWS[i]
                    if i - 2 > 0:
                        pool.wait_ge(sem(f"collected@{l}"), at(f"collected@{l}", i - 2))
                    for c in range(2):
                        pool.indirect_dma_start(ygat[0:n, i % 3, c, :], None, scratch["y"], bass.IndirectOffsetOnAxis(ap=slot_i[0:n, c, i:i + 1], axis=0)).then_inc(sem(f"ygat_{i % 3}@{l}"), 16)

        @block.tensor
        def _(pe):
            pe.wait_ge(sem("con_in"), at("con_in", 16))
            turn_pe(pe, "mix0", xhat, NT)
            def state_turned(k):
                for b in range(2):
                    if k > 0:
                        pe.wait_ge(sem(f"past{b}"), at(f"past{b}", k))
                    pe.transpose(ps[6 + b][:, 0:120], state[0:120, b, 128 * k:128 * k + 128], ident[0:120, 0:120]).then_inc(sem("state_t"), 1)
            wait_turned(pe, "mix0")
            for m in range(KD):
                c = m // 2
                if m % 2 == 0:
                    pe.wait_ge(sem(f"w_pw1_{c}"), at(f"w_pw1_{c}", 32))
                if m - 1 > 0:
                    pe.wait_ge(sem("glu"), at("glu", m - 1))
                if m == 1:
                    pe.wait_ge(sem("past0"), at("past0", KD))
                    pe.wait_ge(sem("past1"), at("past1", KD))
                w = RG(c * SLOT, 4096).rearrange("p (k b n) -> p k b n", k=KD, b=2)
                for b in range(2):
                    for k in range(KD):
                        mm = all_tokens(pe, 4 * (m % 2) + 2 * b, w[:, k, b, 128 * (m % 2):128 * (m % 2) + 128], xT, k)
                        if m == 0 and b == 0:
                            pe.wait_ge(sem("state_in"), at("state_in", 16))
                            state_turned(k)
                mm.then_inc(sem("pw1_mm"), 1)
            pe.wait_ge(sem("glu"), at("glu", KD))
            for half in range(2):
                for m in range(4 * half, 4 * half + 4):
                    c0 = 128 * (m % 4)
                    pe.transpose(ps[half][0:32, c0:c0 + 128], gp[:, m, 510:542], ident)
                    mm = pe.transpose(ps[2 + half][0:32, c0:c0 + 128], gp[:, m, PASTC + SEQ:], ident)
                mm.then_inc(sem("last_t"), 1)
            for m in range(KD):
                if m in DVE_TILES:
                    pe.wait_ge(sem("conv"), at("conv", DVE_TILES.index(m) + 1))
                if m in POOL_TILES:
                    pe.wait_ge(sem("taps"), at("taps", (CONVW - 1) * (POOL_TILES.index(m) + 1)))
                pe.wait_ge(sem("conv_s"), at("conv_s", m + 1))
                mm = all_tokens(pe, 6, C("mean"), cv, m)
            mm.then_inc(sem("mean"), 1)
            pe.wait_ge(sem("last_rows"), at("last_rows", 4))
            for m in range(KD):
                pe.wait_ge(sem("sq"), at("sq", m + 1))
                mm = all_tokens(pe, 0, C("mean"), sq, m)
            mm.then_inc(sem("var"), 1)
            for c in range(2):
                pe.wait_ge(sem(f"w_pw2_{c}"), at(f"w_pw2_{c}", 16))
            pw2_rows(pe)
            for l in LAYERS:
                moe_pe(pe, l)
                if l == 0:
                    attention_pe(pe)

        @block.scalar
        def _(act):
            act.wait_ge(sem("pad"), at("pad", 2))
            for i in range(NT):
                if i in (0, 2, 4):
                    act.wait_ge(sem(f"x_in{i // 2}"), at(f"x_in{i // 2}", 16))
                row_squares(act, "mix0", i)
            row_roots(act, "mix0", NT - 1)
            act.wait_ge(sem("par_in"), at("par_in", 16))
            turned_act(act, "mix0", [(xT, P("g_mix0"))])
            for k in range(KD):
                act.wait_ge(sem("state_t"), at("state_t", 2 * k + 2))
                act.copy(gw[:, k, 4:8, 0:PASTC], ps[7][:, 0:120].rearrange("p (s t) -> p s t", s=4)).then_inc(sem("past1"), 1)
            bp = P("b_pw1")
            wdw = P("w_dw").rearrange("p (m x) -> p m x", m=8)

            def sigmoid(m):
                act.wait_ge(sem("pw1_mm"), at("pw1_mm", m + 1))
                if m - 1 > 0:
                    act.wait_ge(sem("glu"), at("glu", m - 1))
                act.activation(halves(sig[:, m % 2, :]), two_banks(4 * (m % 2) + 2), ACT.Sigmoid, bias=bp[:, 8 + m:9 + m]).then_inc(sem("sig"), 1)

            def tapped(n, taps):
                m = POOL_TILES[n]
                act.wait_ge(sem("glu"), at("glu", m + 1))
                act.wait_ge(sem("t_mix0"), at("t_mix0", KD + 1))
                act.wait_ge(sem("pad"), at("pad", 1))
                for x in taps:
                    src = gp[:, m, x:x + SEQ]
                    if x == 0:
                        i = act.activation(cv[:, m, 0:SEQ], src, ACT.Identity, bias=P("b_dw")[:, m:m + 1], scale=wdw[:, m, 0:1])
                    else:
                        if (CONVW - 1) * n + max(x - 2, 0) > 0:
                            act.wait_ge(sem("taps"), at("taps", (CONVW - 1) * n + max(x - 2, 0)))
                        i = act.activation(junk[:, SEQ * (x % 2):SEQ * (x % 2) + SEQ], src, ACT.Copy, scale=wdw[:, m, x:x + 1])
                    i.then_inc(sem("tapped"), 1)
            for m in range(3):
                sigmoid(m)
            for n in range(2):
                tapped(n, range(0, 10))
                sigmoid(3 * n + 3)
                tapped(n, range(10, 21))
                sigmoid(3 * n + 4)
                tapped(n, range(21, CONVW))
                if n == 0:
                    sigmoid(5)
            for half in range(2):
                act.wait_ge(sem("last_t"), at("last_t", half + 1))
                act.wait_ge(sem("y_zero"), at("y_zero", 16 * EXTRA))
                act.copy(last_p[0:32, 512 * half:512 * half + 512], ps[half][0:32, :]).then_inc(sem("last_rows"), 1)
                act.copy(last_s[0:32, 512 * half:512 * half + 512], ps[2 + half][0:32, :]).then_inc(sem("last_rows"), 1)
            for m in range(KD):
                act.wait_ge(sem("centred"), at("centred", m + 1))
                act.activation(sq[:, m, :], cv[:, m, :], ACT.Square).then_inc(sem("sq"), 1)
            act.wait_ge(sem("var_eps"), at("var_eps", 1))
            act.activation(lnr, lnr, ACT.Sqrt).then_inc(sem("ln_sd"), 1)
            for m in range(KD):
                act.wait_ge(sem("scaled"), at("scaled", m + 1))
                act.activation(xT[:, m, :], cv[:, m, :], ACT.Silu, bias=P("ln_b")[:, m:m + 1], scale=P("ln_g")[:, m:m + 1]).then_inc(sem("conv_h"), 1)
            for i in range(NT):
                act.wait_ge(sem("pw2_add"), at("pw2_add", min(2 * (i + 1), N_ROWS)))
                row_squares(act, "ffn0", i)
            row_roots(act, "ffn0", NT - 1)
            for l in LAYERS:
                moe_act(act, l)
                if l == 0:
                    attention_act(act)
                    for i in range(2, NT):
                        act.wait_ge(sem("wo_add"), at("wo_add", min(2 * (i + 1), N_ROWS)))
                        row_squares(act, "ffn1", i)
                    row_roots(act, "ffn1", NT - 1)
            for i in range(NT):
                act.wait_ge(sem("collected@1"), at("collected@1", i + 1))
                row_squares(act, "final", i)
            row_roots(act, "final", NT - 1)

        @block.vector
        def _(v):
            for i in range(NT + 2):
                norm_step(v, "mix0", i)
            v.wait_ge(sem("par_in"), at("par_in", 16))
            turned_dve(v, "mix0", [(xT, P("g_mix0"))])
            for k in range(KD):
                v.wait_ge(sem("state_t"), at("state_t", 2 * k + 1))
                v.tensor_copy(gw[:, k, 0:4, 0:PASTC], ps[6][:, 0:120].rearrange("p (s t) -> p s t", s=4)).then_inc(sem("past0"), 1)
            bp = P("b_pw1")
            wdw = P("w_dw").rearrange("p (m x) -> p m x", m=8)
            v.wait_ge(sem("pad"), at("pad", 1))
            v.wait_ge(sem("con_in"), at("con_in", 16))

            def glu(m):
                v.wait_ge(sem("sig"), at("sig", m + 1))
                link(v, v.scalar_tensor_tensor(halves(gp[:, m, PASTC:]), two_banks(4 * (m % 2)), bp[:, m:m + 1], halves(sig[:, m % 2, :]), ALU.add, ALU.mult))
                v.tensor_copy(gw[:, m, :, PASTC:], gp[:, m, PASTC + SEQ:].rearrange("p (s t) -> p s t", s=NSEQ)).then_inc(sem("windows"), 1)
                v.sem_inc(sem("glu"), 1)

            def conv(tiles, between):
                last = {}
                for x in range(CONVW):
                    for m in tiles:
                        out = cv[:, m, 0:SEQ]
                        if x == 0:
                            i = v.tensor_scalar(out, gp[:, m, 0:SEQ], wdw[:, m, 0:1], P("b_dw")[:, m:m + 1], ALU.mult, ALU.add)
                        else:
                            v.wait_ge(sem("dve_chain"), at("dve_chain", last[m]))
                            i = v.scalar_tensor_tensor(out, gp[:, m, x:x + SEQ], wdw[:, m, x:x + 1], out, ALU.mult, ALU.add)
                        i.then_inc(sem("dve_chain"), 1)
                        chain[0] += 1
                        last[m] = chain[0]
                    for step, m in between.get(x, ()):
                        step(m)
                v.wait_ge(sem("dve_chain"), at("dve_chain", chain[0]))
                for _ in tiles:
                    v.sem_inc(sem("conv"), 1)

            def conv_sampled(m):
                v.wait_ge(sem("prod"), at("prod", m + 1))
                link(v, v.tensor_reduce(cv[:, m, SEQ:NTOK], prod[:, m % 2, :, :], AX.X, ALU.add))
                v.sem_inc(sem("prod_used"), 1)
                v.tensor_scalar(cv[:, m, SEQ:NTOK], cv[:, m, SEQ:NTOK], P("b_dw")[:, m:m + 1], None, ALU.add).then_inc(sem("conv_s"), 1)

            v.tensor_copy(count[:, 0, :], C("before"))
            v.tensor_copy(count[:, 1, :], C("ones"))
            v.wait_ge(sem("t_mix0"), at("t_mix0", KD + 1))
            glu(0)
            glu(1)
            conv((0, 1), {12: [(glu, 2)], 25: [(glu, 3)]})
            conv_sampled(0)
            conv_sampled(1)
            glu(4)
            conv((3, 4), {13: [(glu, 5)], 25: [(glu, 6)]})
            conv_sampled(2)
            conv_sampled(3)
            glu(7)
            conv((6, 7), {14: [(conv_sampled, 4), (conv_sampled, 5)]})
            conv_sampled(6)
            conv_sampled(7)
            v.wait_ge(sem("mean"), at("mean", 1))
            v.wait_ge(sem("conv_s"), at("conv_s", KD))
            v.wait_ge(sem("taps"), at("taps", (CONVW - 1) * len(POOL_TILES)))
            for m in range(KD):
                v.tensor_tensor(halves(cv[:, m, :]), halves(cv[:, m, :]), two_banks(6), ALU.subtract).then_inc(sem("centred"), 1)
            v.wait_ge(sem("var"), at("var", 1))
            v.tensor_scalar(halves(lnr), two_banks(0), EPS, None, ALU.add).then_inc(sem("var_eps"), 1)
            v.wait_ge(sem("ln_sd"), at("ln_sd", 1))
            link(v, v.reciprocal(lnr, lnr))
            v.wait_ge(sem("centred"), at("centred", KD))
            for m in range(KD):
                v.tensor_tensor(cv[:, m, :], cv[:, m, :], lnr, ALU.mult).then_inc(sem("scaled"), 1)
            v.wait_ge(sem("bias_added"), at("bias_added", NT))
            v.wait_ge(sem("conv_h"), at("conv_h", KD))
            for n in range(8):
                row_added(v, "pw2", "ffn0", PW2_BANKS, n)
            sampled_added(v, "pw2", "ffn0", PW2_BANKS)
            for l in LAYERS:
                moe_dve(v, l)
                if l == 0:
                    attention_dve(v)


_INS = ["x_prompt", "x_sample", "cache_k", "cache_v", "state_conv", "conv_w_pw1", "conv_w_pw2", "w_kv", "attn_w_q", "attn_w_o",
        "moe_w_gate", "moe_w_up", "moe_w_down"]
_OUTS = [("y_prompt", (1, SEQ, D)), ("y_sample", (NSEQ, DSEQ, D)), ("conv_prompt", (1, 1, PASTC, D)), ("conv_sample", (1, NSEQ, PASTC, D)),
         ("k_prompt", (1, SEQ, NH, 2, HD)), ("v_prompt", (1, SEQ, NH, 2 * HD)), ("k_sample", (NSEQ, DSEQ, NH, 2, HD)),
         ("v_sample", (NSEQ, DSEQ, NH, 2 * HD))]


def laid_out(inp):
    def feat(x):
        x = np.asarray(x)
        return x.reshape(-1, 128).T

    def rows(x):
        return np.tile(np.asarray(x).reshape(1, -1), (128, 1))
    t = {}
    for l in range(2):
        t[f"g_mix{l}"] = feat(inp["norm_mix"][l])
        t[f"g_ffn{l}"] = feat(inp["norm_ffn"][l])
        wr = np.concatenate([np.asarray(inp["moe_w_grp"][l]), np.asarray(inp["moe_w_exp_router"][l]).reshape(D, NE)], axis=1)
        t[f"wr{l}"] = wr.reshape(KD, 128, 20).transpose(1, 0, 2).reshape(128, -1)
        t[f"br{l}"] = rows(np.concatenate([np.asarray(inp["moe_b_grp"][l]), np.asarray(inp["moe_b_exp_router"][l]).reshape(-1)]))
    t["g_kv"] = feat(inp["norm_kv"])
    t["b_pw1"] = feat(inp["conv_b_pw1"][0])
    t["b_dw"] = feat(inp["conv_b_dw"][0])
    t["ln_g"] = feat(inp["conv_ln_g"][0])
    t["ln_b"] = feat(inp["conv_ln_b"][0])
    t["subln"] = feat(inp["attn_subln_g"][0])
    t["w_dw"] = np.asarray(inp["conv_w_dw"][0]).reshape(CONVW, KD, 128).transpose(2, 1, 0).reshape(128, -1)
    t["lams"] = rows(np.concatenate([np.asarray(inp[f"attn_lambda_{n}"][0]) for n in ("q1", "k1", "q2", "k2")]))
    pt = np.asarray(inp["page_table"])
    order = np.concatenate([pt.reshape(4, 2, 8).transpose(0, 2, 1).reshape(-1), pt.reshape(2, 4, 8).transpose(0, 2, 1).reshape(-1)])
    return {"params": np.concatenate([t[n] for n in PCOL], axis=1), "page_order": order.reshape(1, -1),
            "b_pw2_rows": rows(inp["conv_b_pw2"][0]), "g_final_rows": rows(inp["norm_final"])}


def kernel(**inputs):
    import concourse.bacc as bacc
    from concourse.bass_utils import run_bass_kernel_spmd

    nc = bacc.Bacc("TRN2", target_bir_lowering=False, num_devices=1)
    arrays = {n: np.ascontiguousarray(inputs[n]) for n in _INS}
    arrays.update({n: np.ascontiguousarray(x) for n, x in {**laid_out(inputs), **constants()}.items()})
    a = {n: nc.dram_tensor(f"in_{n}", x.shape, mybir.dt.from_np(x.dtype), kind="ExternalInput").ap() for n, x in arrays.items()}
    o = {n: nc.dram_tensor(f"out_{n}", s, F32, kind="ExternalOutput").ap() for n, s in _OUTS}
    scratch = {"y": nc.dram_tensor("y_rows", (SLOTS, D), F32, kind="Internal").ap()}
    for l in range(2):
        scratch[f"owner{l}"] = nc.dram_tensor(f"owner{l}", (SLOTS, 1), I32, kind="Internal").ap()
        scratch[f"rows{l}"] = nc.dram_tensor(f"rows{l}", (NTOK, D), F32, kind="Internal").ap()
    program(nc, a, o, scratch)
    nc.compile()
    r = run_bass_kernel_spmd(nc, [{f"in_{n}": x for n, x in arrays.items()}], core_ids=[0])
    return tuple(r.results[0][f"out_{n}"] for n, _ in _OUTS)
```
